# Optimizing a Trainium2 kernel written in Bass

```python
import math
import jax
import jax.numpy as jnp
from jax import lax
import numpy as np
import jax, jax.numpy as jnp

D_MODEL = 1024
BATCH = 1
SEQ = 512
DEPTH = 1

MEM_LEN = 256
MIX_W = 512
N_BRANCH = 3
CONV_K = 3
SB_HEADS = 8
SB_HEAD_DIM = MIX_W // SB_HEADS
SB_BLOCK = 128
RWKV_HEADS = 8
RWKV_HEAD = MIX_W // RWKV_HEADS
DECAY_LORA = 64
ICLR_LORA = 64
GATE_LORA = 128
VRES_LORA = 32
DECAY_SCALE = math.exp(-0.5)
CA_HEADS = 4
CA_HEAD_DIM = D_MODEL // CA_HEADS
FFN_DIM = 2816
FFN_CONV_K = 3
RMS_EPS = 1e-6
GN_EPS = 64e-5

CONV_COLS = 3 * MIX_W
SB_COLS = 3 * MIX_W
GATE_COLS = N_BRANCH * D_MODEL
RWKV_COLS = 3 * MIX_W + DECAY_LORA + ICLR_LORA + GATE_LORA
COMB_COLS = CONV_COLS + SB_COLS + GATE_COLS + RWKV_COLS
OFF_SB = CONV_COLS
OFF_GATE = OFF_SB + SB_COLS
OFF_RWKV = OFF_GATE + GATE_COLS


def rms_norm(x, g):
    xf = x.astype(jnp.float32)
    y = xf * lax.rsqrt(jnp.mean(xf * xf, axis=-1, keepdims=True) + RMS_EPS)
    return (y * g.astype(jnp.float32)).astype(x.dtype)

def causal_dwconv(x, w):
    c = x.shape[-1]
    return lax.conv_general_dilated(
        x, w[:, None, :].astype(x.dtype), window_strides=(1,),
        padding=[(w.shape[0] - 1, 0)], dimension_numbers=("NWC", "WIO", "NWC"),
        feature_group_count=c)

def stick_breaking_attention(q, k, v):
    s_len, dh = q.shape[2], q.shape[3]
    scale = dh ** -0.5
    outs = []
    for i in range(s_len // SB_BLOCK):
        start, end = i * SB_BLOCK, (i + 1) * SB_BLOCK
        q_blk = q[:, :, start:end]
        k_blk, v_blk = k[:, :, :end], v[:, :, :end]
        z = jnp.einsum("bhqd,bhkd->bhqk", q_blk, k_blk).astype(jnp.float32) * scale
        q_pos = start + jnp.arange(SB_BLOCK)
        k_pos = jnp.arange(end)
        mask = k_pos[None, :] < q_pos[:, None]
        log_not = jnp.where(mask, jax.nn.log_sigmoid(-z), 0.0)
        suffix = lax.cumsum(log_not, axis=3, reverse=True) - log_not
        log_w = jax.nn.log_sigmoid(z) + suffix
        att = jnp.where(mask, jnp.exp(log_w), 0.0)
        outs.append(jnp.einsum("bhqk,bhkd->bhqd", att.astype(v.dtype), v_blk))
    return jnp.concatenate(outs, axis=2)

def rwkv7_time_mix(p, mu, w0, w_lora, a0, a_lora, g_lora, k_k, k_a, r_k, lnx_w, lnx_b,
                   v_first, v0, v_lora):
    b, s, _ = p.shape
    f32 = jnp.float32
    p = p.astype(f32)
    prev = jnp.pad(p, ((0, 0), (1, 0), (0, 0)))[:, :-1]
    p = p + mu.astype(f32) * (prev - p)
    w_ = MIX_W
    r, k, v = p[..., :w_], p[..., w_:2 * w_], p[..., 2 * w_:3 * w_]
    o = 3 * w_
    xw = p[..., o:o + DECAY_LORA]; o += DECAY_LORA
    xa = p[..., o:o + ICLR_LORA]; o += ICLR_LORA
    xg = p[..., o:o + GATE_LORA]; o += GATE_LORA
    log_decay = -DECAY_SCALE * jax.nn.sigmoid(w0 + jnp.tanh(xw) @ w_lora)
    a = jax.nn.sigmoid(a0 + xa @ a_lora)
    if v0 is None:
        v_first = v
    else:
        xv = p[..., o:o + VRES_LORA]
        v = v + (v_first - v) * jax.nn.sigmoid(v0 + xv @ v_lora)
    g = jax.nn.sigmoid(xg) @ g_lora

    def heads(t):
        return t.reshape(b, s, RWKV_HEADS, RWKV_HEAD)

    kk = heads(k * k_k)
    kk = kk / jnp.maximum(jnp.linalg.norm(kk, axis=-1, keepdims=True), 1e-12)
    k = k * (1.0 + (a - 1.0) * k_a)
    rh, kh, vh, ah, wh = heads(r), heads(k), heads(v), heads(a), heads(jnp.exp(log_decay))

    def step(state, inp):
        r_t, w_t, k_t, v_t, kk_t, a_t = inp
        sa = jnp.einsum("bhvk,bhk->bhv", state, kk_t)
        state = (state * w_t[:, :, None, :]
                 - sa[..., None] * (kk_t * a_t)[:, :, None, :]
                 + v_t[..., None] * k_t[:, :, None, :])
        return state, jnp.einsum("bhvk,bhk->bhv", state, r_t)

    xs = tuple(jnp.moveaxis(t, 1, 0) for t in (rh, wh, kh, vh, kk, ah))
    state0 = jnp.zeros((b, RWKV_HEADS, RWKV_HEAD, RWKV_HEAD), f32)
    _, out = lax.scan(step, state0, xs)
    out = jnp.moveaxis(out, 0, 1)
    mean = jnp.mean(out, axis=-1, keepdims=True)
    var = jnp.mean(jnp.square(out - mean), axis=-1, keepdims=True)
    out = ((out - mean) * lax.rsqrt(var + GN_EPS)).reshape(b, s, w_) * lnx_w + lnx_b
    bonus = (jnp.sum(rh * kh * r_k, axis=-1, keepdims=True) * vh).reshape(b, s, w_)
    return (out + bonus) * g, v_first

def hybrid_token_mixer(xn, w_comb, conv_w, mu_rwkv, w0, w_lora, a0, a_lora, g_lora, k_k, k_a,
                       r_k, lnx_w, lnx_b, branch_proj, gate_b, w_mix_out, v_first, vres):
    b, s, _ = xn.shape
    mu = mu_rwkv
    v0 = v_lora = None
    if vres is not None:
        w_vres, mu_vres, v0, v_lora = vres
        w_comb = jnp.concatenate([w_comb, w_vres], axis=1)
        mu = jnp.concatenate([mu_rwkv, mu_vres], axis=0)
    proj = xn @ w_comb

    c_b, c_c, c_x = jnp.split(proj[..., :OFF_SB], 3, axis=-1)
    y_conv = c_b * causal_dwconv(c_c * c_x, conv_w)

    q, k, v = jnp.split(proj[..., OFF_SB:OFF_GATE], 3, axis=-1)

    def to_heads(t):
        return t.reshape(b, s, SB_HEADS, SB_HEAD_DIM).transpose(0, 2, 1, 3)

    y_sb = stick_breaking_attention(to_heads(q), to_heads(k), to_heads(v))
    y_sb = y_sb.transpose(0, 2, 1, 3).reshape(b, s, MIX_W)

    y_rwkv, v_first = rwkv7_time_mix(proj[..., OFF_RWKV:], mu, w0, w_lora, a0, a_lora, g_lora,
                                     k_k, k_a, r_k, lnx_w, lnx_b, v_first, v0, v_lora)

    gates = jax.nn.sigmoid(
        proj[..., OFF_GATE:OFF_RWKV].reshape(b, s, N_BRANCH, D_MODEL).astype(jnp.float32)
        + gate_b).astype(xn.dtype)
    ys = jnp.stack([y_conv.astype(xn.dtype), y_sb.astype(xn.dtype), y_rwkv.astype(xn.dtype)],
                   axis=2)
    branches = jnp.einsum("bsnc,ncd->bsnd", ys, branch_proj)
    merged = jnp.einsum("bsnd,bsnd->bsd", gates, branches)
    return merged @ w_mix_out, v_first

def memory_cross_attention(hn, mem_n, wq, wkv, wo):
    b, s, _ = hn.shape
    m = mem_n.shape[1]
    q = (hn @ wq).reshape(b, s, CA_HEADS, CA_HEAD_DIM)
    k, v = jnp.split(mem_n @ wkv, 2, axis=-1)
    k = k.reshape(b, m, CA_HEADS, CA_HEAD_DIM)
    v = v.reshape(b, m, CA_HEADS, CA_HEAD_DIM)
    scores = jnp.einsum("bshd,bmhd->bhsm", q, k).astype(jnp.float32) * (CA_HEAD_DIM ** -0.5)
    probs = jax.nn.softmax(scores, axis=-1).astype(v.dtype)
    out = jnp.einsum("bhsm,bmhd->bshd", probs, v).reshape(b, s, D_MODEL)
    return out @ wo

def conv_ffn(hn, w_up, conv_w, conv_b, w_down):
    u = causal_dwconv(hn @ w_up, conv_w) + conv_b
    gate, val = jnp.split(u, 2, axis=-1)
    return (jax.nn.silu(gate) * val) @ w_down

def first_inputs(seed: int = 0) -> dict:
    key = jax.random.key(seed)
    ks = iter(jax.random.split(key, 48))

    def nrm(shape, scale):
        return jax.random.normal(next(ks), shape, jnp.float32) * scale

    def gain(shape):
        return 1.0 + nrm(shape, 0.02)

    L, Lv, D, W, F = DEPTH, DEPTH - 1, D_MODEL, MIX_W, FFN_DIM
    return {
        "x": nrm((BATCH, SEQ, D), 1.0),
        "mem": nrm((BATCH, MEM_LEN, D), 1.0),
        "norm_mix": gain((L, D)),
        "w_comb": nrm((L, D, COMB_COLS), D ** -0.5),
        "conv_w": nrm((L, CONV_K, W), 0.5),
        "mu_rwkv": jax.random.uniform(next(ks), (L, RWKV_COLS), jnp.float32),
        "w0": 0.5 + nrm((L, W), 0.5),
        "w_lora": nrm((L, DECAY_LORA, W), 0.1),
        "a0": nrm((L, W), 0.3),
        "a_lora": nrm((L, ICLR_LORA, W), 0.1),
        "g_lora": nrm((L, GATE_LORA, W), GATE_LORA ** -0.5),
        "k_k": 1.0 + nrm((L, W), 0.1),
        "k_a": 1.0 + nrm((L, W), 0.1),
        "r_k": nrm((L, RWKV_HEADS, RWKV_HEAD), 0.1),
        "lnx_w": gain((L, W)),
        "lnx_b": nrm((L, W), 0.02),
        "w_vres": nrm((Lv, D, VRES_LORA), D ** -0.5),
        "mu_vres": jax.random.uniform(next(ks), (Lv, VRES_LORA), jnp.float32),
        "v0": nrm((Lv, W), 0.3),
        "v_lora": nrm((Lv, VRES_LORA, W), 0.1),
        "branch_proj": nrm((L, N_BRANCH, W, D), W ** -0.5),
        "gate_b": nrm((L, N_BRANCH, D), 0.01),
        "w_mix_out": nrm((L, D, D), D ** -0.5),
        "norm_ca": gain((L, D)),
        "norm_mem": gain((L, D)),
        "ca_wq": nrm((L, D, D), D ** -0.5),
        "ca_wkv": nrm((L, D, 2 * D), D ** -0.5),
        "ca_wo": nrm((L, D, D), D ** -0.5),
        "norm_ffn": gain((L, D)),
        "ffn_up": nrm((L, D, 2 * F), D ** -0.5),
        "ffn_conv_w": nrm((L, FFN_CONV_K, 2 * F), 0.5),
        "ffn_conv_b": nrm((L, 2 * F), 0.02),
        "ffn_down": nrm((L, F, D), F ** -0.5),
        "norm_final": gain((D,)),
    }

def first_block(x, mem, norm_mix, w_comb, conv_w, mu_rwkv, w0, w_lora, a0, a_lora, g_lora, k_k,
              k_a, r_k, lnx_w, lnx_b, w_vres, mu_vres, v0, v_lora, branch_proj, gate_b,
              w_mix_out, norm_ca, norm_mem, ca_wq, ca_wkv, ca_wo, norm_ffn, ffn_up, ffn_conv_w,
              ffn_conv_b, ffn_down, norm_final):
    h = x
    v_first = None
    for l in range(DEPTH):
        vres = None if l == 0 else (w_vres[l - 1], mu_vres[l - 1], v0[l - 1], v_lora[l - 1])
        mix, v_first = hybrid_token_mixer(
            rms_norm(h, norm_mix[l]), w_comb[l], conv_w[l], mu_rwkv[l], w0[l], w_lora[l], a0[l],
            a_lora[l], g_lora[l], k_k[l], k_a[l], r_k[l], lnx_w[l], lnx_b[l], branch_proj[l],
            gate_b[l], w_mix_out[l], v_first, vres)
        h = h + mix
        h = h + memory_cross_attention(rms_norm(h, norm_ca[l]), rms_norm(mem, norm_mem[l]),
                                       ca_wq[l], ca_wkv[l], ca_wo[l])
        h = h + conv_ffn(rms_norm(h, norm_ffn[l]), ffn_up[l], ffn_conv_w[l], ffn_conv_b[l],
                         ffn_down[l])
    return rms_norm(h, norm_final)


D_SSM = D_MODEL
SSM_HEAD_DIM = 64
SSM_HEADS = D_SSM // SSM_HEAD_DIM
SSM_GROUPS = 2
SSM_STATE = 128
CONV_WIDTH = 5
CHUNK = 128
D_XBC = D_SSM + 2 * SSM_GROUPS * SSM_STATE

ATTN_HEAD_DIM = 64
ATTN_HEADS = D_MODEL // ATTN_HEAD_DIM
ATTN_KV_HEADS = 4
D_ATTN = ATTN_HEADS * ATTN_HEAD_DIM
D_KV = ATTN_KV_HEADS * ATTN_HEAD_DIM
WINDOW = 128
BLOCK = 128

D_MIX = D_SSM + D_ATTN
D_FF = 4 * D_MODEL
EPS = 1e-6

IN_SIZES = (D_SSM, D_XBC, 2 * SSM_HEADS, D_ATTN, D_KV, D_KV)
D_IN = sum(IN_SIZES)
IN_OFFSETS = tuple(int(o) for o in np.cumsum(IN_SIZES)[:-1])


def rmsnorm(x, w):
    xf = x.astype(jnp.float32)
    y = xf * lax.rsqrt(jnp.mean(xf * xf, axis=-1, keepdims=True) + EPS)
    return (y * w.astype(jnp.float32)).astype(x.dtype)

def depthwise_conv_centred(u, w, b):
    c = u.shape[-1]
    out = lax.conv_general_dilated(
        u, w[:, None, :].astype(u.dtype), window_strides=(1,),
        padding=[(CONV_WIDTH // 2, CONV_WIDTH // 2)],
        dimension_numbers=("NWC", "WIO", "NWC"), feature_group_count=c)
    return out + b.astype(u.dtype)

def ssd_scan(X, dt, A, B, C):
    b, l, h, p = X.shape
    g, n = B.shape[2], B.shape[3]
    r = h // g
    c = l // CHUNK
    Xd = (X.astype(jnp.float32) * dt[..., None]).reshape(b, c, CHUNK, g, r, p)
    dA = (dt * A).reshape(b, c, CHUNK, g, r).transpose(0, 3, 4, 1, 2)
    Bc = B.astype(jnp.float32).reshape(b, c, CHUNK, g, n)
    Cc = C.astype(jnp.float32).reshape(b, c, CHUNK, g, n)
    A_cs = jnp.cumsum(dA, axis=-1)
    tri = jnp.tril(jnp.ones((CHUNK, CHUNK), dtype=bool))
    Lmat = jnp.exp(jnp.where(tri, A_cs[..., :, None] - A_cs[..., None, :], -jnp.inf))
    CB = jnp.einsum("bclgn,bcsgn->bgcls", Cc, Bc)
    Y_diag = jnp.einsum("bgrcls,bcsgrp->bclgrp", CB[:, :, None] * Lmat, Xd)
    decay_states = jnp.exp(A_cs[..., -1:] - A_cs)
    states = jnp.einsum("bcsgn,bgrcs,bcsgrp->bcgrpn", Bc, decay_states, Xd)
    chunk_decay = jnp.exp(A_cs[..., -1])

    def step(carry, inp):
        s_c, dec_c = inp
        return carry * dec_c[..., None, None] + s_c, carry

    init = jnp.zeros_like(states[:, 0])
    _, prev = lax.scan(step, init, (states.transpose(1, 0, 2, 3, 4, 5),
                                    chunk_decay.transpose(3, 0, 1, 2)))
    Y_off = jnp.einsum("bclgn,cbgrpn,bgrcl->bclgrp", Cc, prev, jnp.exp(A_cs))
    return (Y_diag + Y_off).reshape(b, l, h, p)

def ssd_mixer(z, xbc, dt_raw, conv_w, conv_b, dt_bias, a_log, d_skip, norm_w):
    b, l, _ = xbc.shape
    xbc = jax.nn.silu(depthwise_conv_centred(xbc, conv_w, conv_b))
    xs, Bm, Cm = jnp.split(xbc, (D_SSM, D_SSM + SSM_GROUPS * SSM_STATE), axis=-1)
    X = xs.reshape(b, l, SSM_HEADS, SSM_HEAD_DIM)
    Bm = Bm.reshape(b, l, SSM_GROUPS, SSM_STATE)
    Cm = Cm.reshape(b, l, SSM_GROUPS, SSM_STATE)
    dt = jax.nn.softplus(dt_raw.astype(jnp.float32).reshape(b, l, 2, SSM_HEADS)
                         + dt_bias.astype(jnp.float32))
    A = -jnp.exp(a_log.astype(jnp.float32))
    flip = lambda t: jnp.flip(t, axis=1)
    y_f = ssd_scan(X, dt[:, :, 0], A[0], Bm, Cm)
    y_b = flip(ssd_scan(flip(X), flip(dt[:, :, 1]), A[1], flip(Bm), flip(Cm)))
    y = y_f + y_b + X.astype(jnp.float32) * d_skip.astype(jnp.float32)[:, None]
    y = y.reshape(b, l, D_SSM)
    return rmsnorm(y * jax.nn.silu(z.astype(jnp.float32)), norm_w)

def window_attention(q, k, v, sink):
    b, l, _ = q.shape
    nb = l // BLOCK
    G, R, Dh = ATTN_KV_HEADS, ATTN_HEADS // ATTN_KV_HEADS, ATTN_HEAD_DIM
    qb = q.reshape(b, nb, BLOCK, G, R, Dh)
    pad = ((0, 0), (WINDOW, WINDOW), (0, 0))
    kp = jnp.pad(k, pad).reshape(b, nb + 2, BLOCK, G, Dh)
    vp = jnp.pad(v, pad).reshape(b, nb + 2, BLOCK, G, Dh)
    kb = jnp.concatenate([kp[:, :-2], kp[:, 1:-1], kp[:, 2:]], axis=2)
    vb = jnp.concatenate([vp[:, :-2], vp[:, 1:-1], vp[:, 2:]], axis=2)
    s = jnp.einsum("bnqgrd,bnkgd->bgrnqk", qb, kb).astype(jnp.float32) * (Dh ** -0.5)
    qi = jnp.arange(BLOCK)[:, None]
    kj = jnp.arange(3 * BLOCK)[None, :]
    dist = kj - BLOCK - qi
    key_abs = jnp.arange(nb)[:, None, None] * BLOCK + (kj - BLOCK)[None]
    valid = (jnp.abs(dist) <= WINDOW)[None] & (key_abs >= 0) & (key_abs < l)
    slopes = 2.0 ** (-8.0 * jnp.arange(1, ATTN_HEADS + 1, dtype=jnp.float32) / ATTN_HEADS)
    slopes = slopes.reshape(G, R)[:, :, None, None, None]
    s = jnp.where(valid, s - slopes * jnp.abs(dist).astype(jnp.float32), -jnp.inf)
    sk = sink.astype(jnp.float32).reshape(G, R)[:, :, None, None, None]
    m = jnp.maximum(jnp.max(s, axis=-1, keepdims=True), sk)
    p = jnp.exp(s - m)
    probs = p / (jnp.sum(p, axis=-1, keepdims=True) + jnp.exp(sk - m))
    o = jnp.einsum("bgrnqk,bnkgd->bnqgrd", probs.astype(v.dtype), vb)
    return o.reshape(b, l, D_ATTN)

def second_inputs(seed: int = 0) -> dict:
    key = jax.random.key(seed)
    ks = jax.random.split(key, 18)
    f32 = jnp.float32
    nrm = lambda k, shape, scale: jax.random.normal(k, shape, f32) * scale
    gain = lambda k, shape: 1.0 + 0.05 * jax.random.normal(k, shape, f32)
    dt0 = jnp.exp(jax.random.uniform(ks[5], (DEPTH, 2, SSM_HEADS), f32,
                                     jnp.log(1e-3), jnp.log(1e-1)))
    dt_bias = dt0 + jnp.log(-jnp.expm1(-dt0))
    a_log = jnp.log(jax.random.uniform(ks[6], (DEPTH, 2, SSM_HEADS), f32, 1.0, 16.0))
    return {
        "x": nrm(ks[0], (BATCH, SEQ, D_MODEL), 1.0),
        "norm_mix_pre": gain(ks[1], (DEPTH, D_MODEL)),
        "w_in": nrm(ks[2], (DEPTH, D_MODEL, D_IN), D_MODEL ** -0.5),
        "conv_w": nrm(ks[3], (DEPTH, CONV_WIDTH, D_XBC), CONV_WIDTH ** -0.5),
        "conv_b": nrm(ks[4], (DEPTH, D_XBC), 0.01),
        "dt_bias": dt_bias,
        "a_log": a_log,
        "d_skip": gain(ks[7], (DEPTH, SSM_HEADS)),
        "ssm_norm": gain(ks[8], (DEPTH, D_SSM)),
        "attn_sink": nrm(ks[9], (DEPTH, ATTN_HEADS), 0.5),
        "w_out": nrm(ks[10], (DEPTH, D_MIX, D_MODEL), D_MIX ** -0.5),
        "norm_mix_post": gain(ks[11], (DEPTH, D_MODEL)),
        "norm_mlp_pre": gain(ks[12], (DEPTH, D_MODEL)),
        "w_up": nrm(ks[13], (DEPTH, D_MODEL, D_FF), D_MODEL ** -0.5),
        "w_down": nrm(ks[14], (DEPTH, D_FF, D_MODEL), D_FF ** -0.5),
        "norm_mlp_post": gain(ks[15], (DEPTH, D_MODEL)),
    }

def second_block(x, norm_mix_pre, w_in, conv_w, conv_b, dt_bias, a_log, d_skip, ssm_norm,
              attn_sink, w_out, norm_mix_post, norm_mlp_pre, w_up, w_down, norm_mlp_post):
    for i in range(DEPTH):
        h = rmsnorm(x, norm_mix_pre[i])
        proj = h @ w_in[i]
        z, xbc, dt_raw, q, k, v = jnp.split(proj, IN_OFFSETS, axis=-1)
        y_ssm = ssd_mixer(z, xbc, dt_raw, conv_w[i], conv_b[i], dt_bias[i], a_log[i],
                          d_skip[i], ssm_norm[i])
        y_attn = window_attention(q, k, v, attn_sink[i])
        mix = jnp.concatenate([y_ssm.astype(x.dtype), y_attn.astype(x.dtype)], axis=-1) @ w_out[i]
        x = x + rmsnorm(mix, norm_mix_post[i])
        h = rmsnorm(x, norm_mlp_pre[i])
        f = jnp.square(jax.nn.relu(h @ w_up[i])) @ w_down[i]
        x = x + rmsnorm(f, norm_mlp_post[i])
    return x


def setup_inputs(seed=0):
    out = dict(first_inputs(seed))
    for name, value in second_inputs(seed + 1).items():
        if name != "x":
            out[name + "_2"] = value
    return out


def reference(
    x, mem, norm_mix, w_comb, conv_w, mu_rwkv, w0, w_lora, a0, a_lora, g_lora, k_k, k_a, r_k,
    lnx_w, lnx_b, w_vres, mu_vres, v0, v_lora, branch_proj, gate_b, w_mix_out, norm_ca,
    norm_mem, ca_wq, ca_wkv, ca_wo, norm_ffn, ffn_up, ffn_conv_w, ffn_conv_b, ffn_down,
    norm_final, norm_mix_pre_2, w_in_2, conv_w_2, conv_b_2, dt_bias_2, a_log_2, d_skip_2,
    ssm_norm_2, attn_sink_2, w_out_2, norm_mix_post_2, norm_mlp_pre_2, w_up_2, w_down_2,
    norm_mlp_post_2,
):
    x = first_block(
        x, mem, norm_mix, w_comb, conv_w, mu_rwkv, w0, w_lora, a0, a_lora, g_lora, k_k, k_a,
        r_k, lnx_w, lnx_b, w_vres, mu_vres, v0, v_lora, branch_proj, gate_b, w_mix_out, norm_ca,
        norm_mem, ca_wq, ca_wkv, ca_wo, norm_ffn, ffn_up, ffn_conv_w, ffn_conv_b, ffn_down,
        norm_final,
    )
    return second_block(
        x, norm_mix_pre_2, w_in_2, conv_w_2, conv_b_2, dt_bias_2, a_log_2, d_skip_2, ssm_norm_2,
        attn_sink_2, w_out_2, norm_mix_post_2, norm_mlp_pre_2, w_up_2, w_down_2,
        norm_mlp_post_2,
    )


_drawn_inputs = setup_inputs


def setup_inputs(seed=0):
    import zlib

    import numpy as np

    out = dict(_drawn_inputs(seed))
    spreads = {}
    factors = {'k_k': 7.617,
     'lnx_w': 8.0,
     'lnx_b': 7.145,
     'gate_b': 8.0,
     'norm_ca': 8.0,
     'norm_mem': 8.0,
     'norm_ffn': 4.038,
     'ffn_conv_b': 3.653,
     'conv_b_2': 5.291,
     'd_skip_2': 2.999,
     'attn_sink_2': 8.0}
    for name, (base, spread) in spreads.items():
        noise = np.random.default_rng([zlib.crc32(name.encode()), seed]).standard_normal(out[name].shape)
        drawn = base * np.exp(spread * noise) if base else spread * noise
        out[name] = jnp.asarray(drawn.astype(out[name].dtype))
    for name, factor in factors.items():
        out[name] = (out[name] * factor).astype(out[name].dtype)
    return out
```

```python
import concourse.bass as bass
from concourse import mybir
from contextlib import ExitStack

F32 = mybir.dt.float32
F32R = mybir.dt.float32r
I32 = mybir.dt.int32
ALU = mybir.AluOpType
ACT = mybir.ActivationFunctionType
AX = mybir.AxisListType
ds = bass.ds

P = 128
S = 512
D = 1024
KD = D // P
SB = S // P
MEM = 256
W = 512
KW = W // P
RMS_EPS = 1e-6
GN_EPS = 64e-5
DECAY_SCALE = 0.6065306597126334
FFN = 2816
HF = FFN // P // 2
MLP = 4096
HM = MLP // P // 2
OFF_SB, OFF_GATE = 3 * W, 6 * W
OFF_RWKV = OFF_GATE + 3 * D
OFF_XBC, OFF_DT, OFF_Q, OFF_K, OFF_V = 1024, 2560, 2592, 3616, 3872
CHUNK = 2048

PARAM_ROWS = [("norm_mix", 8), ("conv_w", 12), ("mu_rwkv", 14), ("w0", 4), ("a0", 4), ("k_k", 4), ("k_a", 4),
              ("r_k", 4), ("lnx_w", 4), ("lnx_b", 4), ("gate_b", 24), ("norm_ca", 8), ("norm_mem", 8),
              ("norm_ffn", 8), ("ffn_conv_w", 132), ("ffn_conv_b", 44), ("norm_final", 8),
              ("norm_mix_pre_2", 8), ("conv_w_2", 60), ("conv_b_2", 12), ("ssm_norm_2", 8),
              ("norm_mix_post_2", 8), ("norm_mlp_pre_2", 8), ("norm_mlp_post_2", 8)]
PARAM_AT = {}
for _name, _rows in PARAM_ROWS:
    PARAM_AT[_name] = sum(r for _, r in PARAM_ROWS[:len(PARAM_AT)])
PARAM_TILES = 4


class Chunk:

    def __init__(self, at, per=0, turn=0):
        self.at, self.per, self.turn = at, per, turn
        self.slot = at % 2

    @property
    def number(self):
        return self.at + self.turn * self.per if self.per else self.at

    @property
    def rounds(self):
        return self.at // 2 + self.turn * (self.per // 2) if self.per else self.at // 2

    def next(self, k=1):
        return Chunk(self.at + k, self.per, self.turn)


class Signal:

    def __init__(self, sem):
        self.sem, self.taken = sem, 0

    def take(self, count):
        base, self.taken = self.taken, self.taken + count
        return base


class Core:

    def __init__(self, nc, inputs, out, stack):
        self.nc, self.a, self.out = nc, inputs, out
        def sb(name, shape, dt=F32):
            return stack.enter_context(nc.sbuf_tensor(name, shape, dt))
        def sem(name):
            return stack.enter_context(nc.semaphore(name))
        self.own, self.cleared = (ExitStack(), []), (ExitStack(), [])
        self.params = sb("params", [P, PARAM_TILES * P])
        self.ident = sb("ident", [P, P])
        self.ones = sb("ones", [P, P])
        self.pair_ones = sb("pair_ones", [P, P])
        self.upper = sb("upper", [P, P])
        self.strict = sb("strict", [P, P])
        self.lower = sb("lower", [P, P])
        self.neg_lower = sb("neg_lower", [P, P])
        self.neg_ones = sb("neg_ones", [P, P])
        self.w_raw = [sb(f"w_raw{u}", [P, CHUNK]) for u in range(2)]
        self.w_hi = [sb(f"w_hi{u}", [P, CHUNK], F32R) for u in range(2)]
        self.w_lo = [sb(f"w_lo{u}", [P, CHUNK], F32R) for u in range(2)]
        self.scrap = sb("scrap", [P, 2])
        self.psum = stack.enter_context(nc.psum_tensor("psum", [P, 8, 512], F32))
        self.w_loaded = [sem(f"w_loaded{u}") for u in range(2)]
        self.w_hi_made = sem("w_hi_made")
        self.w_split = sem("w_split")
        self.chunk_done = sem("chunk_done")
        self.signals = {}
        for name in ("act_evac", "dve_evac", "squares_made", "square_sums", "inverse_made", "rstd_made", "normed",
                     "x_hi_made", "x_split", "dve_chain", "act_chain", "loads", "stores"):
            self.signals[name] = Signal(sem(name))
        dram = lambda name, shape: nc.dram_tensor(name, shape, F32, kind="Internal").ap()
        self.h_dram = dram("h_spill", [P, KD * S])
        self.x_dram = [dram(f"x_spill{u}", [P, KD * S]) for u in range(2)]
        self.y_dram = [dram(f"y_spill{u}", [P, 3 * KW * S]) for u in range(2)]
        self.chunks = 0
        self.stages = []

    def next_phase(self):
        self.cleared[0].close()
        for s in self.own[1]:
            self.nc.gpsimd.sem_clear(s)
        self.cleared, self.own = self.own, (ExitStack(), [])

    def sem(self, name):
        s = self.own[0].enter_context(self.nc.semaphore(name))
        self.own[1].append(s)
        return s

    def param(self, name, col, n=1):
        return self.params[:, ds(PARAM_AT[name] + col, n)]


    def load_chunk(self, sp, c, parts):
        if c.at >= 2:
            wait_alone(sp, self.w_split, c.number - 1)
        at = 0
        for part in parts:
            rows, cols = part.shape[1:]
            dst = self.w_raw[c.slot][:, at:at + rows * cols].rearrange("p (a b) -> p a b", a=rows)
            sp.dma_start(dst, part).then_inc(self.w_loaded[c.slot], 16)
            at += rows * cols

    def split_chunk(self, dve, c):
        dve.wait_ge(self.w_loaded[c.slot], 32 * (c.rounds + 1))
        if c.at >= 2:
            dve.wait_ge(self.chunk_done, c.number - 1)
        self.nc.vector.tensor_copy(self.w_hi[c.slot][:, :], self.w_raw[c.slot][:, :]).then_inc(self.w_hi_made, 1)
        dve.wait_ge(self.w_hi_made, c.number + 1)
        self.nc.vector.tensor_tensor(self.w_lo[c.slot][:, :], self.w_raw[c.slot][:, :],
                                     self.w_hi[c.slot][:, :].bitcast(F32), ALU.subtract).then_inc(self.w_split, 1)

    def weights(self, c, *shape):
        n = 1
        for x in shape:
            n *= x
        names = "abc"[:len(shape)]
        pattern = f"p ({' '.join(names)}) -> p {' '.join(names)}"
        sizes = {k: v for k, v in zip(names, shape)}
        return [w[c.slot][:, 0:n].rearrange(pattern, **sizes) for w in (self.w_hi, self.w_lo)]

    def product(self, out, w, x, first, last):
        mm = self.nc.tensor.matmul
        mm(out, w[0], x[0], start=first, stop=False)
        mm(out, w[0], x[1], start=False, stop=False)
        return mm(out, w[1], x[0], start=False, stop=last)


def wait_alone(engine, sem, value):
    if not isinstance(value, int):
        value = engine.to_reg(value)
        engine.wait_ge(sem, 1)
    engine.wait_ge(sem, value)


def turns_of(engine, stage, peeled=0):
    kinds, per = len(stage.kinds), stage.per
    turns = stage.steps // per - peeled
    if turns == 1:
        for u in range(per):
            yield u, u % 2, Chunk(stage.base + u * kinds)
    elif turns:
        with engine.Fori(0, turns) as i:
            for u in range(per):
                yield i * per + u, u % 2, Chunk(stage.base + u * kinds, per * kinds, i)
    for s in range(turns * per, stage.steps):
        yield s, s % 2, Chunk(stage.base + s * kinds)


class Stage:

    def __init__(self, core, steps, kinds, per=2):
        assert per * len(kinds) % 2 == 0
        self.steps, self.kinds, self.per = steps, kinds, per
        self.base = core.chunks
        self.count = steps * len(kinds)
        core.chunks += self.count
        core.stages.append(self)


def load_from(core, sp, number):
    for st in core.stages:
        if st.base <= number < st.base + st.count:
            at = number - st.base
            core.load_chunk(sp, Chunk(number), st.kinds[at % len(st.kinds)](at // len(st.kinds)))


def load_stage(core, sp, st):
    period = st.per * len(st.kinds)
    turns = st.steps // st.per
    looped = turns if turns >= 3 else 1
    for number in range(st.base + 2, st.base + period):
        if number < st.base + st.count:
            load_from(core, sp, number)
    if looped > 1:
        with sp.Fori(1, looped) as i:
            for u in range(st.per):
                for k, kind in enumerate(st.kinds):
                    core.load_chunk(sp, Chunk(st.base + u * len(st.kinds) + k, period, i), kind(i * st.per + u))
    for number in range(max(st.base + 2, st.base + looped * period), st.base + st.count + 2):
        load_from(core, sp, number)


def one(i):
    return ds(i, 1)


def weight_stages(core):
    a = core.a
    kp = lambda w: w.rearrange("(k p) m -> p k m", p=P)
    wc = kp(a["w_comb"][0])
    bp = a["branch_proj"][0].rearrange("g (k p) m -> p (g k) m", p=P)
    half = lambda w: [w[:, 0:w.shape[1] // 2, :], w[:, w.shape[1] // 2:, :]]
    cols = lambda w, n: (lambda s: half(w[:, :, ds(s * n, n)]))
    tiles2 = lambda w: cols(w, 2 * P)
    tile1 = lambda w: cols(w, P)
    two = lambda at, gap: (lambda s: [wc[:, :, ds(s * P + at + g * gap, P)] for g in range(2)])
    st = {}
    st["conv"] = Stage(core, KW, [two(W, W), tile1(wc)])
    st["sb_v"] = Stage(core, 2, [tiles2(wc[:, :, OFF_SB + 2 * W:OFF_GATE])])
    st["sb_qk"] = Stage(core, KW, [two(OFF_SB, W)])
    st["rkv"] = Stage(core, KW, [two(OFF_RWKV, W), tile1(wc[:, :, OFF_RWKV + 2 * W:])])
    st["lora"] = Stage(core, 1, [tiles2(wc[:, :, OFF_RWKV + 3 * W:])])
    st["gates"] = Stage(core, KD, [two(OFF_GATE, D), tile1(wc[:, :, OFF_GATE + 2 * D:]), tile1(bp)])
    st["mix"] = Stage(core, 4, [tiles2(kp(a["w_mix_out"][0]))])
    st["ca_q"] = Stage(core, 4, [tiles2(kp(a["ca_wq"][0]))])
    wkv = kp(a["ca_wkv"][0])
    st["ca_k"] = Stage(core, 4, [tiles2(wkv[:, :, 0:D])])
    st["ca_v"] = Stage(core, 4, [tiles2(wkv[:, :, D:2 * D])])
    st["ca_o"] = Stage(core, 4, [tiles2(kp(a["ca_wo"][0]))])
    up = kp(a["ffn_up"][0])
    down = a["ffn_down"][0].rearrange("(h k p) m -> h p k m", h=2, p=P)
    for h in range(2):
        st[f"ffn_up{h}"] = Stage(core, HF, [(lambda h: lambda s: [up[:, :, ds(s * P + (h * HF + g * 2 * HF) * P, P)] for g in range(2)])(h)])
        st[f"ffn_down{h}"] = Stage(core, KD, [tile1(down[h])])
    wi = kp(a["w_in_2"][0])
    st["xbc"] = Stage(core, 6, [tiles2(wi[:, :, OFF_XBC:OFF_DT])])
    st["z"] = Stage(core, 4, [tiles2(wi[:, :, 0:OFF_XBC])])
    st["q2"] = Stage(core, 4, [tiles2(wi[:, :, OFF_Q:OFF_K])])
    st["kvdt"] = Stage(core, 3, [lambda s: half(wi[:, :, OFF_DT:OFF_DT + P] if s == 2 else
                                                wi[:, :, OFF_K + 256 * s:OFF_K + 256 * s + 256])])
    st["out2"] = Stage(core, KD, [tile1(kp(a["w_out_2"][0]))])
    up2 = kp(a["w_up_2"][0])
    down2 = a["w_down_2"][0].rearrange("(h k p) m -> h p k m", h=2, p=P)
    for h in range(2):
        st[f"mlp_up{h}"] = Stage(core, HM // 2, [tiles2(up2[:, :, h * HM * P:(h + 1) * HM * P])])
        st[f"mlp_down{h}"] = Stage(core, KD, [tile1(down2[h])])
    return st



def start(core):
    core.next_phase()
    nc, a, psum = core.nc, core.a, core.psum
    with ExitStack() as scope, nc.Block() as block:
        x_rows = scope.enter_context(nc.sbuf_tensor("x_rows", [P, SB, D], F32))
        param_rows = scope.enter_context(nc.sbuf_tensor("param_rows", [P, PARAM_TILES, P], F32))
        rows_cleared, rows_loaded, x_loaded = core.sem("rows_cleared"), core.sem("param_rows_loaded"), core.sem("x_loaded")
        made, masks = core.sem("constants_made"), core.sem("masks_made")
        turned, kept = core.sem("start_turned"), core.sem("start_kept")
        h_stored = core.sem("h_stored")
        raw_cleared = core.sem("w_raw_cleared")
        column_dmas = []

        @block.sync
        def _(sp):
            sp.wait_ge(raw_cleared, 1)
            load_from(core, sp, 0)
            sp.dma_start(x_rows[:, :, :], a["x"][0].rearrange("(b p) d -> p b d", p=P)).then_inc(x_loaded, 16)
            load_from(core, sp, 1)
            sp.wait_ge(rows_cleared, 1)
            for name, rows in PARAM_ROWS:
                v = a[name]
                flat = v.rearrange(" ".join("abcd"[:len(v.shape)]) + " -> (" + " ".join("abcd"[:len(v.shape)]) + ")")
                flat = flat.rearrange("(r c) -> r c", c=P)
                done = 0
                while done < rows:
                    at = PARAM_AT[name] + done
                    n = min(rows - done, P - at % P)
                    sp.dma_start(param_rows[at % P:at % P + n, at // P, :], flat[done:done + n, :])\
                        .then_inc(rows_loaded, 16)
                    column_dmas.append(name)
                    done += n
            sp.wait_ge(kept, KD + PARAM_TILES)
            sp.dma_start(core.h_dram.rearrange("p (k s) -> p k s", k=KD), core.h[:, :, :]).then_inc(h_stored, 16)
            sp.wait_ge(h_stored, 16)

        @block.gpsimd
        def _(pool):
            g = nc.gpsimd
            g.memset(param_rows[:, :, :], 0.0).then_inc(rows_cleared, 1)
            g.memset(core.ident[:, :], 0.0).then_inc(made, 1)
            g.memset(core.ones[:, :], 1.0).then_inc(made, 1)
            g.memset(core.neg_ones[:, :], -1.0).then_inc(made, 1)
            g.memset(core.pair_ones[:, :], 0.0).then_inc(made, 1)
            pool.wait_ge(made, 4)
            g.memset(core.pair_ones[0:64, 0:64], 1.0).then_inc(made, 1)
            pool.wait_ge(made, 5)
            g.memset(core.pair_ones[64:128, 64:128], 1.0).then_inc(made, 1)
            pool.wait_ge(made, 6)
            g.affine_select(out=core.ident[:, :], in_=core.ident[:, :], compare_op=ALU.not_equal, fill=1.0, base=0,
                            pattern=[[-1, P]], channel_multiplier=1).then_inc(masks, 1)
            g.affine_select(out=core.upper[:, :], in_=core.ones[:, :], compare_op=ALU.is_ge, fill=0.0, base=0,
                            pattern=[[1, P]], channel_multiplier=-1).then_inc(masks, 1)
            g.affine_select(out=core.strict[:, :], in_=core.ones[:, :], compare_op=ALU.is_gt, fill=0.0, base=0,
                            pattern=[[1, P]], channel_multiplier=-1).then_inc(masks, 1)
            g.affine_select(out=core.lower[:, :], in_=core.ones[:, :], compare_op=ALU.is_ge, fill=0.0, base=0,
                            pattern=[[-1, P]], channel_multiplier=1).then_inc(masks, 1)
            g.affine_select(out=core.neg_lower[:, :], in_=core.neg_ones[:, :], compare_op=ALU.is_ge, fill=0.0, base=0,
                            pattern=[[-1, P]], channel_multiplier=1).then_inc(masks, 1)

        @block.tensor
        def _(pe):
            pe.wait_ge(masks, 5)
            pe.wait_ge(x_loaded, 16)
            for k in range(KD):
                for b in range(SB):
                    last = nc.tensor.transpose(psum[:, k, b * P:(b + 1) * P], x_rows[:, b, k * P:(k + 1) * P],
                                               core.ident[:, :])
                last.then_inc(turned, 1)
            pe.wait_ge(rows_loaded, 16 * len(column_dmas))
            pe.wait_ge(kept, 1)
            for t in range(PARAM_TILES):
                last = nc.tensor.transpose(psum[:, 0, t * P:(t + 1) * P], param_rows[:, t, :], core.ident[:, :])
            last.then_inc(turned, 1)

        @block.vector
        def _(dve):
            nc.vector.memset(core.w_raw[0][:, :], 0.0)
            nc.vector.memset(core.w_raw[1][:, :], 0.0).then_inc(raw_cleared, 1)
            core.split_chunk(dve, Chunk(0))
            for k in range(KD):
                dve.wait_ge(turned, k + 1)
                nc.vector.tensor_copy(core.h[:, k, :], psum[:, k, :]).then_inc(kept, 1)
            dve.wait_ge(turned, KD + 1)
            nc.vector.tensor_copy(core.params[:, :], psum[:, 0, :]).then_inc(kept, PARAM_TILES)
            nc.vector.memset(core.scrap[:, 0:1], 0.0).then_inc(core.signals["dve_evac"].sem, core.signals["dve_evac"].take(2) + 2)

        @block.scalar
        def _(act):
            act.wait_ge(made, 6)
            nc.scalar.activation(core.scrap[:, 1:2], core.ones[:, 0:1], ACT.Copy)\
                .then_inc(core.signals["act_evac"].sem, core.signals["act_evac"].take(2) + 2)



class Norm:

    def __init__(self, core, src, work, rstd, gain, hi=None, lo=None, width=S, bank=7, dest=None):
        self.core, self.src, self.work, self.rstd, self.gain = core, src, work, rstd, gain
        self.hi, self.lo, self.width, self.bank = hi, lo, width, bank
        self.dest = work if dest is None else dest
        take = lambda name, n: core.signals[name].take(n)
        self.squares, self.sums, self.inverse = take("squares_made", 4), take("square_sums", 1), take("inverse_made", 2)
        self.made, self.normed = take("rstd_made", 1), take("normed", KD)
        self.his, self.split = (take("x_hi_made", 4), take("x_split", 4)) if hi is not None else (0, 0)

    def on(self, name):
        return self.core.signals[name].sem

    def act(self, act):
        nc = self.core.nc
        for q in range(4):
            nc.scalar.activation(self.work[:, 2 * q:2 * q + 2, :], self.src[:, 2 * q:2 * q + 2, :], ACT.Square)\
                .then_inc(self.on("squares_made"), 1)
        act.wait_ge(self.on("inverse_made"), self.inverse + 2)
        nc.scalar.activation(self.rstd[:, 0:self.width], self.rstd[:, 0:self.width], ACT.Sqrt)\
            .then_inc(self.on("rstd_made"), 1)
        if self.hi is None:
            return
        for q in range(4):
            act.wait_ge(self.on("normed"), self.normed + 2 * q + 2)
            nc.scalar.activation(self.hi[:, 2 * q:2 * q + 2, :], self.work[:, 2 * q:2 * q + 2, :], ACT.Copy)\
                .then_inc(self.on("x_hi_made"), 1)

    def pe(self, pe):
        nc = self.core.nc
        for k in range(KD):
            if k % 2 == 0:
                pe.wait_ge(self.on("squares_made"), self.squares + k // 2 + 1)
            last = nc.tensor.matmul(self.core.psum[:, self.bank, 0:self.width], self.core.ones[:, :],
                                    self.work[:, k, :], start=k == 0, stop=k == KD - 1)
        last.then_inc(self.on("square_sums"), 1)

    def dve(self, dve):
        nc, n = self.core.nc, self.width
        dve.wait_ge(self.on("square_sums"), self.sums + 1)
        nc.vector.tensor_scalar(self.rstd[:, 0:n], self.core.psum[:, self.bank, 0:n], 1.0 / D, RMS_EPS,
                                ALU.mult, ALU.add).then_inc(self.on("inverse_made"), 1)
        dve.wait_ge(self.on("inverse_made"), self.inverse + 1)
        nc.vector.reciprocal(self.rstd[:, 0:n], self.rstd[:, 0:n]).then_inc(self.on("inverse_made"), 1)
        dve.wait_ge(self.on("rstd_made"), self.made + 1)
        for k in range(KD):
            nc.vector.scalar_tensor_tensor(self.dest[:, k, :], self.src[:, k, :], self.core.param(self.gain, k),
                                           self.rstd[:, 0:n], ALU.mult, ALU.mult).then_inc(self.on("normed"), 1)
        if self.hi is None:
            return
        for q in range(4):
            dve.wait_ge(self.on("x_hi_made"), self.his + q + 1)
            nc.vector.tensor_tensor(self.lo[:, 2 * q:2 * q + 2, :], self.work[:, 2 * q:2 * q + 2, :],
                                    self.hi[:, 2 * q:2 * q + 2, :].bitcast(F32), ALU.subtract)\
                .then_inc(self.on("x_split"), 1)

    def ready(self, engine, k):
        engine.wait_ge(self.on("x_split"), self.split + k // 2 + 1)


def store_split(core, sp, tiles, at, parts, sem):
    for v, part in enumerate(parts):
        sp.dma_start(core.y_dram[v][:, at * S:(at + tiles) * S].rearrange("p (k s) -> p k s", k=tiles),
                     part[:, :, :].bitcast(F32)).then_inc(sem, 16)



def conv_branch(core):
    core.next_phase()
    nc, psum, st = core.nc, core.psum, core.st["conv"]
    evac, evac0 = core.signals["dve_evac"].sem, core.signals["dve_evac"].take(KW)
    with ExitStack() as scope, nc.Block() as block:
        sb = lambda name, shape, dt=F32: scope.enter_context(nc.sbuf_tensor(name, shape, dt))
        work, rstd = sb("norm_work", [P, KD, S]), sb("rstd", [P, S])
        norm = Norm(core, core.h, work, rstd, "norm_mix", core.x_hi, core.x_lo)
        gate_c = sb("conv_c", [P, 2, S])
        y, product, mixed = work[:, 0:4, :], work[:, 4:6, :], work[:, 6:8, :]
        y_hi, y_lo = sb("conv_y_hi", [P, KW, S], F32R), sb("conv_y_lo", [P, KW, S], F32R)
        c_kept, cx_made, taps = (core.sem(n) for n in ("conv_c_kept", "conv_cx_made", "conv_taps"))
        y_hi_made, y_split, y_stored = core.sem("conv_y_hi_made"), core.sem("conv_y_split"), core.sem("conv_y_stored")
        x_stored = core.sem("x_stored")
        done = core.chunk_done

        @block.sync
        def _(sp):
            load_stage(core, sp, st)
            norm.ready(sp, KD - 1)
            for u, x in enumerate((core.x_hi, core.x_lo)):
                sp.dma_start(core.x_dram[u].rearrange("p (k s) -> p k s", k=KD), x[:, :, :].bitcast(F32))\
                    .then_inc(x_stored, 16)
            sp.wait_ge(y_split, KW)
            store_split(core, sp, KW, 0, (y_hi, y_lo), y_stored)
            sp.wait_ge(y_stored, 32)
            sp.wait_ge(x_stored, 32)

        @block.tensor
        def _(pe):
            norm.pe(pe)
            norm.ready(pe, KD - 1)
            for j, u, c in turns_of(pe, st):
                pe.wait_ge(core.w_split, c.number + 1)
                pe.wait_ge(evac, j + (evac0 - 1))
                hi, lo = core.weights(c, 2, KD, P)
                for g in range(2):
                    for k in range(KD):
                        last = core.product(psum[:, 3 * u + g, :], (hi[:, g, k, :], lo[:, g, k, :]),
                                            (core.x_hi[:, k, :], core.x_lo[:, k, :]), k == 0, k == KD - 1)
                last.then_inc(done, 1)
                b = c.next()
                pe.wait_ge(core.w_split, b.number + 1)
                hi, lo = core.weights(b, KD, P)
                for k in range(KD):
                    last = core.product(psum[:, 3 * u + 2, :], (hi[:, k, :], lo[:, k, :]),
                                        (core.x_hi[:, k, :], core.x_lo[:, k, :]), k == 0, k == KD - 1)
                last.then_inc(done, 1)

        @block.scalar
        def _(act):
            norm.act(act)
            for j, u, c in turns_of(act, st):
                act.wait_ge(done, c.number + 1)
                nc.scalar.activation(gate_c[:, u, :], psum[:, 3 * u, :], ACT.Copy).then_inc(c_kept, 1)
                act.wait_ge(evac, j + (evac0 + 1))
                nc.scalar.activation(y_hi[:, one(j), :], y[:, one(j), :], ACT.Copy).then_inc(y_hi_made, 1)

        @block.vector
        def _(dve):
            norm.dve(dve)
            for j, u, c in turns_of(dve, st):
                core.split_chunk(dve, c.next())
                dve.wait_ge(done, c.number + 1)
                dve.wait_ge(c_kept, j + 1)
                nc.vector.tensor_tensor(product[:, u, :], gate_c[:, u, :], psum[:, 3 * u + 1, :], ALU.mult)\
                    .then_inc(cx_made, 1)
                dve.wait_ge(cx_made, j + 1)
                nc.vector.tensor_scalar(mixed[:, u, :], product[:, u, :], core.param("conv_w", j + 2 * KW), None,
                                        ALU.mult).then_inc(taps, 1)
                for lag in (1, 2):
                    dve.wait_ge(taps, 3 * j + lag)
                    nc.vector.scalar_tensor_tensor(mixed[:, u, lag:], product[:, u, :S - lag],
                                                   core.param("conv_w", j + (2 - lag) * KW), mixed[:, u, lag:],
                                                   ALU.mult, ALU.add).then_inc(taps, 1)
                core.split_chunk(dve, c.next(2))
                dve.wait_ge(done, c.number + 2)
                dve.wait_ge(taps, 3 * j + 3)
                nc.vector.tensor_tensor(y[:, one(j), :], mixed[:, one(u), :], psum[:, one(3 * u + 2), :], ALU.mult)\
                    .then_inc(evac, 1)
                dve.wait_ge(y_hi_made, j + 1)
                nc.vector.tensor_tensor(y_lo[:, one(j), :], y[:, one(j), :], y_hi[:, one(j), :].bitcast(F32),
                                        ALU.subtract).then_inc(y_split, 1)



Z_WIDTH = [S - b * P for b in range(SB)]
Z_AT = [0, 512, 1024, 896]


def stick_breaking(core):
    core.next_phase()
    nc, psum = core.nc, core.psum
    st_v, st = core.st["sb_v"], core.st["sb_qk"]
    flat = psum[:, :, :].rearrange("p b c -> p (b c)")
    mm = nc.tensor.matmul
    with ExitStack() as scope, nc.Block() as block:
        sb = lambda name, shape, dt=F32: scope.enter_context(nc.sbuf_tensor(name, shape, dt))
        v_rows, v_pair = sb("sb_v_rows", [P, SB, W]), sb("sb_v_pair", [P, 2, SB, P])
        q, k_, y = sb("sb_q", [P, 2, S]), sb("sb_k", [P, 2, S]), sb("sb_y", [P, KW, S])
        y_hi, y_lo = sb("sb_y_hi", [P, KW, S], F32R), sb("sb_y_lo", [P, KW, S], F32R)
        t = sb("sb_softplus", [P, 2, 1280])
        done = core.chunk_done
        names = ("v_kept", "v_staged", "q_kept", "k_kept", "z_made", "abs_made", "exp_made", "log_made", "sp_raw",
                 "sp_masked", "cum_made", "att_raw", "att_masked", "o_made", "o_kept", "y_hi_made", "y_split", "y_stored")
        s_ = {n: core.sem("sb_" + n) for n in names}

        @block.sync
        def _(sp):
            load_stage(core, sp, st_v)
            load_stage(core, sp, st)
            sp.wait_ge(s_["y_split"], 1)
            store_split(core, sp, KW, KW, (y_hi, y_lo), s_["y_stored"])
            sp.wait_ge(s_["y_stored"], 32)

        @block.tensor
        def _(pe):
            for c in range(2):
                pe.wait_ge(core.w_split, st_v.base + c + 1)
                w = core.weights(Chunk(st_v.base + c), KD, 256)
                for b in range(SB):
                    for k in range(KD):
                        x = [v[:, k, b * P:(b + 1) * P] for v in (core.x_hi, core.x_lo)]
                        last = core.product(psum[:, 2 * c + b // 2, b % 2 * 256:b % 2 * 256 + 256], x,
                                            (w[0][:, k, :], w[1][:, k, :]), k == 0, k == KD - 1)
                last.then_inc(done, 1)

            def project(j):
                c = Chunk(st.base + j)
                pe.wait_ge(core.w_split, c.number + 1)
                if j == 0:
                    pe.wait_ge(s_["v_kept"], 2)
                else:
                    pe.wait_ge(s_["q_kept"], j)
                    pe.wait_ge(s_["k_kept"], j)
                hi, lo = core.weights(c, 2, KD, P)
                for g in range(2):
                    for k in range(KD):
                        last = core.product(psum[:, g, :], (hi[:, g, k, :], lo[:, g, k, :]),
                                            (core.x_hi[:, k, :], core.x_lo[:, k, :]), k == 0, k == KD - 1)
                last.then_inc(done, 1)

            project(0)
            for j in range(KW):
                u = j % 2
                pe.wait_ge(s_["q_kept"], j + 1)
                pe.wait_ge(s_["k_kept"], j + 1)
                for r in range(2):
                    if j:
                        pe.wait_ge(s_["o_kept"], 2 * j + r - 1)
                    z0, rows = (2 + 3 * r) * 512, slice(64 * r, 64 * r + 64)
                    for b in range(SB):
                        last = mm(flat[:, z0 + Z_AT[b]:z0 + Z_AT[b] + Z_WIDTH[b]], k_[rows, u, b * P:(b + 1) * P],
                                  q[rows, u, b * P:], start=b != 3, stop=False, skip_group_check=True)
                    last.then_inc(s_["z_made"], 1)
                if j + 1 < KW:
                    project(j + 1)
                for r in range(2):
                    z0 = (2 + 3 * r) * 512
                    pe.wait_ge(s_["sp_masked"], 2 * (2 * j + r) + 2)
                    for b in range(SB):
                        for c in range(b, SB):
                            at = z0 + Z_AT[b] + (c - b) * P
                            last = mm(flat[:, at:at + Z_WIDTH[c]], (core.neg_lower if c == b else core.neg_ones)[:, :],
                                      t[:, r, Z_AT[c]:Z_AT[c] + Z_WIDTH[c]], start=False, stop=False,
                                      skip_group_check=True)
                    last.then_inc(s_["cum_made"], 1)
                pe.wait_ge(s_["v_staged"], j + 1)
                for r in range(2):
                    pe.wait_ge(s_["att_masked"], 4 * (2 * j + r) + 4)
                    for b in range(SB):
                        last = mm(psum[64 * r:64 * r + 64, 2 + 3 * r, b * P:], v_pair[:, u, b, 64 * r:64 * r + 64],
                                  t[:, r, Z_AT[b]:Z_AT[b] + Z_WIDTH[b]], start=b == 0, stop=b == SB - 1,
                                  skip_group_check=True)
                    last.then_inc(s_["o_made"], 1)

        @block.scalar
        def _(act):
            for c in range(2):
                act.wait_ge(done, st_v.base + c + 1)
                nc.scalar.activation(v_rows[:, :, 256 * c:256 * c + 256],
                                     psum[:, 2 * c:2 * c + 2, :].rearrange("p a (b c) -> p (a b) c", b=2),
                                     ACT.Copy).then_inc(s_["v_kept"], 1)
            act.wait_ge(s_["v_kept"], 2)

            def keep_q(j):
                act.wait_ge(done, st.base + j + 1)
                nc.scalar.activation(q[:, j % 2, :], psum[:, 0, :], ACT.Copy, scale=0.125).then_inc(s_["q_kept"], 1)
                nc.scalar.activation(v_pair[:, j % 2, :, :], v_rows[:, :, j * P:(j + 1) * P], ACT.Copy)\
                    .then_inc(s_["v_staged"], 1)

            keep_q(0)
            for j in range(KW):
                for r in range(2):
                    n = 2 * j + r
                    z = flat[:, (2 + 3 * r) * 512:(2 + 3 * r) * 512 + 1280]
                    act.wait_ge(s_["z_made"], n + 1)
                    nc.scalar.activation(t[:, r, :], z, ACT.Abs).then_inc(s_["abs_made"], 1)
                    act.wait_ge(s_["abs_made"], n + 1)
                    nc.scalar.activation(t[:, r, :], t[:, r, :], ACT.Exp, scale=-1.0).then_inc(s_["exp_made"], 1)
                    act.wait_ge(s_["exp_made"], n + 1)
                    nc.scalar.activation(t[:, r, :], t[:, r, :], ACT.Ln, bias=1.0).then_inc(s_["log_made"], 1)
                if j + 1 < KW:
                    keep_q(j + 1)
                for r in range(2):
                    n = 2 * j + r
                    act.wait_ge(s_["cum_made"], n + 1)
                    nc.scalar.activation(t[:, r, :], flat[:, (2 + 3 * r) * 512:(2 + 3 * r) * 512 + 1280], ACT.Exp)\
                        .then_inc(s_["att_raw"], 1)
                for r in range(2):
                    act.wait_ge(s_["o_made"], 2 * j + r + 1)
                    nc.scalar.activation(y[64 * r:64 * r + 64, j, :], psum[64 * r:64 * r + 64, 2 + 3 * r, :], ACT.Copy)\
                        .then_inc(s_["o_kept"], 1)
            act.wait_ge(s_["o_kept"], 2 * KW)
            nc.scalar.activation(y_hi[:, :, :], y[:, :, :], ACT.Copy).then_inc(s_["y_hi_made"], 1)

        @block.gpsimd
        def _(pool):
            for n in range(2 * KW):
                pool.wait_ge(s_["att_raw"], n + 1)
                for b in range(SB):
                    diagonal = t[:, n % 2, Z_AT[b]:Z_AT[b] + P]
                    nc.gpsimd.affine_select(out=diagonal, in_=diagonal, compare_op=ALU.is_gt, fill=0.0, base=0,
                                            pattern=[[1, P]], channel_multiplier=-1).then_inc(s_["att_masked"], 1)

        @block.vector
        def _(dve):
            core.split_chunk(dve, Chunk(st_v.base + 1))
            core.split_chunk(dve, Chunk(st.base))

            def keep_and_split(j):
                core.split_chunk(dve, Chunk(st.base + j + 1))
                dve.wait_ge(done, st.base + j + 1)
                nc.vector.tensor_copy(k_[:, j % 2, :], psum[:, 1, :]).then_inc(s_["k_kept"], 1)

            keep_and_split(0)
            for j in range(KW):
                for r in range(2):
                    n = 2 * j + r
                    z = flat[:, (2 + 3 * r) * 512:(2 + 3 * r) * 512 + 1280]
                    dve.wait_ge(s_["log_made"], n + 1)
                    nc.vector.scalar_tensor_tensor(t[:, r, :], z, 0.0, t[:, r, :], ALU.max, ALU.add)\
                        .then_inc(s_["sp_raw"], 1)
                    dve.wait_ge(s_["sp_raw"], n + 1)
                    mask = core.strict[:, :].unsqueeze(1).broadcast_to([P, 2, P])
                    for at, gap in ((0, 512), (896, 128)):
                        pair = t[:, r, at:at + 2 * gap].rearrange("p (a c) -> p a c", a=2)[:, :, 0:P]
                        nc.vector.tensor_tensor(pair, pair, mask, ALU.mult).then_inc(s_["sp_masked"], 1)
                if j + 1 < KW:
                    keep_and_split(j + 1)
            dve.wait_ge(s_["y_hi_made"], 1)
            nc.vector.tensor_tensor(y_lo[:, :, :], y[:, :, :], y_hi[:, :, :].bitcast(F32), ALU.subtract)\
                .then_inc(s_["y_split"], 1)



LEVELS = 7
ALL = (slice(None), slice(None), slice(None))


def rwkv_projections(core):
    core.next_phase()
    nc, psum, a = core.nc, core.psum, core.a
    st, st_l = core.st["rkv"], core.st["lora"]
    evac, evac0 = core.signals["dve_evac"].sem, core.signals["dve_evac"].take(KW)
    rw = core.rw
    with ExitStack() as scope, nc.Block() as block:
        sb = lambda name, shape, dt=F32: scope.enter_context(nc.sbuf_tensor(name, shape, dt))
        scaled = sb("rw_scaled", [P, 6, S])
        one_minus = sb("rw_one_minus_mu", [P, 14])
        low = sb("rw_low", [P, 2, S])
        up = sb("rw_up", [P, 2, W])
        names = ("one_minus_made", "scaled_made", "up_loaded", "low_shifted", "low_mapped", "low_products",
                 "decay_sigmoid", "a_made", "decay_made", "g_kept", "mask_zeroed", "mask_from", "mask_made")
        s_ = {n: core.sem("rw_" + n) for n in names}
        done = core.chunk_done

        @block.sync
        def _(sp):
            sp.dma_start(up[0:64, 0, :], a["w_lora"][0]).then_inc(s_["up_loaded"], 16)
            sp.dma_start(up[64:128, 0, :], a["a_lora"][0]).then_inc(s_["up_loaded"], 16)
            sp.dma_start(up[:, 1, :], a["g_lora"][0]).then_inc(s_["up_loaded"], 16)
            load_stage(core, sp, st)
            load_stage(core, sp, st_l)

        @block.gpsimd
        def _(pool):
            g = nc.gpsimd
            g.memset(core.level_masks[:, :, :, :], 0.0).then_inc(s_["mask_zeroed"], 1)
            pool.wait_ge(s_["mask_zeroed"], 1)
            n = 0
            for level in range(LEVELS):
                w = 1 << level
                q = P // (2 * w)
                source = core.ones[:, 0:q * w].rearrange("p (q w) -> p q w", w=w)
                for flip in range(2):
                    view = core.level_masks[:, flip, level, :].rearrange("p (q h w) -> p q h w", h=2, w=w)[:, :, flip, :]
                    lo_edge = 0 if flip else w
                    g.affine_select(out=view, in_=source, compare_op=ALU.is_ge, fill=0.0, base=-lo_edge,
                                    pattern=[[-2 * w, q], [0, w]], channel_multiplier=1).then_inc(s_["mask_from"], 1)
                    n += 1
                    pool.wait_ge(s_["mask_from"], n)
                    g.affine_select(out=view, in_=view, compare_op=ALU.is_ge, fill=0.0, base=lo_edge + w - 1,
                                    pattern=[[2 * w, q], [0, w]], channel_multiplier=-1).then_inc(s_["mask_made"], 1)

        @block.tensor
        def _(pe):
            for j, u, c in turns_of(pe, st):
                pe.wait_ge(core.w_split, c.number + 1)
                pe.wait_ge(evac, j + (evac0 - 1))
                hi, lo = core.weights(c, 2, KD, P)
                for g in range(2):
                    for k in range(KD):
                        last = core.product(psum[:, 3 * u + g, :], (hi[:, g, k, :], lo[:, g, k, :]),
                                            (core.x_hi[:, k, :], core.x_lo[:, k, :]), k == 0, k == KD - 1)
                last.then_inc(done, 1)
                v = c.next()
                pe.wait_ge(core.w_split, v.number + 1)
                hi, lo = core.weights(v, KD, P)
                for k in range(KD):
                    last = core.product(psum[:, 3 * u + 2, :], (hi[:, k, :], lo[:, k, :]),
                                        (core.x_hi[:, k, :], core.x_lo[:, k, :]), k == 0, k == KD - 1)
                last.then_inc(done, 1)
            pe.wait_ge(core.w_split, st_l.base + 1)
            hi, lo = core.weights(Chunk(st_l.base), KD, 2, P)
            for g in range(2):
                for k in range(KD):
                    last = core.product(psum[:, 6 + g, :], (hi[:, k, g, :], lo[:, k, g, :]),
                                        (core.x_hi[:, k, :], core.x_lo[:, k, :]), k == 0, k == KD - 1)
            last.then_inc(done, 1)
            pe.wait_ge(s_["up_loaded"], 48)
            pe.wait_ge(s_["low_mapped"], 2)
            pe.wait_ge(evac, evac0 + KW)
            for j in range(KW):
                for part, rows in ((0, slice(0, 64)), (1, slice(64, 128))):
                    last = nc.tensor.matmul(psum[:, 4 * part + j, :], up[rows, 0, j * P:(j + 1) * P], low[rows, 0, :],
                                            start=True, stop=True)
                last.then_inc(s_["low_products"], 1)
            for j in range(KW):
                pe.wait_ge(s_["decay_sigmoid"], j + 1)
                nc.tensor.matmul(psum[:, j, :], up[:, 1, j * P:(j + 1) * P], low[:, 1, :], start=True, stop=True)\
                    .then_inc(s_["low_products"], 1)

        @block.scalar
        def _(act):
            for j, u, c in turns_of(act, st):
                for g in range(3):
                    if g != 1:
                        act.wait_ge(done, c.number + (1 if g == 0 else 2))
                    nc.scalar.activation(scaled[:, 3 * u + g, :], psum[:, 3 * u + g, :], ACT.Copy,
                                         scale=core.param("mu_rwkv", j + g * KW)).then_inc(s_["scaled_made"], 1)
            act.wait_ge(done, st_l.base + 1)
            act.wait_ge(evac, evac0 + KW)
            for g in range(2):
                nc.scalar.activation(scaled[:, g, :], psum[:, 6 + g, :], ACT.Copy,
                                     scale=core.param("mu_rwkv", 12 + g)).then_inc(s_["scaled_made"], 1)
            act.wait_ge(s_["low_shifted"], 1)
            nc.scalar.activation(low[0:64, 0, :], low[0:64, 0, :], ACT.Tanh).then_inc(s_["low_mapped"], 1)
            act.wait_ge(s_["low_shifted"], 2)
            nc.scalar.activation(low[:, 1, :], low[:, 1, :], ACT.Sigmoid).then_inc(s_["low_mapped"], 1)
            for j in range(KW):
                act.wait_ge(s_["low_products"], j + 1)
                nc.scalar.activation(rw["rw_decay"][:, j, :], psum[:, j, :], ACT.Sigmoid, bias=core.param("w0", j))\
                    .then_inc(s_["decay_sigmoid"], 1)
            for j in range(KW):
                nc.scalar.activation(rw["rw_a"][:, j, :], psum[:, 4 + j, :], ACT.Sigmoid, bias=core.param("a0", j))\
                    .then_inc(s_["a_made"], 1)

        @block.vector
        def _(dve):
            nc.vector.tensor_scalar(one_minus[:, :], core.params[:, ds(PARAM_AT["mu_rwkv"], 14)], -1.0, 1.0,
                                    ALU.mult, ALU.add).then_inc(s_["one_minus_made"], 1)
            dve.wait_ge(s_["one_minus_made"], 1)

            def shift(out, p, before, weight, sem):
                nc.vector.tensor_scalar(out[:, :, 0:1], p[:, :, 0:1], weight, None, ALU.mult)
                nc.vector.scalar_tensor_tensor(out[:, :, 1:], p[:, :, 1:], weight, before[:, :, 0:S - 1],
                                               ALU.mult, ALU.add).then_inc(sem, 1)

            shifted = core.sem("rw_rk_shifted")
            for j, u, c in turns_of(dve, st):
                core.split_chunk(dve, c.next())
                for g, name in enumerate(("rw_r", "rw_k", "rw_v")):
                    if g == 2:
                        core.split_chunk(dve, c.next(2))
                    dve.wait_ge(s_["scaled_made"], 3 * j + g + 1)
                    shift(rw[name][:, one(j), :], psum[:, one(3 * u + g), :], scaled[:, one(3 * u + g), :],
                          one_minus[:, ds(j + g * KW, 1)], evac if g == 2 else shifted)
            core.split_chunk(dve, Chunk(st_l.base + 1))
            for g in range(2):
                dve.wait_ge(s_["scaled_made"], 3 * KW + g + 1)
                shift(low[:, g:g + 1, :], psum[:, 6 + g:7 + g, :], scaled[:, g:g + 1, :], one_minus[:, 12 + g:13 + g],
                      s_["low_shifted"])
            dve.wait_ge(s_["decay_sigmoid"], KW)
            nc.vector.tensor_scalar(rw["rw_decay"][ALL], rw["rw_decay"][ALL], -DECAY_SCALE, None, ALU.mult)\
                .then_inc(s_["decay_made"], 1)
            for j in range(KW):
                dve.wait_ge(s_["low_products"], KW + j + 1)
                nc.vector.tensor_copy(rw["rw_g"][:, j, :], psum[:, j, :]).then_inc(s_["g_kept"], 1)



class Chain:

    def __init__(self, core, engine, name):
        self.engine, self.counted = engine, core.signals[name]

    def __call__(self, instruction):
        instruction.then_inc(self.counted.sem, 1)
        self.engine.wait_ge(self.counted.sem, self.counted.take(1) + 1)


def rwkv_prepare(core):
    core.next_phase()
    nc, psum, rw = core.nc, core.psum, core.rw
    r, k_, v, lw, a = (rw[n] for n in ("rw_r", "rw_k", "rw_v", "rw_decay", "rw_a"))
    kk, e_plus, e_minus, bonus = core.kk, core.e_plus, core.e_minus, core.bonus
    with nc.Block() as block:
        names = ("kk_raw", "kk_squares", "kk_sums", "kk_inverse", "kk_rstd", "bonus_terms", "bonus_sums",
                 "centred", "before_centred", "exps_made", "middle_made", "growth_made")
        s_ = {n: core.sem("rp_" + n) for n in names}
        by_chunk = lambda t: t[:, :, :].rearrange("p j (c t) -> p j c t", c=SB)

        @block.tensor
        def _(pe):
            pe.wait_ge(s_["kk_squares"], 1)
            for j in range(KW):
                last = nc.tensor.matmul(psum[:, j, :], core.pair_ones[:, :], e_plus[:, j, :], start=True, stop=True)
            last.then_inc(s_["kk_sums"], 1)
            pe.wait_ge(s_["bonus_terms"], KW)
            for j in range(KW):
                last = nc.tensor.matmul(psum[:, 4 + j, :], core.pair_ones[:, :], e_plus[:, j, :], start=True, stop=True)
            last.then_inc(s_["bonus_sums"], 1)

        @block.scalar
        def _(act):
            act.wait_ge(s_["kk_raw"], KW)
            nc.scalar.activation(e_plus[ALL], kk[ALL], ACT.Square).then_inc(s_["kk_squares"], 1)
            act.wait_ge(s_["kk_inverse"], 1)
            nc.scalar.activation(e_plus[ALL], e_plus[ALL], ACT.Sqrt).then_inc(s_["kk_rstd"], 1)
            act.wait_ge(s_["before_centred"], 1)
            nc.scalar.activation(e_plus[ALL], e_minus[ALL], ACT.Exp).then_inc(s_["exps_made"], 1)
            act.wait_ge(s_["exps_made"], 1)
            nc.scalar.activation(e_minus[ALL], e_minus[ALL], ACT.Exp, scale=-1.0).then_inc(s_["exps_made"], 1)
            nc.scalar.activation(lw[ALL], lw[ALL], ACT.Exp).then_inc(s_["exps_made"], 1)
            act.wait_ge(s_["middle_made"], 1)
            nc.scalar.activation(core.growth[ALL], core.growth[ALL], ACT.Exp).then_inc(s_["growth_made"], 1)

        @block.vector
        def _(dve):
            V = nc.vector
            chain = Chain(core, dve, "dve_chain")
            for j in range(KW):
                V.tensor_scalar(kk[:, j, :], k_[:, j, :], core.param("k_k", j), None, ALU.mult)\
                    .then_inc(s_["kk_raw"], 1)
            dve.wait_ge(s_["kk_sums"], 1)
            chain(V.tensor_scalar(e_plus[ALL], psum[:, 0:KW, :], 1e-24, None, ALU.max))
            V.reciprocal(e_plus[ALL], e_plus[ALL]).then_inc(s_["kk_inverse"], 1)
            dve.wait_ge(s_["kk_rstd"], 1)
            chain(V.tensor_tensor(kk[ALL], kk[ALL], e_plus[ALL], ALU.mult))
            chain(V.tensor_scalar(core.k_a_less_1[:, :], core.params[:, ds(PARAM_AT["k_a"], KW)], -1.0, None, ALU.add))
            for j in range(KW):
                chain(V.tensor_scalar(e_minus[:, j, :], a[:, j, :], core.param("k_a", j), core.k_a_less_1[:, j:j + 1],
                                      ALU.mult, ALU.subtract))
            chain(V.tensor_tensor(k_[ALL], k_[ALL], e_minus[ALL], ALU.mult))
            chain(V.tensor_tensor(a[ALL], a[ALL], kk[ALL], ALU.mult))
            for j in range(KW):
                V.scalar_tensor_tensor(e_plus[:, j, :], r[:, j, :], core.param("r_k", j), k_[:, j, :],
                                       ALU.mult, ALU.mult).then_inc(s_["bonus_terms"], 1)
            for j in range(KW):
                for c in range(SB):
                    part = slice(c * P, (c + 1) * P)
                    chain(V.tensor_tensor_scan(e_minus[:, j, part], core.ones[:, :], lw[:, j, part], 0.0,
                                               ALU.mult, ALU.add))
            dve.wait_ge(s_["bonus_sums"], 1)
            chain(V.tensor_tensor(bonus[ALL], v[ALL], psum[:, KW:2 * KW, :], ALU.mult))
            ends = by_chunk(e_minus)[:, :, :, P - 1:P].rearrange("p j c o -> p j (c o)")
            chain(V.tensor_scalar(core.middle[ALL], ends, 0.5, None, ALU.mult))
            middle = core.middle[:, :, :].unsqueeze(3).broadcast_to([P, KW, SB, P])
            V.tensor_tensor(by_chunk(e_minus), by_chunk(e_minus), middle, ALU.subtract).then_inc(s_["centred"], 1)
            dve.wait_ge(s_["centred"], 1)
            V.tensor_tensor(lw[ALL], e_minus[ALL], lw[ALL], ALU.subtract).then_inc(s_["before_centred"], 1)
            chain(V.tensor_copy(core.growth[ALL], core.middle[ALL]))
            V.tensor_tensor(core.growth[:, :, 0:SB - 1], core.middle[:, :, 0:SB - 1], core.middle[:, :, 1:SB], ALU.add)\
                .then_inc(s_["middle_made"], 1)


def rwkv_recurrence(core):
    core.next_phase()
    nc, psum, rw = core.nc, core.psum, core.rw
    r, k_, v, e_before, b_ = (rw[n] for n in ("rw_r", "rw_k", "rw_v", "rw_decay", "rw_a"))
    kk, e_plus, e_minus = core.kk, core.e_plus, core.e_minus
    mm = nc.tensor.matmul
    masks = core.level_masks
    with ExitStack() as scope, nc.Block() as block:
        sb = lambda name, shape, dt=F32: scope.enter_context(nc.sbuf_tensor(name, shape, dt))
        kr = sb("rc_kr", [P, KW, 2, P])
        bh, kh, vc = sb("rc_bh", [P, KW, P]), sb("rc_kh", [P, KW, P]), sb("rc_v", [P, KW, P])
        rows_ = sb("rc_rows", [P, 3, W])
        scores = sb("rc_scores", [P, 2, KW, 4, P])
        x, xt, nx = sb("rc_x", [P, 2, KW, P]), sb("rc_xt", [P, 2, KW, P]), sb("rc_nx", [P, 2, KW, P])
        rhs, u_, state = sb("rc_rhs", [P, 2, KW, 64]), sb("rc_u", [P, 2, KW, 64]), sb("rc_state", [P, KW, 64])
        names = ("staged", "v_staged", "turned", "rows_kept", "scored", "score_kept", "x_set", "x_made", "nx_made",
                 "nx_kept", "q_made", "rhs_made", "rhs_kept", "u_made", "u_kept", "o_made", "s_made", "o_kept",
                 "s_sum", "s_kept")
        s_ = {n: core.sem("rc_" + n) for n in names}
        half = (slice(0, 64), slice(64, 128))
        L1 = LEVELS - 1

        @block.tensor
        def _(pe):
            with pe.Fori(0, SB) as i:
                pe.wait_ge(s_["staged"], i + 1)
                pe.wait_ge(s_["v_staged"], i + 1)
                for n, t in enumerate((bh, kh, vc)):
                    for j in range(KW):
                        last = nc.tensor.transpose(psum[:, n, j * P:(j + 1) * P], t[:, j, :], core.ident[:, :])
                last.then_inc(s_["turned"], 1)
                for e in range(2):
                    if e:
                        pe.wait_ge(s_["score_kept"], 2 * i + 1)
                        pe.wait_ge(s_["rows_kept"], i + 1)
                    for j in range(KW):
                        both = kr[half[e], j, :, :].rearrange("p a t -> p (a t)")
                        mm(psum[:, 3 + j, 0:256], bh[half[e], j, :], both, start=True, stop=True)
                        mm(psum[:, 3 + j, 256:512], kh[half[e], j, :], both, start=True, stop=True)
                        last = mm(psum[:, (7, 2)[e], j * P:(j + 1) * P], kr[half[e], j, 0, :], bh[half[e], j, :],
                                  start=True, stop=True)
                    last.then_inc(s_["scored"], 1)
                for level in range(1, LEVELS):
                    n = 2 * (level - 1)
                    for e in range(2):
                        pe.wait_ge(s_["x_made"], i * 2 * LEVELS + (n + e + 1))
                        for j in range(KW):
                            last = mm(psum[:, 3 * e, j * P:(j + 1) * P], scores[:, e, j, 0, :], x[:, e, j, :],
                                      start=True, stop=True)
                        last.then_inc(s_["nx_made"], 1)
                    for e in range(2):
                        pe.wait_ge(s_["nx_kept"], i * 2 * L1 + (n + e + 1))
                        for j in range(KW):
                            part = slice(j * P, (j + 1) * P)
                            if level < L1:
                                mm(psum[:, 3 * e + 1, part], xt[:, e, j, :], nx[:, e, j, :], start=True, stop=True)
                            last = mm(psum[:, 3 * e + 2, part], nx[:, e, j, :], xt[:, e, j, :], start=True, stop=True)
                        last.then_inc(s_["q_made"], 1)
                pe.wait_ge(s_["s_kept"], i + 1)
                pe.wait_ge(s_["score_kept"], 2 * i + 2)
                for e in range(2):
                    for j in range(KW):
                        out = psum[:, 6 + e, j * 64:(j + 1) * 64]
                        vj = rows_[:, 2, j * P + 64 * e:j * P + 64 * e + 64]
                        mm(out, kr[half[e], j, 0, :], state[half[e], j, :], start=True, stop=False)
                        last = mm(out, scores[:, e, j, 2, :], vj, start=False, stop=True)
                last.then_inc(s_["rhs_made"], 1)
                pe.wait_ge(s_["x_made"], i * 2 * LEVELS + 2 * LEVELS)
                pe.wait_ge(s_["rhs_kept"], i + 1)
                for e in range(2):
                    for j in range(KW):
                        last = mm(psum[:, e, j * 64:(j + 1) * 64], xt[:, e, j, :], rhs[:, e, j, :], start=True, stop=True)
                last.then_inc(s_["u_made"], 1)
                wait_alone(pe, s_["u_kept"], i + 1)
                for e in range(2):
                    for j in range(KW):
                        out = psum[half[e], 2 + e, j * P:(j + 1) * P]
                        vj = rows_[:, 2, j * P + 64 * e:j * P + 64 * e + 64]
                        mm(out, state[half[e], j, :], kr[half[e], j, 1, :], start=True, stop=False)
                        mm(out, u_[:, e, j, :], scores[:, e, j, 1, :], start=False, stop=False)
                        last = mm(out, vj, scores[:, e, j, 3, :], start=False, stop=True)
                last.then_inc(s_["o_made"], 1)
                for e in range(2):
                    for j in range(KW):
                        out = psum[half[e], 4 + e, j * 64:(j + 1) * 64]
                        at = slice(j * P + 64 * e, j * P + 64 * e + 64)
                        mm(out, rows_[:, 0, at], u_[:, e, j, :], start=True, stop=False)
                        last = mm(out, rows_[:, 1, at], rows_[:, 2, at], start=False, stop=True)
                last.then_inc(s_["s_made"], 1)

        @block.scalar
        def _(act):
            A = nc.scalar.activation
            ident8 = core.ident[:, :].unsqueeze(1).broadcast_to([P, 2 * KW, P])
            with act.Fori(0, SB) as i:
                A(vc[ALL], v[:, :, ds(i * P, P)], ACT.Copy).then_inc(s_["v_staged"], 1)
                A(x[:, :, :, :].rearrange("p e j t -> p (e j) t"), ident8, ACT.Copy)
                A(xt[:, :, :, :].rearrange("p e j t -> p (e j) t"), ident8, ACT.Copy).then_inc(s_["x_set"], 1)
                act.wait_ge(s_["turned"], i + 1)
                A(rows_[ALL], psum[:, 0:3, :], ACT.Copy).then_inc(s_["rows_kept"], 1)
                for n in range(2 * L1):
                    act.wait_ge(s_["nx_made"], i * 2 * L1 + (n + 1))
                    A(nx[:, n % 2, :, :].rearrange("p j t -> p (j t)"), psum[:, 3 * (n % 2), :], ACT.Copy)\
                        .then_inc(s_["nx_kept"], 1)
                act.wait_ge(s_["rhs_made"], i + 1)
                A(rhs[:, :, :, :].rearrange("p e j d -> p e (j d)"), psum[:, 6:8, 0:256], ACT.Copy)\
                    .then_inc(s_["rhs_kept"], 1)
                act.wait_ge(s_["u_made"], i + 1)
                A(u_[:, :, :, :].rearrange("p e j d -> p e (j d)"), psum[:, 0:2, 0:256], ACT.Copy)\
                    .then_inc(s_["u_kept"], 1)
                act.wait_ge(s_["o_made"], i + 1)
                for e in range(2):
                    A(core.o_t[half[e], :, ds(i * P, P)],
                      psum[half[e], 2 + e, :].rearrange("p (j t) -> p j t", j=KW), ACT.Copy).then_inc(s_["o_kept"], 1)

        @block.vector
        def _(dve):
            V = nc.vector
            V.memset(state[ALL], 0.0).then_inc(s_["s_kept"], 1)
            spread = lambda m, n: m.unsqueeze(1).broadcast_to([P, n, P])
            with dve.Fori(0, SB) as i:
                now = (slice(None), slice(None), ds(i * P, P))
                V.scalar_tensor_tensor(kr[:, :, 0, :], kk[now], -1.0, e_before[now], ALU.mult, ALU.mult)
                V.tensor_tensor(kr[:, :, 1, :], r[now], e_plus[now], ALU.mult)
                V.tensor_tensor(bh[ALL], b_[now], e_minus[now], ALU.mult)
                V.tensor_tensor(kh[ALL], k_[now], e_minus[now], ALU.mult).then_inc(s_["staged"], 1)
                for e in range(2):
                    dve.wait_ge(s_["scored"], 2 * i + (e + 1))
                    for kind, mask in ((0, core.strict), (1, core.upper)):
                        for part in (kind, kind + 2):
                            last = V.tensor_tensor(scores[:, e, :, part, :], psum[:, 3:7, part * P:(part + 1) * P],
                                                   spread(mask[:, :], KW), ALU.mult)
                    last.then_inc(s_["score_kept"], 1)
                    wait_alone(dve, s_["x_set"], i + 1)
                    dve.wait_ge(s_["score_kept"], 2 * i + (e + 1))
                    V.copy_predicated(x[:, e, :, :], spread(masks[:, 0, 0, :], KW).bitcast(I32),
                                      psum[:, (7, 2)[e], :].rearrange("p (j t) -> p j t", j=KW))
                    V.copy_predicated(xt[:, e, :, :], spread(masks[:, 1, 0, :], KW).bitcast(I32),
                                      scores[:, e, :, 0, :]).then_inc(s_["x_made"], 1)
                for level in range(1, LEVELS):
                    for e in range(2):
                        wait_alone(dve, s_["q_made"], i * 2 * L1 + (2 * (level - 1) + e + 1))
                        if level < L1:
                            V.copy_predicated(x[:, e, :, :], spread(masks[:, 0, level, :], KW).bitcast(I32),
                                              psum[:, 3 * e + 1, :].rearrange("p (j t) -> p j t", j=KW))
                        V.copy_predicated(xt[:, e, :, :], spread(masks[:, 1, level, :], KW).bitcast(I32),
                                          psum[:, 3 * e + 2, :].rearrange("p (j t) -> p j t", j=KW))\
                            .then_inc(s_["x_made"], 1)
                dve.wait_ge(s_["s_made"], i + 1)
                for e in range(2):
                    V.tensor_tensor(state[half[e], :, :], state[half[e], :, :],
                                    psum[half[e], 4 + e, 0:256].rearrange("p (j d) -> p j d", j=KW), ALU.add)\
                        .then_inc(s_["s_sum"], 1)
                dve.wait_ge(s_["s_sum"], 2 * i + 2)
                V.tensor_tensor(state[ALL], state[ALL], core.growth[:, :, ds(i, 1)].broadcast_to([P, KW, 64]),
                                ALU.mult).then_inc(s_["s_kept"], 1)


def rwkv_finish(core):
    core.next_phase()
    nc, psum, o = core.nc, core.psum, core.o_t
    squares, rstd = core.e_plus, core.e_minus
    with ExitStack() as scope, nc.Block() as block:
        y_hi = scope.enter_context(nc.sbuf_tensor("rw_y_hi", [P, KW, S], F32R))
        y_lo = scope.enter_context(nc.sbuf_tensor("rw_y_lo", [P, KW, S], F32R))
        names = ("sums", "centred", "squares", "square_sums", "inverse", "rstd", "y_made", "y_hi_made", "y_split", "y_stored")
        s_ = {n: core.sem("rf_" + n) for n in names}

        @block.sync
        def _(sp):
            sp.wait_ge(s_["y_split"], 1)
            store_split(core, sp, KW, 2 * KW, (y_hi, y_lo), s_["y_stored"])
            sp.wait_ge(s_["y_stored"], 32)

        @block.tensor
        def _(pe):
            for j in range(KW):
                last = nc.tensor.matmul(psum[:, j, :], core.pair_ones[:, :], o[:, j, :], start=True, stop=True)
            last.then_inc(s_["sums"], 1)
            pe.wait_ge(s_["squares"], 1)
            for j in range(KW):
                last = nc.tensor.matmul(psum[:, 4 + j, :], core.pair_ones[:, :], squares[:, j, :], start=True, stop=True)
            last.then_inc(s_["square_sums"], 1)

        @block.scalar
        def _(act):
            act.wait_ge(s_["centred"], 1)
            nc.scalar.activation(squares[ALL], o[ALL], ACT.Square).then_inc(s_["squares"], 1)
            act.wait_ge(s_["inverse"], 1)
            nc.scalar.activation(rstd[ALL], rstd[ALL], ACT.Sqrt).then_inc(s_["rstd"], 1)
            act.wait_ge(s_["y_made"], 1)
            nc.scalar.activation(y_hi[ALL], o[ALL], ACT.Copy).then_inc(s_["y_hi_made"], 1)

        @block.vector
        def _(dve):
            V = nc.vector
            chain = Chain(core, dve, "dve_chain")
            dve.wait_ge(s_["sums"], 1)
            V.scalar_tensor_tensor(o[ALL], psum[:, 0:KW, :], -1.0 / 64, o[ALL], ALU.mult, ALU.add)\
                .then_inc(s_["centred"], 1)
            dve.wait_ge(s_["square_sums"], 1)
            chain(V.tensor_scalar(rstd[ALL], psum[:, KW:2 * KW, :], 1.0 / 64, GN_EPS, ALU.mult, ALU.add))
            V.reciprocal(rstd[ALL], rstd[ALL]).then_inc(s_["inverse"], 1)
            dve.wait_ge(s_["rstd"], 1)
            chain(V.tensor_tensor(o[ALL], o[ALL], rstd[ALL], ALU.mult))
            for j in range(KW):
                chain(V.tensor_scalar(o[:, j, :], o[:, j, :], core.param("lnx_w", j), core.param("lnx_b", j),
                                      ALU.mult, ALU.add))
            chain(V.tensor_tensor(o[ALL], o[ALL], core.bonus[ALL], ALU.add))
            V.tensor_tensor(o[ALL], o[ALL], core.rw["rw_g"][ALL], ALU.mult).then_inc(s_["y_made"], 1)
            dve.wait_ge(s_["y_hi_made"], 1)
            V.tensor_tensor(y_lo[ALL], o[ALL], y_hi[ALL].bitcast(F32), ALU.subtract).then_inc(s_["y_split"], 1)



def gate_and_merge(core):
    core.next_phase()
    nc, psum, st = core.nc, core.psum, core.st["gates"]
    with ExitStack() as scope, nc.Block() as block:
        sb = lambda name, shape, dt=F32: scope.enter_context(nc.sbuf_tensor(name, shape, dt))
        x = [sb("g_x_hi", [P, KD, S], F32R), sb("g_x_lo", [P, KD, S], F32R)]
        y = [sb("g_y_hi", [P, 3 * KW, S], F32R), sb("g_y_lo", [P, 3 * KW, S], F32R)]
        gate = sb("g_gate", [P, 3, S])
        total = sb("g_total", [P, S])
        names = ("x_loaded", "y_loaded", "h_loaded", "gates_mapped", "gate_read", "weighted", "added", "hi_made", "split")
        s_ = {n: core.sem("g_" + n) for n in names}
        done = core.chunk_done
        evac, evac0 = core.signals["dve_evac"].sem, core.signals["dve_evac"].take(KD)

        @block.sync
        def _(sp):
            for u in range(2):
                sp.dma_start(x[u][ALL].bitcast(F32), core.x_dram[u].rearrange("p (k s) -> p k s", k=KD))\
                    .then_inc(s_["x_loaded"], 16)
            for u in range(2):
                sp.dma_start(y[u][ALL].bitcast(F32), core.y_dram[u].rearrange("p (k s) -> p k s", k=3 * KW))\
                    .then_inc(s_["y_loaded"], 16)
            sp.dma_start(core.h[ALL], core.h_dram.rearrange("p (k s) -> p k s", k=KD)).then_inc(s_["h_loaded"], 16)
            load_stage(core, sp, st)
            sp.wait_ge(s_["h_loaded"], 16)

        @block.tensor
        def _(pe):
            pe.wait_ge(s_["x_loaded"], 32)
            pe.wait_ge(s_["y_loaded"], 32)
            for d, u, c in turns_of(pe, st):
                pe.wait_ge(core.w_split, c.number + 1)
                pe.wait_ge(evac, d + evac0)
                hi, lo = core.weights(c, 2, KD, P)
                for g in range(2):
                    for k in range(KD):
                        last = core.product(psum[:, g, :], (hi[:, g, k, :], lo[:, g, k, :]),
                                            (x[0][:, k, :], x[1][:, k, :]), k == 0, k == KD - 1)
                last.then_inc(done, 1)
                c = c.next()
                pe.wait_ge(core.w_split, c.number + 1)
                hi, lo = core.weights(c, KD, P)
                for k in range(KD):
                    last = core.product(psum[:, 2, :], (hi[:, k, :], lo[:, k, :]), (x[0][:, k, :], x[1][:, k, :]),
                                        k == 0, k == KD - 1)
                last.then_inc(done, 1)
                c = c.next()
                pe.wait_ge(core.w_split, c.number + 1)
                hi, lo = core.weights(c, 3, KW, P)
                for g in range(3):
                    for k in range(KW):
                        last = core.product(psum[:, 3 + g, :], (hi[:, g, k, :], lo[:, g, k, :]),
                                            (y[0][:, g * KW + k, :], y[1][:, g * KW + k, :]), k == 0, k == KW - 1)
                last.then_inc(done, 1)

        @block.scalar
        def _(act):
            nc.scalar.preload_act_table(ACT.Sigmoid)
            for d, u, c in turns_of(act, st):
                act.wait_ge(evac, d + evac0)
                for g in range(3):
                    if g != 1:
                        act.wait_ge(done, c.number + (1 if g == 0 else 2))
                    nc.scalar.activation(gate[:, g, :], psum[:, g, :], ACT.Sigmoid,
                                         bias=core.param("gate_b", d + g * KD)).then_inc(s_["gates_mapped"], 1)
                act.wait_ge(evac, d + (evac0 + 1))
                nc.scalar.activation(core.m_hi[:, one(d), :], total[:, :].unsqueeze(1), ACT.Copy).then_inc(s_["hi_made"], 1)

        @block.vector
        def _(dve):
            V = nc.vector
            for d, u, c in turns_of(dve, st):
                core.split_chunk(dve, c.next())
                core.split_chunk(dve, c.next(2))
                core.split_chunk(dve, c.next(3))
                dve.wait_ge(s_["gates_mapped"], 3 * d + 3)
                dve.wait_ge(done, c.number + 3)
                for g in range(3):
                    V.tensor_tensor(gate[:, g, :], gate[:, g, :], psum[:, 3 + g, :], ALU.mult).then_inc(s_["weighted"], 1)
                dve.wait_ge(s_["weighted"], 3 * d + 3)
                V.tensor_tensor(gate[:, 0, :], gate[:, 0, :], gate[:, 1, :], ALU.add).then_inc(s_["added"], 1)
                dve.wait_ge(s_["added"], d + 1)
                V.tensor_tensor(total[:, :], gate[:, 0, :], gate[:, 2, :], ALU.add).then_inc(evac, 1)
                dve.wait_ge(s_["hi_made"], d + 1)
                V.tensor_tensor(core.m_lo[:, one(d), :], total[:, :].unsqueeze(1), core.m_hi[:, one(d), :].bitcast(F32),
                                ALU.subtract).then_inc(s_["split"], 1)



def pe_tiles(core, pe, st, x, tiles=2, shape=None, k_tiles=KD, evac="dve_evac"):
    signal = core.signals[evac]
    base = signal.taken
    for s, u, c in turns_of(pe, st):
        pe.wait_ge(core.w_split, c.number + 1)
        pe.wait_ge(signal.sem, s + (base - 1))
        if shape == "gk":
            hi, lo = [w.rearrange("p g k m -> p k g m") for w in core.weights(c, tiles, k_tiles, P)]
        else:
            hi, lo = core.weights(c, k_tiles, tiles, P)
        for g in range(tiles):
            for k in range(k_tiles):
                last = core.product(core.psum[:, 2 * u + g, 0:x[0].shape[2]], (hi[:, k, g, :], lo[:, k, g, :]),
                                    (x[0][:, k, :], x[1][:, k, :]), k == 0, k == k_tiles - 1)
        last.then_inc(core.chunk_done, 1)


def add_to(core, dve, st, acc, tiles):
    signal = core.signals["dve_evac"]
    signal.take(st.steps)
    for s, u, c in turns_of(dve, st):
        core.split_chunk(dve, c.next())
        dve.wait_ge(core.chunk_done, c.number + 1)
        part = acc[:, ds(s * tiles, tiles), :]
        core.nc.vector.tensor_tensor(part, part, core.psum[:, 2 * u:2 * u + tiles, :], ALU.add).then_inc(signal.sem, 1)


def split_stage(core, dve, st):
    for s, u, c in turns_of(dve, st):
        core.split_chunk(dve, c.next())


def mix_out(core):
    core.next_phase()
    with core.nc.Block() as block:
        st = core.st["mix"]

        @block.sync
        def _(sp):
            load_stage(core, sp, st)

        @block.tensor
        def _(pe):
            pe_tiles(core, pe, st, (core.m_hi, core.m_lo))

        @block.vector
        def _(dve):
            add_to(core, dve, st, core.h, 2)



def memory_projections(core):
    core.next_phase()
    nc, psum = core.nc, core.psum
    st_q, st_k, st_v = (core.st[n] for n in ("ca_q", "ca_k", "ca_v"))
    with ExitStack() as scope, nc.Block() as block:
        sb = lambda name, shape, dt=F32: scope.enter_context(nc.sbuf_tensor(name, shape, dt))
        work, rstd = sb("cn_work", [P, KD, S]), sb("cn_rstd", [P, S])
        x = [sb("cn_x_hi", [P, KD, S], F32R), sb("cn_x_lo", [P, KD, S], F32R)]
        mx = [sb("cn_m_hi", [P, KD, MEM], F32R), sb("cn_m_lo", [P, KD, MEM], F32R)]
        rows, mem_t = sb("cn_mem_rows", [P, 2, D]), sb("cn_mem_t", [P, KD, MEM])
        mwork, mrstd = sb("cn_m_work", [P, KD, MEM]), sb("cn_m_rstd", [P, MEM])
        loaded, turned, kept, v_kept = (core.sem("cn_" + n) for n in ("loaded", "turned", "kept", "v_kept"))
        norm = Norm(core, core.h, work, rstd, "norm_ca", *x)
        norm_m = Norm(core, mem_t, mwork, mrstd, "norm_mem", *mx, width=MEM, bank=6)

        @block.sync
        def _(sp):
            sp.dma_start(rows[ALL], core.a["mem"][0].rearrange("(b p) d -> p b d", p=P)).then_inc(loaded, 16)
            for st in (st_q, st_k, st_v):
                load_stage(core, sp, st)

        @block.tensor
        def _(pe):
            norm.pe(pe)
            pe.wait_ge(loaded, 16)
            for k in range(KD):
                for b in range(2):
                    last = nc.tensor.transpose(psum[:, k // 2, k % 2 * MEM + b * P:k % 2 * MEM + (b + 1) * P],
                                               rows[:, b, k * P:(k + 1) * P], core.ident[:, :])
            last.then_inc(turned, 1)
            norm_m.pe(pe)
            pe.wait_ge(kept, 1)
            norm.ready(pe, KD - 1)
            pe_tiles(core, pe, st_q, x)
            core.signals["dve_evac"].taken += st_q.steps
            norm_m.ready(pe, KD - 1)
            pe_tiles(core, pe, st_k, mx)
            core.signals["dve_evac"].taken -= st_q.steps
            for s, u, c in turns_of(pe, st_v):
                pe.wait_ge(core.w_split, c.number + 1)
                pe.wait_ge(core.signals["act_evac"].sem, s + (core.signals["act_evac"].taken - 1))
                w = core.weights(c, KD, 256)
                for b in range(2):
                    for k in range(KD):
                        mb = [t[:, k, b * P:(b + 1) * P] for t in mx]
                        last = core.product(psum[:, 4 + u, b * 256:(b + 1) * 256], mb, (w[0][:, k, :], w[1][:, k, :]),
                                            k == 0, k == KD - 1)
                last.then_inc(core.chunk_done, 1)

        @block.scalar
        def _(act):
            norm.act(act)
            act.wait_ge(kept, 1)
            norm_m.act(act)
            signal = core.signals["act_evac"]
            signal.take(st_v.steps)
            for s, u, c in turns_of(act, st_v):
                act.wait_ge(core.chunk_done, c.number + 1)
                nc.scalar.activation(core.ca_v[:, :, ds(s * 256, 256)],
                                     psum[:, 4 + u, :].rearrange("p (b c) -> p b c", b=2), ACT.Copy)\
                    .then_inc(signal.sem, 1)

        @block.vector
        def _(dve):
            norm.dve(dve)
            dve.wait_ge(turned, 1)
            nc.vector.tensor_copy(mem_t[ALL], psum[:, 0:4, :].rearrange("p a (b c) -> p (a b) c", b=2)).then_inc(kept, 1)
            norm_m.dve(dve)
            signal = core.signals["dve_evac"]
            for st, out, scale in ((st_q, core.ca_q, 0.0625), (st_k, core.ca_k, 1.0)):
                signal.take(st.steps)
                for s, u, c in turns_of(dve, st):
                    core.split_chunk(dve, c.next())
                    dve.wait_ge(core.chunk_done, c.number + 1)
                    nc.vector.tensor_scalar(out[:, ds(2 * s, 2), :], psum[:, 2 * u:2 * u + 2, 0:out.shape[2]], scale,
                                            None, ALU.mult).then_inc(signal.sem, 1)
            split_stage(core, dve, st_v)


def memory_attention(core):
    core.next_phase()
    nc, psum = core.nc, core.psum
    heads = 4
    with ExitStack() as scope, nc.Block() as block:
        sb = lambda name, shape, dt=F32: scope.enter_context(nc.sbuf_tensor(name, shape, dt))
        prob = sb("ca_prob", [P, 2, SB, MEM])
        prob_t = sb("ca_prob_t", [P, 2, 2, S])
        out = sb("ca_out", [P, KD, S])
        top, total = sb("ca_top", [P, 2, SB]), sb("ca_total", [P, 2, SB])
        names = ("scored", "top_made", "exps", "inverse", "scaled", "turned", "turned_kept", "out_made", "out_kept",
                 "hi_made", "split")
        s_ = {n: core.sem("ca_" + n) for n in names}

        @block.tensor
        def _(pe):
            def scores(h):
                if h >= 2:
                    pe.wait_ge(s_["exps"], SB * (h - 1))
                for b in range(SB):
                    for k in range(2):
                        last = nc.tensor.matmul(psum[:, 2 * (h % 2) + b // 2, b % 2 * MEM:(b % 2 + 1) * MEM],
                                                core.ca_q[:, 2 * h + k, b * P:(b + 1) * P], core.ca_k[:, 2 * h + k, :],
                                                start=k == 0, stop=k == 1)
                last.then_inc(s_["scored"], 1)

            scores(0)
            for h in range(heads):
                if h + 1 < heads:
                    scores(h + 1)
                pe.wait_ge(s_["scaled"], SB * (h + 1))
                if h:
                    pe.wait_ge(s_["turned_kept"], 2 * h)
                for m in range(2):
                    for b in range(SB):
                        last = nc.tensor.transpose(psum[:, 4 + m, b * P:(b + 1) * P],
                                                   prob[:, h % 2, b, m * P:(m + 1) * P], core.ident[:, :])
                    last.then_inc(s_["turned"], 1)
                pe.wait_ge(s_["turned_kept"], 2 * h + 2)
                if h:
                    pe.wait_ge(s_["out_kept"], h)
                for d in range(2):
                    for m in range(2):
                        last = nc.tensor.matmul(psum[:, 6 + d, :], core.ca_v[:, m, (2 * h + d) * P:(2 * h + d + 1) * P],
                                                prob_t[:, h % 2, m, :], start=m == 0, stop=m == 1)
                last.then_inc(s_["out_made"], 1)

        @block.scalar
        def _(act):
            nc.scalar.preload_act_table(ACT.Exp)
            for h in range(heads):
                act.wait_ge(s_["top_made"], h + 1)
                if h >= 2:
                    act.wait_ge(s_["turned"], 2 * (h - 1))
                for b in range(SB):
                    nc.scalar.activation(prob[:, h % 2, b, :],
                                         psum[:, 2 * (h % 2) + b // 2, b % 2 * MEM:(b % 2 + 1) * MEM], ACT.Exp,
                                         bias=top[:, h % 2, b:b + 1], accum_out=total[:, h % 2, b:b + 1])\
                        .then_inc(s_["exps"], 1)
                if h:
                    act.wait_ge(s_["out_made"], h)
                    nc.scalar.activation(out[:, 2 * h - 2:2 * h, :], psum[:, 6:8, :], ACT.Copy).then_inc(s_["out_kept"], 1)
            act.wait_ge(s_["out_made"], heads)
            nc.scalar.activation(out[:, 2 * heads - 2:2 * heads, :], psum[:, 6:8, :], ACT.Copy).then_inc(s_["out_kept"], 1)
            act.wait_ge(s_["out_kept"], heads)
            nc.scalar.activation(core.m_hi[ALL], out[ALL], ACT.Copy).then_inc(s_["hi_made"], 1)

        @block.vector
        def _(dve):
            V = nc.vector
            chain = Chain(core, dve, "dve_chain")

            def maxima(h):
                dve.wait_ge(s_["scored"], h + 1)
                if h >= 2:
                    dve.wait_ge(s_["exps"], SB * (h - 1))
                u = h % 2
                chain(V.tensor_reduce(top[:, u, :], psum[:, 2 * u:2 * u + 2, :].rearrange("p a (b c) -> p (a b) c", b=2),
                                      AX.X, ALU.max))
                V.tensor_scalar(top[:, u, :], top[:, u, :], -1.0, None, ALU.mult).then_inc(s_["top_made"], 1)

            maxima(0)
            for h in range(heads):
                if h + 1 < heads:
                    maxima(h + 1)
                u = h % 2
                dve.wait_ge(s_["exps"], SB * (h + 1))
                chain(V.reciprocal(total[:, u, :], total[:, u, :]))
                for b in range(SB):
                    V.tensor_scalar(prob[:, u, b, :], prob[:, u, b, :], total[:, u, b:b + 1], None, ALU.mult)\
                        .then_inc(s_["scaled"], 1)
                for m in range(2):
                    dve.wait_ge(s_["turned"], 2 * h + m + 1)
                    V.tensor_copy(prob_t[:, u, m, :], psum[:, 4 + m, :]).then_inc(s_["turned_kept"], 1)
            dve.wait_ge(s_["hi_made"], 1)
            V.tensor_tensor(core.m_lo[ALL], out[ALL], core.m_hi[ALL].bitcast(F32), ALU.subtract).then_inc(s_["split"], 1)


def memory_out(core):
    core.next_phase()
    with core.nc.Block() as block:
        st = core.st["ca_o"]

        @block.sync
        def _(sp):
            load_stage(core, sp, st)

        @block.tensor
        def _(pe):
            pe_tiles(core, pe, st, (core.m_hi, core.m_lo))

        @block.vector
        def _(dve):
            add_to(core, dve, st, core.h, 2)



def ffn(core):
    core.next_phase()
    nc, psum = core.nc, core.psum
    with ExitStack() as scope, nc.Block() as block:
        sb = lambda name, shape, dt=F32: scope.enter_context(nc.sbuf_tensor(name, shape, dt))
        work, rstd = sb("fn_work", [P, KD, S]), sb("fn_rstd", [P, S])
        x = [sb("fn_x_hi", [P, KD, S], F32R), sb("fn_x_lo", [P, KD, S], F32R)]
        hid = [sb("fn_hid_hi", [P, HF, S], F32R), sb("fn_hid_lo", [P, HF, S], F32R)]
        taps, hidden = sb("fn_taps", [P, 2, 2, S]), sb("fn_hidden", [P, 2, S])
        names = ("first_taps", "second_taps", "third_taps", "silu", "hidden_made", "hi_made", "split")
        s_ = {n: core.sem("fn_" + n) for n in names}
        norm = Norm(core, core.h, work, rstd, "norm_ffn", *x)
        evac = core.signals["dve_evac"]
        done = core.chunk_done

        @block.sync
        def _(sp):
            for h in range(2):
                load_stage(core, sp, core.st[f"ffn_up{h}"])
                load_stage(core, sp, core.st[f"ffn_down{h}"])

        @block.tensor
        def _(pe):
            norm.pe(pe)
            norm.ready(pe, KD - 1)
            before = evac.taken
            for h in range(2):
                pe_tiles(core, pe, core.st[f"ffn_up{h}"], x, shape="gk")
                evac.taken += HF
                pe.wait_ge(s_["split"], HF * (h + 1))
                pe_tiles(core, pe, core.st[f"ffn_down{h}"], hid, tiles=1, k_tiles=HF)
                evac.taken += KD
            evac.taken = before

        @block.scalar
        def _(act):
            norm.act(act)
            for h in range(2):
                st = core.st[f"ffn_up{h}"]
                for j, u, c in turns_of(act, st):
                    act.wait_ge(done, c.number + 1)
                    for g in range(2):
                        at = j + (g * 2 * HF + h * HF)
                        nc.scalar.activation(taps[:, u, g, :], psum[:, 2 * u + g, :], ACT.Identity,
                                             scale=core.param("ffn_conv_w", at + 4 * 2 * HF),
                                             bias=core.param("ffn_conv_b", at)).then_inc(s_["first_taps"], 1)
                    act.wait_ge(s_["third_taps"], 2 * j + (2 * HF * h + 1))
                    nc.scalar.activation(taps[:, u, 0, :], taps[:, u, 0, :], ACT.Silu).then_inc(s_["silu"], 1)
                    act.wait_ge(s_["hidden_made"], j + (HF * h + 1))
                    nc.scalar.activation(hid[0][:, one(j), :], hidden[:, one(u), :], ACT.Copy).then_inc(s_["hi_made"], 1)

        @block.vector
        def _(dve):
            V = nc.vector
            norm.dve(dve)
            for h in range(2):
                st = core.st[f"ffn_up{h}"]
                base = evac.take(HF)
                for j, u, c in turns_of(dve, st):
                    core.split_chunk(dve, c.next())
                    for g in range(2):
                        at = j + (g * 2 * HF + h * HF)
                        n = 2 * j + (2 * HF * h + g + 1)
                        dve.wait_ge(s_["first_taps"], n)
                        V.scalar_tensor_tensor(taps[:, u, g, 1:], psum[:, 2 * u + g, 0:S - 1],
                                               core.param("ffn_conv_w", at + 2 * 2 * HF), taps[:, u, g, 1:],
                                               ALU.mult, ALU.add).then_inc(s_["second_taps"], 1)
                        dve.wait_ge(s_["second_taps"], n)
                        V.scalar_tensor_tensor(taps[:, u, g, 2:], psum[:, 2 * u + g, 0:S - 2],
                                               core.param("ffn_conv_w", at), taps[:, u, g, 2:],
                                               ALU.mult, ALU.add).then_inc(s_["third_taps"], 1)
                    dve.wait_ge(s_["third_taps"], 2 * j + (2 * HF * h + 2))
                    dve.wait_ge(s_["silu"], j + (HF * h + 1))
                    V.tensor_tensor(hidden[:, u, :], taps[:, u, 0, :], taps[:, u, 1, :], ALU.mult)\
                        .then_inc(s_["hidden_made"], 1)
                    dve.wait_ge(s_["hi_made"], j + (HF * h + 1))
                    V.tensor_tensor(hid[1][:, one(j), :], hidden[:, one(u), :], hid[0][:, one(j), :].bitcast(F32),
                                    ALU.subtract).then_inc(s_["split"], 1)
                    dve.wait_ge(s_["split"], j + (HF * h + 1))
                    V.memset(core.scrap[:, 0:1], 0.0).then_inc(evac.sem, 1)
                add_to(core, dve, core.st[f"ffn_down{h}"], core.h, 1)



HEADS2, WIDE = 16, 3 * P


def input_projections(core):
    core.next_phase()
    nc, psum = core.nc, core.psum
    st_x, st_z, st_q, st_r = (core.st[n] for n in ("xbc", "z", "q2", "kvdt"))
    with ExitStack() as scope, nc.Block() as block:
        sb = lambda name, shape, dt=F32: scope.enter_context(nc.sbuf_tensor(name, shape, dt))
        work, rstd = sb("in_work", [P, KD, S]), sb("in_rstd", [P, S])
        x = [sb("in_x_hi", [P, KD, S], F32R), sb("in_x_lo", [P, KD, S], F32R)]
        k_t, skip_all = sb("in_k", [P, 2, S]), sb("in_skip_all", [P, HEADS2])
        final = Norm(core, core.h, work, rstd, "norm_final", dest=core.h)
        norm = Norm(core, core.h, work, rstd, "norm_mix_pre_2", *x)
        conv = work
        offsets = core.offsets
        names = ("tap_2", "taps", "xbc_made", "rest_kept", "k_placed", "offsets_made", "bias_made", "bias_masked",
                 "slopes_made", "broadcast")
        s_ = {n: core.sem("in_" + n) for n in names}
        done = core.chunk_done
        dsig, asig = core.signals["dve_evac"], core.signals["act_evac"]

        @block.sync
        def _(sp):
            sp.dma_start(core.dt_bias[:, :], core.a["dt_bias_2"].rearrange("a b c -> a (b c)")[0].partition_broadcast(P))\
                .then_inc(s_["broadcast"], 16)
            sp.dma_start(core.a_log[:, :], core.a["a_log_2"].rearrange("a b c -> a (b c)")[0].partition_broadcast(P))\
                .then_inc(s_["broadcast"], 16)
            sp.dma_start(core.sink[:, :], core.a["attn_sink_2"][0].partition_broadcast(P)).then_inc(s_["broadcast"], 16)
            sp.dma_start(skip_all[:, :], core.a["d_skip_2"][0].partition_broadcast(P)).then_inc(s_["broadcast"], 16)
            for st in (st_x, st_z, st_q, st_r):
                load_stage(core, sp, st)
            sp.wait_ge(s_["rest_kept"], 1)
            for g in range(4):
                for e in range(2):
                    sp.dma_start(core.k2[64 * e:64 * e + 64, g, :], k_t[64 * (g % 2):64 * (g % 2) + 64, g // 2, :])\
                        .then_inc(s_["k_placed"], 16)
            sp.wait_ge(s_["k_placed"], 128)

        @block.gpsimd
        def _(pool):
            nc.gpsimd.iota(offsets[:, :], pattern=[[1, WIDE]], base=-P, channel_multiplier=-1)\
                .then_inc(s_["offsets_made"], 1)
            for h in range(HEADS2):
                nc.gpsimd.memset(core.slopes[:, h:h + 1], float(2.0 ** (-8.0 * (h + 1) / HEADS2)))\
                    .then_inc(s_["slopes_made"], 1)
            pool.wait_ge(s_["bias_made"], 1)
            nc.gpsimd.affine_select(out=core.distance[:, :], in_=core.distance[:, :], compare_op=ALU.is_ge, fill=-1e30,
                                    base=0, pattern=[[1, WIDE]], channel_multiplier=-1).then_inc(s_["bias_masked"], 1)
            pool.wait_ge(s_["bias_masked"], 1)
            nc.gpsimd.affine_select(out=core.distance[:, :], in_=core.distance[:, :], compare_op=ALU.is_ge, fill=-1e30,
                                    base=2 * P, pattern=[[-1, WIDE]], channel_multiplier=1)\
                .then_inc(s_["bias_masked"], 1)

        @block.tensor
        def _(pe):
            final.pe(pe)
            norm.pe(pe)
            norm.ready(pe, KD - 1)
            at = dsig.taken
            pe_tiles(core, pe, st_x, x)
            pe.wait_ge(dsig.sem, at + st_x.steps)
            pe_tiles(core, pe, st_z, x, evac="act_evac")
            pe.wait_ge(asig.sem, asig.taken + st_z.steps)
            dsig.taken += st_x.steps
            pe_tiles(core, pe, st_q, x)
            dsig.taken -= st_x.steps
            pe.wait_ge(dsig.sem, at + st_x.steps + st_q.steps)
            for s, u, c in turns_of(pe, st_r):
                pe.wait_ge(core.w_split, c.number + 1)
                w = core.weights(c, KD, *((2, P), (256,), (P,))[s])
                for g in range((2, SB, 1)[s]):
                    for k in range(KD):
                        xk = [t[:, k, :] for t in x]
                        if s == 0:
                            args = psum[:, g, :], [t[:, k, g, :] for t in w], xk
                        elif s == 1:
                            args = (psum[:, 2 + g // 2, g % 2 * 256:g % 2 * 256 + 256],
                                    [t[:, k, g * P:(g + 1) * P] for t in x], [t[:, k, :] for t in w])
                        else:
                            args = psum[:, 4, :], [t[:, k, :] for t in w], xk
                        last = core.product(*args, k == 0, k == KD - 1)
                last.then_inc(done, 1)

        @block.scalar
        def _(act):
            A = nc.scalar.activation
            final.act(act)
            act.wait_ge(core.signals["normed"].sem, final.normed + KD)
            norm.act(act)
            for s, u, c in turns_of(act, st_x):
                act.wait_ge(done, c.number + 1)
                for g in range(2):
                    at = 2 * s + g
                    A(conv[:, 2 * u + g, :], psum[:, 2 * u + g, :], ACT.Identity,
                      scale=core.param("conv_w_2", at + 2 * 12), bias=core.param("conv_b_2", at))\
                        .then_inc(s_["tap_2"], 1)
                for g in range(2):
                    act.wait_ge(s_["taps"], 8 * s + 4 * g + 4)
                    A(core.xbc[:, ds(2 * s + g, 1), :], conv[:, one(2 * u + g), :], ACT.Silu).then_inc(s_["xbc_made"], 1)
            asig.take(st_z.steps)
            for s, u, c in turns_of(act, st_z):
                act.wait_ge(done, c.number + 1)
                A(core.z[:, ds(2 * s, 2), :], psum[:, 2 * u:2 * u + 2, :], ACT.Silu).then_inc(asig.sem, 1)
            act.wait_ge(done, st_r.base + 1)
            A(k_t[ALL], psum[:, 0:2, :], ACT.Copy).then_inc(s_["rest_kept"], 1)
            act.wait_ge(done, st_r.base + 2)
            A(core.v2[ALL], psum[:, 2:4, :].rearrange("p a (b c) -> p (a b) c", b=2), ACT.Copy)\
                .then_inc(s_["rest_kept"], 1)
            act.wait_ge(done, st_r.base + 3)
            A(core.dt_t[:, :], psum[0:32, 4, :], ACT.Copy).then_inc(s_["rest_kept"], 1)

        @block.vector
        def _(dve):
            V = nc.vector
            chain = Chain(core, dve, "dve_chain")
            final.dve(dve)
            norm.dve(dve)
            dve.wait_ge(s_["offsets_made"], 1)
            chain(V.tensor_copy(core.distance[:, :], offsets[:, :]))
            V.scalar_tensor_tensor(core.distance[:, :], core.distance[:, :], -1.0, core.distance[:, :], ALU.mult, ALU.min)\
                .then_inc(s_["bias_made"], 1)
            dsig.take(st_x.steps)
            for s, u, c in turns_of(dve, st_x):
                core.split_chunk(dve, c.next())
                for g in range(2):
                    dve.wait_ge(s_["tap_2"], 2 * s + g + 1)
                    p, out = psum[:, 2 * u + g, :], conv[:, 2 * u + g, :]
                    for n, tap in enumerate((0, 1, 3, 4)):
                        lag = 2 - tap
                        dst, src = (out[:, lag:], p[:, 0:S - lag]) if lag > 0 else (out[:, 0:S + lag], p[:, -lag:])
                        V.scalar_tensor_tensor(dst, src, core.param("conv_w_2", 2 * s + (g + 12 * tap)), dst,
                                               ALU.mult, ALU.add).then_inc(s_["taps"], 1)
                        dve.wait_ge(s_["taps"], 8 * s + 4 * g + n + 1)
                V.memset(core.scrap[:, 0:1], 0.0).then_inc(dsig.sem, 1)
            split_stage(core, dve, st_z)
            dsig.take(st_q.steps)
            for s, u, c in turns_of(dve, st_q):
                core.split_chunk(dve, c.next())
                dve.wait_ge(done, c.number + 1)
                V.tensor_scalar(core.q2[:, ds(2 * s, 2), :], psum[:, 2 * u:2 * u + 2, :], 0.125, None, ALU.mult)\
                    .then_inc(dsig.sem, 1)
            split_stage(core, dve, st_r)
            dve.wait_ge(s_["broadcast"], 64)
            by_head = skip_all[:, :].rearrange("p (j e) -> p e j", e=2)
            for e in range(2):
                half = slice(64 * e, 64 * e + 64)
                V.tensor_copy(core.d_skip[half, :], by_head[half, e, :])



R2 = 2 * HEADS2


def ssd_prepare(core):
    core.next_phase()
    nc, psum = core.nc, core.psum
    with ExitStack() as scope, nc.Block() as block:
        sb = lambda name, shape, dt=F32: scope.enter_context(nc.sbuf_tensor(name, shape, dt))
        raw, soft, a_ = sb("sp_raw", [P, SB, R2]), sb("sp_soft", [P, SB, R2]), sb("sp_a", [P, SB, R2])
        names = ("turned", "biased", "abs", "exp", "log", "a_exp", "a_made", "sums", "sums_kept", "sums_turned",
                 "decay_arg", "decay_exp", "chunk_exp", "done")
        s_ = {n: core.sem("sp_" + n) for n in names}

        @block.tensor
        def _(pe):
            for c in range(SB):
                last = nc.tensor.transpose(psum[:, 0, c * R2:(c + 1) * R2], core.dt_t[:, c * P:(c + 1) * P],
                                           core.ident[0:R2, 0:R2])
            last.then_inc(s_["turned"], 1)
            pe.wait_ge(s_["a_made"], 1)
            mm = nc.tensor.matmul
            mm(psum[:, 1, 0:64], core.upper[:, :], a_[:, :, 0:HEADS2], start=True, stop=True)
            mm(psum[:, 1, 64:128], core.lower[:, :], a_[:, :, HEADS2:R2], start=True, stop=True)
            mm(psum[:, 1, 128:256], core.ones[:, :], a_[ALL], start=True, stop=True).then_inc(s_["sums"], 1)
            pe.wait_ge(s_["sums_kept"], 1)
            for c in range(SB):
                last = nc.tensor.transpose(psum[0:R2, 2, c * P:(c + 1) * P], core.sums[:, c, :], core.ident[:, :])
            last.then_inc(s_["sums_turned"], 1)

        @block.scalar
        def _(act):
            A = nc.scalar.activation
            A(core.a_log[:, :], core.a_log[:, :], ACT.Exp).then_inc(s_["a_exp"], 1)
            act.wait_ge(s_["biased"], 1)
            A(soft[ALL], raw[ALL], ACT.Abs).then_inc(s_["abs"], 1)
            act.wait_ge(s_["abs"], 1)
            A(soft[ALL], soft[ALL], ACT.Exp, scale=-1.0).then_inc(s_["exp"], 1)
            act.wait_ge(s_["exp"], 1)
            A(soft[ALL], soft[ALL], ACT.Ln, bias=1.0).then_inc(s_["log"], 1)
            act.wait_ge(s_["decay_arg"], 1)
            A(core.state_weight[ALL], core.state_weight[ALL], ACT.Exp).then_inc(s_["decay_exp"], 1)
            A(core.chunk_decay[ALL], core.chunk_decay[ALL], ACT.Exp).then_inc(s_["chunk_exp"], 1)
            act.wait_ge(s_["sums_turned"], 1)
            A(core.sums_t[:, :], psum[0:R2, 2, :], ACT.Copy).then_inc(s_["done"], 1)

        @block.vector
        def _(dve):
            V = nc.vector
            chain = Chain(core, dve, "dve_chain")
            dve.wait_ge(s_["turned"], 1)
            V.tensor_tensor(raw[ALL], psum[:, 0, 0:SB * R2].rearrange("p (c r) -> p c r", c=SB),
                            core.dt_bias[:, :].unsqueeze(1).broadcast_to([P, SB, R2]), ALU.add).then_inc(s_["biased"], 1)
            dve.wait_ge(s_["log"], 1)
            dve.wait_ge(s_["biased"], 1)
            chain(V.scalar_tensor_tensor(core.dt[ALL], raw[ALL], 0.0, soft[ALL], ALU.max, ALU.add))
            dve.wait_ge(s_["a_exp"], 1)
            V.scalar_tensor_tensor(a_[ALL], core.dt[ALL], -1.0, core.a_log[:, :].unsqueeze(1).broadcast_to([P, SB, R2]),
                                   ALU.mult, ALU.mult).then_inc(s_["a_made"], 1)
            dve.wait_ge(s_["sums"], 1)
            for part in range(2):
                last = V.tensor_copy(core.sums[:, :, part * HEADS2:(part + 1) * HEADS2],
                                     psum[:, 1, part * 64:part * 64 + 64].rearrange("p (c r) -> p c r", c=SB))
            last.then_inc(s_["sums_kept"], 1)
            chain(V.tensor_copy(core.chunk_decay[ALL], psum[:, 1, 128:256].rearrange("p (c r) -> p c r", c=SB)))
            dve.wait_ge(s_["sums_kept"], 1)
            V.tensor_tensor(core.state_weight[ALL], core.chunk_decay[ALL], core.sums[ALL], ALU.subtract)\
                .then_inc(s_["decay_arg"], 1)
            dve.wait_ge(s_["decay_exp"], 1)
            chain(V.tensor_tensor(core.state_weight[ALL], core.state_weight[ALL], core.dt[ALL], ALU.mult))


def ssd(core):
    core.next_phase()
    nc, psum, mm = core.nc, core.psum, core.nc.tensor.matmul
    with ExitStack() as scope, nc.Block() as block:
        sb = lambda name, shape, dt=F32: scope.enter_context(nc.sbuf_tensor(name, shape, dt))
        select = sb("ss_select", [R2, 2, 2, P])
        x_t, x_rows = sb("ss_x_t", [P, S]), sb("ss_x_rows", [P, SB, P])
        grown = sb("ss_grown", [P, 4, S])
        inner = sb("ss_inner", [P, 4, S])
        cb = sb("ss_cb", [P, 2, SB, P])
        b_rows = sb("ss_b_rows", [P, SB, P])
        x_weighed = sb("ss_x_weighed", [P, 2, SB, P])
        prev = sb("ss_prev", [P, 2, SB, P])
        y = sb("ss_y", [P, S])
        names = ("cb_made", "cb_kept", "b_kept", "staged", "spread", "x_turned", "x_kept", "grown_exp", "diffs",
                 "inner_exp", "grown_made", "weighed", "x_weighed", "states", "prev_steps", "prev_made",
                 "inner_made", "y_made", "y_sum", "y_kept", "cb_free")
        s_ = {n: core.sem("ss_" + n) for n in names}
        per_g = KD // 2

        @block.tensor
        def _(pe):
            for g in range(2):
                b_t, c_t = core.xbc[:, KD + g, :], core.xbc[:, KD + 2 + g, :]
                if g:
                    pe.wait_ge(s_["y_kept"], per_g + 1)
                for c in range(SB):
                    part = slice(c * P, (c + 1) * P)
                    mm(psum[:, 1, part], b_t[:, part], c_t[:, part], start=True, stop=True)
                    last = nc.tensor.transpose(psum[:, 2, part], b_t[:, part], core.ident[:, :])
                last.then_inc(s_["cb_made"], 1)
                with pe.Fori(0, per_g) as i:
                    n = lambda k, m=1: i * m + (k + g * per_g * m)
                    pe.wait_ge(s_["staged"], n(1))
                    pe.wait_ge(s_["cb_kept"], g + 1)
                    pe.wait_ge(s_["b_kept"], g + 1)
                    for q in range(4):
                        mm(psum[:, 1 + q, :], select[:, q // 2, q % 2, :], core.sums_t[:, :], start=True, stop=True)\
                            .then_inc(s_["spread"], 1)
                    for c in range(SB):
                        last = nc.tensor.transpose(psum[:, 0, c * P:(c + 1) * P], x_t[:, c * P:(c + 1) * P],
                                                   core.ident[:, :])
                    last.then_inc(s_["x_turned"], 1)
                    pe.wait_ge(s_["x_weighed"], n(2, 2))
                    for way in range(2):
                        for c in (range(0, SB - 1) if way == 0 else range(1, SB)):
                            last = mm(psum[:, 5 + way, c * P:(c + 1) * P], b_rows[:, c, :], x_weighed[:, way, c, :],
                                      start=True, stop=True)
                    last.then_inc(s_["states"], 1)
                    pe.wait_ge(s_["inner_made"], n(2, 2))
                    pe.wait_ge(s_["grown_made"], n(4, 4))
                    pe.wait_ge(s_["prev_made"], n(1))
                    for e in range(2):
                        rows = slice(64 * e, 64 * e + 64)
                        for c in range(SB):
                            out, part = psum[rows, 7, c * P:(c + 1) * P], slice(c * P, (c + 1) * P)
                            mm(out, x_rows[:, c, rows], inner[:, e, part], start=True, stop=False)
                            if c > 0:
                                last = mm(out, prev[:, 0, c, rows], grown[:, e, part], start=False, stop=c == SB - 1)
                            if c < SB - 1:
                                last = mm(out, prev[:, 1, c, rows], grown[:, 2 + e, part], start=False, stop=True)
                    last.then_inc(s_["y_made"], 1)

        @block.scalar
        def _(act):
            A = nc.scalar.activation
            for g in range(2):
                act.wait_ge(s_["cb_made"], g + 1)
                A(b_rows[ALL], psum[:, 2, :].rearrange("p (c n) -> p c n", c=SB), ACT.Copy).then_inc(s_["b_kept"], 1)
                with act.Fori(0, per_g) as i:
                    n = lambda k, m=1: i * m + (k + g * per_g * m)
                    act.wait_ge(s_["y_kept"], n(1))
                    for way in range(2):
                        A(select[:, way, :, :],
                          core.ident[0:R2, ds(2 * i + (8 * g + HEADS2 * way), 2)].unsqueeze(2).broadcast_to([R2, 2, P]),
                          ACT.Copy)
                    A(x_t[:, :].unsqueeze(1), core.xbc[:, ds(i + g * per_g, 1), :], ACT.Copy).then_inc(s_["staged"], 1)
                    act.wait_ge(s_["x_turned"], n(1))
                    A(x_rows[ALL], psum[:, 0, :].rearrange("p (c n) -> p c n", c=SB), ACT.Copy).then_inc(s_["x_kept"], 1)
                    for q in range(4):
                        act.wait_ge(s_["diffs"], n(q + 1, 4))
                        A(grown[:, q, :], psum[:, 1 + q, :], ACT.Exp).then_inc(s_["grown_exp"], 1)
                        A(inner[:, q, :], inner[:, q, :], ACT.Exp).then_inc(s_["inner_exp"], 1)

        @block.gpsimd
        def _(pool):
            for g in range(2):
                with pool.Fori(0, per_g) as i:
                    pool.wait_ge(s_["x_kept"], i + (1 + g * per_g))
                    for way in range(2):
                        weight = core.state_weight[:, :, ds(2 * i + (8 * g + HEADS2 * way), 2)].unsqueeze(3)
                        nc.gpsimd.tensor_tensor(x_weighed[:, way, :, :].rearrange("p c (e d) -> p c e d", e=2),
                                                x_rows[:, :, :].rearrange("p c (e d) -> p c e d", e=2),
                                                weight.broadcast_to([P, SB, 2, 64]), ALU.mult)\
                            .then_inc(s_["x_weighed"], 1)

        @block.vector
        def _(dve):
            V = nc.vector
            V.memset(core.scrap[:, 0:1], 0.0).then_inc(s_["y_kept"], 1)
            for g in range(2):
                c_t = core.xbc[:, KD + 2 + g, :]
                dve.wait_ge(s_["cb_made"], g + 1)
                for way, mask in enumerate((core.upper, core.lower)):
                    last = V.tensor_tensor(cb[:, way, :, :], psum[:, 1, :].rearrange("p (c l) -> p c l", c=SB),
                                           mask[:, :].unsqueeze(1).broadcast_to([P, SB, P]), ALU.mult)
                last.then_inc(s_["cb_kept"], 1)
                with dve.Fori(0, per_g) as i:
                    n = lambda k, m=1: i * m + (k + g * per_g * m)
                    row = lambda t, c, way, e: t[:, c, ds(2 * i + (8 * g + HEADS2 * way + e), 1)]
                    for q in range(4):
                        dve.wait_ge(s_["spread"], n(q + 1, 4))
                        for c in range(SB):
                            part = slice(c * P, (c + 1) * P)
                            last = V.tensor_scalar(inner[:, q, part], psum[:, 1 + q, part],
                                                   row(core.sums, c, q // 2, q % 2), 0.0, ALU.subtract, ALU.min)
                        last.then_inc(s_["diffs"], 1)
                    for q in range(4):
                        dve.wait_ge(s_["inner_exp"], n(q + 1, 4))
                        for c in range(SB):
                            part = slice(c * P, (c + 1) * P)
                            last = V.scalar_tensor_tensor(inner[:, q, part], inner[:, q, part],
                                                          row(core.dt, c, q // 2, q % 2), cb[:, q // 2, c, :],
                                                          ALU.mult, ALU.mult)
                        last.then_inc(s_["weighed"], 1)
                        dve.wait_ge(s_["grown_exp"], n(q + 1, 4))
                        V.tensor_tensor(grown[:, q, :], grown[:, q, :], c_t, ALU.mult).then_inc(s_["grown_made"], 1)
                    dve.wait_ge(s_["weighed"], n(4, 4))
                    for e in range(2):
                        V.tensor_tensor(inner[:, e, :], inner[:, e, :], inner[:, 2 + e, :], ALU.add)\
                            .then_inc(s_["inner_made"], 1)
                    dve.wait_ge(s_["states"], n(1))
                    V.tensor_copy(prev[:, 0, 1, :], psum[:, 5, 0:P])
                    V.tensor_copy(prev[:, 1, 2, :], psum[:, 6, 3 * P:4 * P]).then_inc(s_["prev_steps"], 1)
                    for step in range(2):
                        dve.wait_ge(s_["prev_steps"], n(step + 1, 2))
                        for way, at, to in ((0, 1 + step, 2 + step), (1, 2 - step, 1 - step)):
                            for e in range(2):
                                rows = slice(64 * e, 64 * e + 64)
                                last = V.scalar_tensor_tensor(
                                    prev[:, way, to, rows], prev[:, way, at, rows], row(core.chunk_decay, at, way, e),
                                    psum[:, 5 + way, at * P + 64 * e:at * P + 64 * e + 64], ALU.mult, ALU.add)
                        last.then_inc(s_["prev_steps"] if step == 0 else s_["prev_made"], 1)
                    dve.wait_ge(s_["y_made"], n(1))
                    V.scalar_tensor_tensor(y[:, :], x_t[:, :], core.d_skip[:, ds(i + g * per_g, 1)], psum[:, 7, :],
                                           ALU.mult, ALU.add).then_inc(s_["y_sum"], 1)
                    dve.wait_ge(s_["y_sum"], n(1))
                    z = core.z[:, ds(i + g * per_g, 1), :]
                    V.tensor_tensor(z, y[:, :].unsqueeze(1), z, ALU.mult).then_inc(s_["y_kept"], 1)



SEEN = [(0, 1), (0, 1, 2), (1, 2, 3), (2, 3)]


def window_attention(core):
    core.next_phase()
    nc, psum, mm = core.nc, core.psum, core.nc.tensor.matmul
    with ExitStack() as scope, nc.Block() as block:
        sb = lambda name, shape, dt=F32: scope.enter_context(nc.sbuf_tensor(name, shape, dt))
        q, k_, v = sb("wa_q", [P, 2, S]), sb("wa_k", [P, S]), sb("wa_v", [P, SB, 64])
        prob, prob_t = sb("wa_prob", [P, 2, SB, WIDE]), sb("wa_prob_t", [P, 2, 10, P])
        top, total, rest = sb("wa_top", [P, 2, SB]), sb("wa_total", [P, 2, SB]), sb("wa_rest", [P, 2, SB])
        names = ("staged", "scored", "scores_kept", "maxima", "floored", "top_made", "exps", "rest_made", "sums",
                 "inverse", "scaled", "turned", "turned_kept", "out_made", "out_kept", "cleared")
        s_ = {n: core.sem("wa_" + n) for n in names}
        half = (slice(0, 64), slice(64, 128))

        def columns(n):
            lo = (SEEN[n][0] - n + 1) * P
            return lo, lo + len(SEEN[n]) * P

        @block.tensor
        def _(pe):
            with pe.Fori(0, 4) as i:
                def scores(r):
                    e = r % 2
                    if r >= 2:
                        pe.wait_ge(s_["out_kept"], 4 * i + (r - 1))
                    for n in range(SB):
                        lo, hi = columns(n)
                        last = mm(psum[:, 4 * e + n, 0:hi - lo], q[half[e], r // 2, n * P:(n + 1) * P],
                                  k_[half[e], SEEN[n][0] * P:(SEEN[n][-1] + 1) * P], start=True, stop=True)
                    last.then_inc(s_["scored"], 1)

                pe.wait_ge(s_["staged"], i + 1)
                scores(0)
                scores(1)
                for r in range(4):
                    e = r % 2
                    pe.wait_ge(s_["scaled"], 4 * i + (r + 1))
                    for n in range(SB):
                        for m in range(len(SEEN[n])):
                            at = columns(n)[0] + m * P
                            last = nc.tensor.transpose(psum[:, 4 * e + n, m * P:(m + 1) * P],
                                                       prob[:, e, n, at:at + P], core.ident[:, :])
                    last.then_inc(s_["turned"], 1)
                    pe.wait_ge(s_["turned_kept"], 4 * i + (r + 1))
                    at = 0
                    for n in range(SB):
                        for m, kb in enumerate(SEEN[n]):
                            last = mm(psum[half[e], 4 * e, n * P:(n + 1) * P], v[:, kb, :], prob_t[:, e, at, :],
                                      start=m == 0, stop=m == len(SEEN[n]) - 1)
                            at += 1
                    last.then_inc(s_["out_made"], 1)
                    if r + 2 < 4:
                        scores(r + 2)

        @block.scalar
        def _(act):
            A = nc.scalar.activation
            nc.scalar.preload_act_table(ACT.Exp)
            with act.Fori(0, 4) as i:
                A(q[ALL], core.q2[:, ds(2 * i, 2), :], ACT.Copy)
                A(k_[:, :].unsqueeze(1), core.k2[:, ds(i, 1), :], ACT.Copy)
                A(v[ALL], core.v2[:, :, ds(64 * i, 64)], ACT.Copy).then_inc(s_["staged"], 1)

                def exps(r):
                    e = r % 2
                    act.wait_ge(s_["top_made"], 4 * i + (r + 1))
                    for n in range(SB):
                        lo, hi = columns(n)
                        A(prob[:, e, n, lo:hi], prob[:, e, n, lo:hi], ACT.Exp, bias=top[:, e, n:n + 1],
                          accum_out=total[:, e, n:n + 1])
                    A(rest[:, e, :], rest[:, e, :], ACT.Exp).then_inc(s_["exps"], 1)

                def keep_turned(r):
                    e = r % 2
                    act.wait_ge(s_["turned"], 4 * i + (r + 1))
                    A(prob_t[:, e, 0:2, :].rearrange("p a c -> p (a c)"), psum[:, 4 * e, 0:2 * P], ACT.Copy)
                    A(prob_t[:, e, 2:8, :].rearrange("p (n a) c -> p n (a c)", n=2), psum[:, 4 * e + 1:4 * e + 3, 0:3 * P],
                      ACT.Copy)
                    A(prob_t[:, e, 8:10, :].rearrange("p a c -> p (a c)"), psum[:, 4 * e + 3, 0:2 * P], ACT.Copy)\
                        .then_inc(s_["turned_kept"], 1)

                def keep_out(r):
                    e = r % 2
                    wait_alone(act, s_["out_made"], 4 * i + (r + 1))
                    A(core.q2[half[e], ds(2 * i + r // 2, 1), :], psum[half[e], one(4 * e), :], ACT.Copy)\
                        .then_inc(s_["out_kept"], 1)

                exps(0)
                for r in range(4):
                    if r + 1 < 4:
                        exps(r + 1)
                    keep_turned(r)
                    keep_out(r)

        @block.vector
        def _(dve):
            V = nc.vector
            for e in range(2):
                V.memset(prob[:, e, 0, 0:P], -1e30)
                last = V.memset(prob[:, e, 3, 2 * P:WIDE], -1e30)
            last.then_inc(s_["cleared"], 1)
            dve.wait_ge(s_["cleared"], 1)
            with dve.Fori(0, 4) as i:
                def maxima(r):
                    e = r % 2
                    dve.wait_ge(s_["scored"], 4 * i + (r + 1))
                    if r >= 2:
                        dve.wait_ge(s_["turned"], 4 * i + (r - 1))
                    for n in range(SB):
                        lo, hi = columns(n)
                        last = V.scalar_tensor_tensor(prob[:, e, n, lo:hi], core.distance[:, lo:hi],
                                                      core.slopes[:, ds(4 * i + r, 1)], psum[:, 4 * e + n, 0:hi - lo],
                                                      ALU.mult, ALU.add)
                    last.then_inc(s_["scores_kept"], 1)
                    dve.wait_ge(s_["scores_kept"], 4 * i + (r + 1))
                    V.tensor_reduce(top[:, e, :], prob[:, e, :, :], AX.X, ALU.max).then_inc(s_["maxima"], 1)
                    dve.wait_ge(s_["maxima"], 4 * i + (r + 1))
                    sink = core.sink[:, ds(4 * i + r, 1)]
                    V.tensor_scalar(top[:, e, :], top[:, e, :], sink, -1.0, ALU.max, ALU.mult)\
                        .then_inc(s_["floored"], 1)
                    dve.wait_ge(s_["floored"], 4 * i + (r + 1))
                    V.tensor_scalar(rest[:, e, :], top[:, e, :], sink, None, ALU.add).then_inc(s_["top_made"], 1)

                def scale(r):
                    e = r % 2
                    dve.wait_ge(s_["exps"], 4 * i + (r + 1))
                    V.tensor_tensor(total[:, e, :], total[:, e, :], rest[:, e, :], ALU.add).then_inc(s_["sums"], 1)
                    dve.wait_ge(s_["sums"], 4 * i + (r + 1))
                    V.reciprocal(total[:, e, :], total[:, e, :]).then_inc(s_["inverse"], 1)
                    dve.wait_ge(s_["inverse"], 4 * i + (r + 1))
                    for n in range(SB):
                        lo, hi = columns(n)
                        last = V.tensor_scalar(prob[:, e, n, lo:hi], prob[:, e, n, lo:hi], total[:, e, n:n + 1], None,
                                               ALU.mult)
                    last.then_inc(s_["scaled"], 1)

                maxima(0)
                for r in range(4):
                    if r + 1 < 4:
                        maxima(r + 1)
                    scale(r)



def project_out(core):
    core.next_phase()
    nc = core.nc
    with ExitStack() as scope, nc.Block() as block:
        sb = lambda name, shape, dt=F32: scope.enter_context(nc.sbuf_tensor(name, shape, dt))
        work, rstd = sb("po_work", [P, KD, S]), sb("po_rstd", [P, S])
        y = [sb("po_y_hi", [P, 2 * KD, S], F32R), sb("po_y_lo", [P, 2 * KD, S], F32R)]
        mix = core.q2
        st = core.st["out2"]
        hi_made, split, added = core.sem("po_hi_made"), core.sem("po_split"), core.sem("po_added")
        ssm = Norm(core, core.z, work, rstd, "ssm_norm_2", y[0][:, 0:KD, :], y[1][:, 0:KD, :])
        post = Norm(core, mix, work, rstd, "norm_mix_post_2")

        @block.sync
        def _(sp):
            load_stage(core, sp, st)

        @block.tensor
        def _(pe):
            ssm.pe(pe)
            ssm.ready(pe, KD - 1)
            pe.wait_ge(split, 1)
            pe_tiles(core, pe, st, y, tiles=1, k_tiles=2 * KD)
            post.pe(pe)

        @block.scalar
        def _(act):
            nc.scalar.activation(y[0][:, KD:, :], core.q2[ALL], ACT.Copy).then_inc(hi_made, 1)
            ssm.act(act)
            act.wait_ge(core.signals["dve_evac"].sem, core.signals["dve_evac"].taken + KD)
            post.act(act)

        @block.vector
        def _(dve):
            dve.wait_ge(hi_made, 1)
            nc.vector.tensor_tensor(y[1][:, KD:, :], core.q2[ALL], y[0][:, KD:, :].bitcast(F32), ALU.subtract)\
                .then_inc(split, 1)
            ssm.dve(dve)
            keep_split(core, dve, st, mix)
            post.dve(dve)
            dve.wait_ge(core.signals["normed"].sem, post.normed + KD)
            nc.vector.tensor_tensor(core.h[ALL], core.h[ALL], work[ALL], ALU.add).then_inc(added, 1)


def keep_split(core, dve, st, out):
    signal = core.signals["dve_evac"]
    signal.take(st.steps)
    for s, u, c in turns_of(dve, st):
        core.split_chunk(dve, c.next())
        dve.wait_ge(core.chunk_done, c.number + 1)
        core.nc.vector.tensor_copy(out[:, one(s), :], core.psum[:, one(2 * u), :]).then_inc(signal.sem, 1)


def mlp(core):
    core.next_phase()
    nc, psum = core.nc, core.psum
    with ExitStack() as scope, nc.Block() as block:
        sb = lambda name, shape, dt=F32: scope.enter_context(nc.sbuf_tensor(name, shape, dt))
        work, rstd, acc = sb("ml_work", [P, KD, S]), sb("ml_rstd", [P, S]), sb("ml_acc", [P, KD, S])
        x = [sb("ml_x_hi", [P, KD, S], F32R), sb("ml_x_lo", [P, KD, S], F32R)]
        hid = [sb("ml_hid_hi", [P, HM, S], F32R), sb("ml_hid_lo", [P, HM, S], F32R)]
        names = ("relu", "hi_made", "split", "added", "out_turned", "out_kept", "out_stored")
        s_ = {n: core.sem("ml_" + n) for n in names}
        norm = Norm(core, core.h, work, rstd, "norm_mlp_pre_2", *x)
        post = Norm(core, acc, work, rstd, "norm_mlp_post_2")
        relu = work
        evac, asig, done = core.signals["dve_evac"], core.signals["act_evac"], core.chunk_done
        steps = HM // 2
        rows_out = acc[:, :, :].rearrange("p (b k) s -> p b (k s)", b=SB)

        @block.sync
        def _(sp):
            for h in range(2):
                load_stage(core, sp, core.st[f"mlp_up{h}"])
                load_stage(core, sp, core.st[f"mlp_down{h}"])
            for b in range(SB):
                sp.wait_ge(s_["out_kept"], 2 * b + 2)
                sp.dma_start(core.out[0, b * P:(b + 1) * P, :], rows_out[:, b, :]).then_inc(s_["out_stored"], 16)
            sp.wait_ge(s_["out_stored"], 16 * SB)

        @block.tensor
        def _(pe):
            norm.pe(pe)
            norm.ready(pe, KD - 1)
            before = evac.taken
            for h in range(2):
                pe_tiles(core, pe, core.st[f"mlp_up{h}"], x)
                evac.taken += steps
                pe.wait_ge(s_["split"], steps * (h + 1))
                pe_tiles(core, pe, core.st[f"mlp_down{h}"], hid, tiles=1, k_tiles=HM)
                evac.taken += KD
            evac.taken = before
            post.pe(pe)
            pe.wait_ge(s_["added"], 1)
            for b in range(SB):
                for a in range(2):
                    for k in range(4):
                        last = nc.tensor.transpose(psum[:, 2 * b + a, k * P:(k + 1) * P],
                                                   core.h[:, 4 * a + k, b * P:(b + 1) * P], core.ident[:, :])
                    last.then_inc(s_["out_turned"], 1)

        @block.scalar
        def _(act):
            norm.act(act)
            at = evac.taken
            for h in range(2):
                st = core.st[f"mlp_up{h}"]
                for s, u, c in turns_of(act, st):
                    act.wait_ge(done, c.number + 1)
                    nc.scalar.activation(relu[:, 2 * u:2 * u + 2, :], psum[:, 2 * u:2 * u + 2, :], ACT.Relu)\
                        .then_inc(s_["relu"], 1)
                    act.wait_ge(evac.sem, s + (at + 1))
                    nc.scalar.activation(hid[0][:, ds(2 * s, 2), :], relu[:, 2 * u:2 * u + 2, :], ACT.Copy)\
                        .then_inc(s_["hi_made"], 1)
                at += steps + KD
            act.wait_ge(evac.sem, at)
            post.act(act)

        @block.vector
        def _(dve):
            V = nc.vector
            norm.dve(dve)
            for h in range(2):
                st = core.st[f"mlp_up{h}"]
                evac.take(steps)
                for s, u, c in turns_of(dve, st):
                    core.split_chunk(dve, c.next())
                    dve.wait_ge(s_["relu"], s + (1 + steps * h))
                    part = relu[:, 2 * u:2 * u + 2, :]
                    V.scalar_tensor_tensor(part, psum[:, 2 * u:2 * u + 2, :], 0.0, part, ALU.max, ALU.mult)\
                        .then_inc(evac.sem, 1)
                    dve.wait_ge(s_["hi_made"], s + (1 + steps * h))
                    V.tensor_tensor(hid[1][:, ds(2 * s, 2), :], part, hid[0][:, ds(2 * s, 2), :].bitcast(F32),
                                    ALU.subtract).then_inc(s_["split"], 1)
                down = core.st[f"mlp_down{h}"]
                if h == 0:
                    keep_split(core, dve, down, acc)
                else:
                    evac.take(KD)
                    for s, u, c in turns_of(dve, down, peeled=1):
                        if c.per or c.number + 1 < core.chunks:
                            core.split_chunk(dve, c.next())
                        dve.wait_ge(done, c.number + 1)
                        V.tensor_tensor(acc[:, one(s), :], acc[:, one(s), :], psum[:, one(2 * u), :], ALU.add)\
                            .then_inc(evac.sem, 1)
            post.dve(dve)
            dve.wait_ge(core.signals["normed"].sem, post.normed + KD)
            V.tensor_tensor(core.h[ALL], core.h[ALL], work[ALL], ALU.add).then_inc(s_["added"], 1)
            for b in range(SB):
                for a in range(2):
                    dve.wait_ge(s_["out_turned"], 2 * b + a + 1)
                    V.tensor_copy(rows_out[:, b, a * S:(a + 1) * S], psum[:, 2 * b + a, :])\
                        .then_inc(s_["out_kept"], 1)


def second_block(core):
    nc = core.nc
    with ExitStack() as outer:
        keep = lambda name, shape, dt=F32: outer.enter_context(nc.sbuf_tensor(name, shape, dt))
        core.q2, core.z = keep("q2", [P, KD, S]), keep("z2", [P, KD, S])
        with ExitStack() as inner:
            keep = lambda name, shape, dt=F32: inner.enter_context(nc.sbuf_tensor(name, shape, dt))
            core.k2, core.v2 = keep("k2", [P, 4, S]), keep("v2", [P, SB, 256])
            core.xbc, core.dt_t = keep("xbc", [P, 12, S]), keep("dt_t", [R2, S])
            core.distance, core.offsets = keep("distance", [P, WIDE]), keep("offsets", [P, WIDE], I32)
            core.dt_bias, core.a_log = keep("dt_bias", [P, R2]), keep("a_log", [P, R2])
            core.sink, core.slopes, core.d_skip = keep("sink", [P, HEADS2]), keep("slopes", [P, HEADS2]), keep("d_skip", [P, KD])
            input_projections(core)
            core.dt, core.sums = keep("dt", [P, SB, R2]), keep("sums", [P, SB, R2])
            core.state_weight, core.chunk_decay = keep("state_weight", [P, SB, R2]), keep("chunk_decay", [P, SB, R2])
            core.sums_t = keep("sums_t", [R2, S])
            ssd_prepare(core)
            ssd(core)
            window_attention(core)
        project_out(core)
    mlp(core)


def program(nc, inputs, out):
    with ExitStack() as stack:
        core = Core(nc, inputs, out, stack)
        core.st = weight_stages(core)
        mixer(core)
        first_block_rest(core, stack)
        second_block(core)


def mixer(core):
    nc = core.nc
    with ExitStack() as scope:
        r_names = ("rw_r", "rw_k", "rw_v", "rw_decay", "rw_a", "rw_g")
        core.rw = {n: scope.enter_context(nc.sbuf_tensor(n, [P, KW, S], F32)) for n in r_names}
        core.level_masks = scope.enter_context(nc.sbuf_tensor("level_masks", [P, 2, LEVELS, P], F32))
        with ExitStack() as inner:
            core.x_hi = inner.enter_context(nc.sbuf_tensor("x_hi", [P, KD, S], F32R))
            core.x_lo = inner.enter_context(nc.sbuf_tensor("x_lo", [P, KD, S], F32R))
            with ExitStack() as h_scope:
                core.h = h_scope.enter_context(nc.sbuf_tensor("h_start", [P, KD, S], F32))
                start(core)
                conv_branch(core)
            stick_breaking(core)
            rwkv_projections(core)
        with ExitStack() as inner:
            keep = lambda name, shape: inner.enter_context(nc.sbuf_tensor(name, shape, F32))
            core.kk, core.e_plus, core.e_minus, core.bonus = (keep("rw_" + name, [P, KW, S])
                                                              for name in ("kk", "e_plus", "e_minus", "bonus"))
            core.middle, core.growth = keep("rw_middle", [P, KW, SB]), keep("rw_growth", [P, KW, SB])
            core.k_a_less_1 = keep("rw_k_a_less_1", [P, KW])
            core.o_t = keep("rw_o_t", [P, KW, S])
            rwkv_prepare(core)
            rwkv_recurrence(core)
            rwkv_finish(core)


def first_block_rest(core, scope):
    nc = core.nc
    core.h = scope.enter_context(nc.sbuf_tensor("h", [P, KD, S], F32))
    def split_tiles(inner, name):
        core.m_hi = inner.enter_context(nc.sbuf_tensor(name + "_hi", [P, KD, S], F32R))
        core.m_lo = inner.enter_context(nc.sbuf_tensor(name + "_lo", [P, KD, S], F32R))

    with ExitStack() as merged:
        split_tiles(merged, "merged")
        gate_and_merge(core)
        mix_out(core)
    with ExitStack() as attention:
        keep = lambda name, shape: attention.enter_context(nc.sbuf_tensor(name, shape, F32))
        core.ca_q, core.ca_k, core.ca_v = keep("ca_q", [P, KD, S]), keep("ca_k", [P, KD, MEM]), keep("ca_v", [P, 2, D])
        memory_projections(core)
        split_tiles(attention, "attended")
        memory_attention(core)
        memory_out(core)
    ffn(core)


_INS = ["x", "mem", "w_comb", "w_lora", "a_lora", "g_lora", "branch_proj", "w_mix_out", "ca_wq", "ca_wkv", "ca_wo",
        "ffn_up", "ffn_down", "w_in_2", "dt_bias_2", "a_log_2", "d_skip_2", "attn_sink_2", "w_out_2", "w_up_2",
        "w_down_2"] + [name for name, _ in PARAM_ROWS]


def kernel(**inputs):
    import numpy as np
    from concourse import bacc
    from concourse.bass_utils import run_bass_kernel_spmd

    nc = bacc.Bacc("TRN2", target_bir_lowering=False, num_devices=1)
    arrays, aps = {}, {}
    for name in _INS:
        arrays[f"in_{name}"] = np.ascontiguousarray(inputs[name])
        aps[name] = nc.dram_tensor(f"in_{name}", arrays[f"in_{name}"].shape, F32, kind="ExternalInput").ap()
    out = nc.dram_tensor("out", (1, S, D), F32, kind="ExternalOutput").ap()
    program(nc, aps, out)
    result = run_bass_kernel_spmd(nc, [arrays], core_ids=[0])
    return result.results[0]["out"]
```

```python
import concourse.bass as bass
from concourse import mybir
from contextlib import ExitStack

F32 = mybir.dt.float32
F32R = mybir.dt.float32r
I32 = mybir.dt.int32
ALU = mybir.AluOpType
ACT = mybir.ActivationFunctionType
AX = mybir.AxisListType
ds = bass.ds

P = 128
S = 512
D = 1024
KD = D // P
SB = S // P
MEM = 256
W = 512
KW = W // P
RMS_EPS = 1e-6
GN_EPS = 64e-5
DECAY_SCALE = 0.6065306597126334
FFN = 2816
HF = FFN // P // 2
MLP = 4096
HM = MLP // P // 2
OFF_SB, OFF_GATE = 3 * W, 6 * W
OFF_RWKV = OFF_GATE + 3 * D
OFF_XBC, OFF_DT, OFF_Q, OFF_K, OFF_V = 1024, 2560, 2592, 3616, 3872
CHUNK = 2048

PARAM_ROWS = [("norm_mix", 8), ("conv_w", 12), ("mu_rwkv", 14), ("w0", 4), ("a0", 4), ("k_k", 4), ("k_a", 4),
              ("r_k", 4), ("lnx_w", 4), ("lnx_b", 4), ("gate_b", 24), ("norm_ca", 8), ("norm_mem", 8),
              ("norm_ffn", 8), ("ffn_conv_w", 132), ("ffn_conv_b", 44), ("norm_final", 8),
              ("norm_mix_pre_2", 8), ("conv_w_2", 60), ("conv_b_2", 12), ("ssm_norm_2", 8),
              ("norm_mix_post_2", 8), ("norm_mlp_pre_2", 8), ("norm_mlp_post_2", 8)]
PARAM_AT = {}
for _name, _rows in PARAM_ROWS:
    PARAM_AT[_name] = sum(r for _, r in PARAM_ROWS[:len(PARAM_AT)])
PARAM_TILES = 4


class Chunk:

    def __init__(self, at, per=0, turn=0):
        self.at, self.per, self.turn = at, per, turn
        self.slot = at % 2

    @property
    def number(self):
        return self.at + self.turn * self.per if self.per else self.at

    @property
    def rounds(self):
        return self.at // 2 + self.turn * (self.per // 2) if self.per else self.at // 2

    def next(self, k=1):
        return Chunk(self.at + k, self.per, self.turn)


class Signal:

    def __init__(self, sem):
        self.sem, self.taken = sem, 0

    def take(self, count):
        base, self.taken = self.taken, self.taken + count
        return base


class Core:

    def __init__(self, nc, inputs, out, stack):
        self.nc, self.a, self.out = nc, inputs, out
        def sb(name, shape, dt=F32):
            return stack.enter_context(nc.sbuf_tensor(name, shape, dt))
        def sem(name):
            return stack.enter_context(nc.semaphore(name))
        self.own, self.cleared = (ExitStack(), []), (ExitStack(), [])
        self.params = sb("params", [P, PARAM_TILES * P])
        self.ident = sb("ident", [P, P])
        self.ones = sb("ones", [P, P])
        self.pair_ones = sb("pair_ones", [P, P])
        self.upper = sb("upper", [P, P])
        self.strict = sb("strict", [P, P])
        self.lower = sb("lower", [P, P])
        self.neg_lower = sb("neg_lower", [P, P])
        self.neg_ones = sb("neg_ones", [P, P])
        self.w_raw = [sb(f"w_raw{u}", [P, CHUNK]) for u in range(2)]
        self.w_hi = [sb(f"w_hi{u}", [P, CHUNK], F32R) for u in range(2)]
        self.w_lo = [sb(f"w_lo{u}", [P, CHUNK], F32R) for u in range(2)]
        self.scrap = sb("scrap", [P, 2])
        self.psum = stack.enter_context(nc.psum_tensor("psum", [P, 8, 512], F32))
        self.w_loaded = [sem(f"w_loaded{u}") for u in range(2)]
        self.w_hi_made = sem("w_hi_made")
        self.w_split = sem("w_split")
        self.chunk_done = sem("chunk_done")
        self.signals = {}
        for name in ("act_evac", "dve_evac", "squares_made", "square_sums", "inverse_made", "rstd_made", "normed",
                     "x_hi_made", "x_split", "dve_chain", "act_chain", "loads", "stores"):
            self.signals[name] = Signal(sem(name))
        dram = lambda name, shape: nc.dram_tensor(name, shape, F32, kind="Internal").ap()
        self.merged_dram = dram("merged_spill", [P, 2 * KD, S])
        self.chunks = 0
        self.stages = []

    def next_phase(self):
        self.cleared[0].close()
        for s in self.own[1]:
            self.nc.gpsimd.sem_clear(s)
        self.cleared, self.own = self.own, (ExitStack(), [])

    def sem(self, name):
        s = self.own[0].enter_context(self.nc.semaphore(name))
        self.own[1].append(s)
        return s

    def param(self, name, col, n=1):
        return self.params[:, ds(PARAM_AT[name] + col, n)]


    def load_chunk(self, sp, c, parts):
        if c.at >= 2:
            wait_alone(sp, self.w_split, c.number - 1)
        at = 0
        for part in parts:
            rows, cols = part.shape[1:]
            dst = self.w_raw[c.slot][:, at:at + rows * cols].rearrange("p (a b) -> p a b", a=rows)
            sp.dma_start(dst, part).then_inc(self.w_loaded[c.slot], 16)
            at += rows * cols

    def split_chunk(self, dve, c):
        dve.wait_ge(self.w_loaded[c.slot], 32 * (c.rounds + 1))
        if c.at >= 2:
            dve.wait_ge(self.chunk_done, c.number - 1)
        self.nc.vector.tensor_copy(self.w_hi[c.slot][:, :], self.w_raw[c.slot][:, :]).then_inc(self.w_hi_made, 1)
        dve.wait_ge(self.w_hi_made, c.number + 1)
        self.nc.vector.tensor_tensor(self.w_lo[c.slot][:, :], self.w_raw[c.slot][:, :],
                                     self.w_hi[c.slot][:, :].bitcast(F32), ALU.subtract).then_inc(self.w_split, 1)

    def weights(self, c, *shape):
        n = 1
        for x in shape:
            n *= x
        names = "abc"[:len(shape)]
        pattern = f"p ({' '.join(names)}) -> p {' '.join(names)}"
        sizes = {k: v for k, v in zip(names, shape)}
        return [w[c.slot][:, 0:n].rearrange(pattern, **sizes) for w in (self.w_hi, self.w_lo)]

    def product(self, out, w, x, first, last):
        mm = self.nc.tensor.matmul
        mm(out, w[0], x[0], start=first, stop=False)
        mm(out, w[0], x[1], start=False, stop=False)
        return mm(out, w[1], x[0], start=False, stop=last)


def wait_alone(engine, sem, value):
    if not isinstance(value, int):
        value = engine.to_reg(value)
        engine.wait_ge(sem, 1)
    engine.wait_ge(sem, value)


def turns_of(engine, stage, peeled=0):
    kinds, per = len(stage.kinds), stage.per
    turns = stage.steps // per - peeled
    if turns == 1:
        for u in range(per):
            yield u, u % 2, Chunk(stage.base + u * kinds)
    elif turns:
        with engine.Fori(0, turns) as i:
            for u in range(per):
                yield i * per + u, u % 2, Chunk(stage.base + u * kinds, per * kinds, i)
    for s in range(turns * per, stage.steps):
        yield s, s % 2, Chunk(stage.base + s * kinds)


class Stage:

    def __init__(self, core, steps, kinds, per=2):
        assert per * len(kinds) % 2 == 0
        self.steps, self.kinds, self.per = steps, kinds, per
        self.base = core.chunks
        self.count = steps * len(kinds)
        core.chunks += self.count
        core.stages.append(self)


def load_from(core, sp, number):
    for st in core.stages:
        if st.base <= number < st.base + st.count:
            at = number - st.base
            core.load_chunk(sp, Chunk(number), st.kinds[at % len(st.kinds)](at // len(st.kinds)))


def load_stage(core, sp, st):
    period = st.per * len(st.kinds)
    turns = st.steps // st.per
    looped = turns if turns >= 3 else 1
    for number in range(st.base + 2, st.base + period):
        if number < st.base + st.count:
            load_from(core, sp, number)
    if looped > 1:
        with sp.Fori(1, looped) as i:
            for u in range(st.per):
                for k, kind in enumerate(st.kinds):
                    core.load_chunk(sp, Chunk(st.base + u * len(st.kinds) + k, period, i), kind(i * st.per + u))
    for number in range(max(st.base + 2, st.base + looped * period), st.base + st.count + 2):
        load_from(core, sp, number)


def one(i):
    return ds(i, 1)


def weight_stages(core):
    a = core.a
    kp = lambda w: w.rearrange("(k p) m -> p k m", p=P)
    wc = kp(a["w_comb"][0])
    bp = a["branch_proj"][0].rearrange("g (k p) m -> p (g k) m", p=P)
    half = lambda w: [w[:, 0:w.shape[1] // 2, :], w[:, w.shape[1] // 2:, :]]
    cols = lambda w, n: (lambda s: half(w[:, :, ds(s * n, n)]))
    tiles2 = lambda w: cols(w, 2 * P)
    tile1 = lambda w: cols(w, P)
    two = lambda at, gap: (lambda s: [wc[:, :, ds(s * P + at + g * gap, P)] for g in range(2)])
    st = {}
    st["conv"] = Stage(core, KW, [two(W, W), tile1(wc)])
    st["sb_v"] = Stage(core, 2, [tiles2(wc[:, :, OFF_SB + 2 * W:OFF_GATE])])
    st["sb_qk"] = Stage(core, KW, [two(OFF_SB, W)])
    st["gates"] = Stage(core, KD, [two(OFF_GATE, D), tile1(wc[:, :, OFF_GATE + 2 * D:]), tile1(bp[:, 0:2 * KW])])
    st["rkv"] = Stage(core, KW, [two(OFF_RWKV, W), tile1(wc[:, :, OFF_RWKV + 2 * W:])])
    st["lora"] = Stage(core, 1, [tiles2(wc[:, :, OFF_RWKV + 3 * W:])])
    st["branch"] = Stage(core, 4, [tiles2(bp[:, 2 * KW:3 * KW])])
    st["mix"] = Stage(core, 4, [tiles2(kp(a["w_mix_out"][0]))])
    st["ca_q"] = Stage(core, 4, [tiles2(kp(a["ca_wq"][0]))])
    wkv = kp(a["ca_wkv"][0])
    st["ca_k"] = Stage(core, 4, [tiles2(wkv[:, :, 0:D])])
    st["ca_v"] = Stage(core, 4, [tiles2(wkv[:, :, D:2 * D])])
    st["ca_o"] = Stage(core, 4, [tiles2(kp(a["ca_wo"][0]))])
    up = kp(a["ffn_up"][0])
    down = a["ffn_down"][0].rearrange("(h k p) m -> h p k m", h=2, p=P)
    for h in range(2):
        st[f"ffn_up{h}"] = Stage(core, HF, [(lambda h: lambda s: [up[:, :, ds(s * P + (h * HF + g * 2 * HF) * P, P)] for g in range(2)])(h)])
        st[f"ffn_down{h}"] = Stage(core, KD, [tile1(down[h])])
    wi = kp(a["w_in_2"][0])
    st["xbc"] = Stage(core, 6, [tiles2(wi[:, :, OFF_XBC:OFF_DT])])
    st["z"] = Stage(core, 4, [tiles2(wi[:, :, 0:OFF_XBC])])
    st["q2"] = Stage(core, 4, [tiles2(wi[:, :, OFF_Q:OFF_K])])
    st["kvdt"] = Stage(core, 3, [lambda s: half(wi[:, :, OFF_DT:OFF_DT + P] if s == 2 else
                                                wi[:, :, OFF_K + 256 * s:OFF_K + 256 * s + 256])])
    st["out2"] = Stage(core, KD, [tile1(kp(a["w_out_2"][0]))])
    up2 = kp(a["w_up_2"][0])
    down2 = a["w_down_2"][0].rearrange("(h k p) m -> h p k m", h=2, p=P)
    for h in range(2):
        st[f"mlp_up{h}"] = Stage(core, HM // 2, [tiles2(up2[:, :, h * HM * P:(h + 1) * HM * P])])
        st[f"mlp_down{h}"] = Stage(core, KD, [tile1(down2[h])])
    return st



def start(core):
    core.next_phase()
    nc, a, psum = core.nc, core.a, core.psum
    with ExitStack() as scope, nc.Block() as block:
        x_rows = scope.enter_context(nc.sbuf_tensor("x_rows", [P, SB, D], F32))
        param_rows = scope.enter_context(nc.sbuf_tensor("param_rows", [P, PARAM_TILES, P], F32))
        rows_cleared, rows_loaded, x_loaded = core.sem("rows_cleared"), core.sem("param_rows_loaded"), core.sem("x_loaded")
        made, masks = core.sem("constants_made"), core.sem("masks_made")
        turned, kept = core.sem("start_turned"), core.sem("start_kept")
        raw_cleared = core.sem("w_raw_cleared")
        column_dmas = []

        @block.sync
        def _(sp):
            sp.wait_ge(raw_cleared, 1)
            load_from(core, sp, 0)
            sp.dma_start(x_rows[:, :, :], a["x"][0].rearrange("(b p) d -> p b d", p=P)).then_inc(x_loaded, 16)
            load_from(core, sp, 1)
            sp.wait_ge(rows_cleared, 1)
            for name, rows in PARAM_ROWS:
                v = a[name]
                flat = v.rearrange(" ".join("abcd"[:len(v.shape)]) + " -> (" + " ".join("abcd"[:len(v.shape)]) + ")")
                flat = flat.rearrange("(r c) -> r c", c=P)
                done = 0
                while done < rows:
                    at = PARAM_AT[name] + done
                    n = min(rows - done, P - at % P)
                    sp.dma_start(param_rows[at % P:at % P + n, at // P, :], flat[done:done + n, :])\
                        .then_inc(rows_loaded, 16)
                    column_dmas.append(name)
                    done += n

        @block.gpsimd
        def _(pool):
            g = nc.gpsimd
            g.memset(param_rows[:, :, :], 0.0).then_inc(rows_cleared, 1)
            g.memset(core.ident[:, :], 0.0).then_inc(made, 1)
            g.memset(core.ones[:, :], 1.0).then_inc(made, 1)
            g.memset(core.neg_ones[:, :], -1.0).then_inc(made, 1)
            g.memset(core.pair_ones[:, :], 0.0).then_inc(made, 1)
            pool.wait_ge(made, 4)
            g.memset(core.pair_ones[0:64, 0:64], 1.0).then_inc(made, 1)
            pool.wait_ge(made, 5)
            g.memset(core.pair_ones[64:128, 64:128], 1.0).then_inc(made, 1)
            pool.wait_ge(made, 6)
            g.affine_select(out=core.ident[:, :], in_=core.ident[:, :], compare_op=ALU.not_equal, fill=1.0, base=0,
                            pattern=[[-1, P]], channel_multiplier=1).then_inc(masks, 1)
            g.affine_select(out=core.upper[:, :], in_=core.ones[:, :], compare_op=ALU.is_ge, fill=0.0, base=0,
                            pattern=[[1, P]], channel_multiplier=-1).then_inc(masks, 1)
            g.affine_select(out=core.strict[:, :], in_=core.ones[:, :], compare_op=ALU.is_gt, fill=0.0, base=0,
                            pattern=[[1, P]], channel_multiplier=-1).then_inc(masks, 1)
            g.affine_select(out=core.lower[:, :], in_=core.ones[:, :], compare_op=ALU.is_ge, fill=0.0, base=0,
                            pattern=[[-1, P]], channel_multiplier=1).then_inc(masks, 1)
            g.affine_select(out=core.neg_lower[:, :], in_=core.neg_ones[:, :], compare_op=ALU.is_ge, fill=0.0, base=0,
                            pattern=[[-1, P]], channel_multiplier=1).then_inc(masks, 1)

        @block.tensor
        def _(pe):
            pe.wait_ge(masks, 5)
            pe.wait_ge(x_loaded, 16)
            for k in range(KD):
                for b in range(SB):
                    last = nc.tensor.transpose(psum[:, k, b * P:(b + 1) * P], x_rows[:, b, k * P:(k + 1) * P],
                                               core.ident[:, :])
                last.then_inc(turned, 1)
            pe.wait_ge(rows_loaded, 16 * len(column_dmas))
            pe.wait_ge(kept, 1)
            for t in range(PARAM_TILES):
                last = nc.tensor.transpose(psum[:, 0, t * P:(t + 1) * P], param_rows[:, t, :], core.ident[:, :])
            last.then_inc(turned, 1)

        @block.vector
        def _(dve):
            nc.vector.memset(core.w_raw[0][:, :], 0.0)
            nc.vector.memset(core.w_raw[1][:, :], 0.0).then_inc(raw_cleared, 1)
            core.split_chunk(dve, Chunk(0))
            for k in range(KD):
                dve.wait_ge(turned, k + 1)
                nc.vector.tensor_copy(core.h[:, k, :], psum[:, k, :]).then_inc(kept, 1)
            dve.wait_ge(turned, KD + 1)
            nc.vector.tensor_copy(core.params[:, :], psum[:, 0, :]).then_inc(kept, PARAM_TILES)
            nc.vector.memset(core.scrap[:, 0:1], 0.0).then_inc(core.signals["dve_evac"].sem, core.signals["dve_evac"].take(2) + 2)

        @block.scalar
        def _(act):
            act.wait_ge(made, 6)
            nc.scalar.activation(core.scrap[:, 1:2], core.ones[:, 0:1], ACT.Copy)\
                .then_inc(core.signals["act_evac"].sem, core.signals["act_evac"].take(2) + 2)



class Norm:

    def __init__(self, core, src, work, rstd, gain, hi=None, lo=None, width=S, bank=7, dest=None):
        self.core, self.src, self.work, self.rstd, self.gain = core, src, work, rstd, gain
        self.hi, self.lo, self.width, self.bank = hi, lo, width, bank
        self.dest = work if dest is None else dest
        take = lambda name, n: core.signals[name].take(n)
        self.squares, self.sums, self.inverse = take("squares_made", 4), take("square_sums", 1), take("inverse_made", 2)
        self.made, self.normed = take("rstd_made", 1), take("normed", KD)
        self.his, self.split = (take("x_hi_made", 4), take("x_split", 4)) if hi is not None else (0, 0)

    def on(self, name):
        return self.core.signals[name].sem

    def act(self, act):
        self.act_squares(act)
        self.act_rest(act)

    def act_squares(self, act):
        nc = self.core.nc
        for q in range(4):
            nc.scalar.activation(self.work[:, 2 * q:2 * q + 2, :], self.src[:, 2 * q:2 * q + 2, :], ACT.Square)\
                .then_inc(self.on("squares_made"), 1)

    def act_rest(self, act):
        nc = self.core.nc
        act.wait_ge(self.on("inverse_made"), self.inverse + 2)
        nc.scalar.activation(self.rstd[:, 0:self.width], self.rstd[:, 0:self.width], ACT.Sqrt)\
            .then_inc(self.on("rstd_made"), 1)
        if self.hi is None:
            return
        for q in range(4):
            act.wait_ge(self.on("normed"), self.normed + 2 * q + 2)
            nc.scalar.activation(self.hi[:, 2 * q:2 * q + 2, :], self.work[:, 2 * q:2 * q + 2, :], ACT.Copy)\
                .then_inc(self.on("x_hi_made"), 1)

    def pe(self, pe):
        nc = self.core.nc
        for k in range(KD):
            if k % 2 == 0:
                pe.wait_ge(self.on("squares_made"), self.squares + k // 2 + 1)
            last = nc.tensor.matmul(self.core.psum[:, self.bank, 0:self.width], self.core.ones[:, :],
                                    self.work[:, k, :], start=k == 0, stop=k == KD - 1)
        last.then_inc(self.on("square_sums"), 1)

    def dve(self, dve):
        nc, n = self.core.nc, self.width
        dve.wait_ge(self.on("square_sums"), self.sums + 1)
        nc.vector.tensor_scalar(self.rstd[:, 0:n], self.core.psum[:, self.bank, 0:n], 1.0 / D, RMS_EPS,
                                ALU.mult, ALU.add).then_inc(self.on("inverse_made"), 1)
        dve.wait_ge(self.on("inverse_made"), self.inverse + 1)
        nc.vector.reciprocal(self.rstd[:, 0:n], self.rstd[:, 0:n]).then_inc(self.on("inverse_made"), 1)
        dve.wait_ge(self.on("rstd_made"), self.made + 1)

        def low(q):
            dve.wait_ge(self.on("x_hi_made"), self.his + q + 1)
            nc.vector.tensor_tensor(self.lo[:, 2 * q:2 * q + 2, :], self.work[:, 2 * q:2 * q + 2, :],
                                    self.hi[:, 2 * q:2 * q + 2, :].bitcast(F32), ALU.subtract)\
                .then_inc(self.on("x_split"), 1)

        for k in range(KD):
            nc.vector.scalar_tensor_tensor(self.dest[:, k, :], self.src[:, k, :], self.core.param(self.gain, k),
                                           self.rstd[:, 0:n], ALU.mult, ALU.mult).then_inc(self.on("normed"), 1)
            if self.hi is not None and k % 2 and k > 1:
                low(k // 2 - 1)
        if self.hi is not None:
            low(3)

    def ready(self, engine, k):
        engine.wait_ge(self.on("x_split"), self.split + k // 2 + 1)



def conv_branch(core):
    core.next_phase()
    nc, psum, st = core.nc, core.psum, core.st["conv"]
    evac, evac0 = core.signals["dve_evac"].sem, core.signals["dve_evac"].take(KW)
    with ExitStack() as scope, nc.Block() as block:
        sb = lambda name, shape, dt=F32: scope.enter_context(nc.sbuf_tensor(name, shape, dt))
        work, rstd = core.rw_all[:, 0:KD, :], sb("rstd", [P, S])
        norm = Norm(core, core.h, work, rstd, "norm_mix", core.x_hi, core.x_lo)
        gate_c = sb("conv_c", [P, 2, S])
        y, product, mixed = work[:, 0:4, :], work[:, 4:6, :], work[:, 6:8, :]
        y_hi, y_lo = core.y_conv
        c_kept, cx_made, taps = (core.sem(n) for n in ("conv_c_kept", "conv_cx_made", "conv_taps"))
        y_hi_made, y_split = core.sem("conv_y_hi_made"), core.sem("conv_y_split")
        done = core.chunk_done

        @block.sync
        def _(sp):
            load_stage(core, sp, st)

        @block.tensor
        def _(pe):
            norm.pe(pe)
            for j, u, c in turns_of(pe, st):
                pe.wait_ge(core.w_split, c.number + 1)
                pe.wait_ge(evac, j + (evac0 - 1))
                hi, lo = core.weights(c, 2, KD, P)
                for k in range(KD):
                    if k % 2 == 0:
                        norm.ready(pe, k)
                    for g in range(2):
                        last = core.product(psum[:, 3 * u + g, :], (hi[:, g, k, :], lo[:, g, k, :]),
                                            (core.x_hi[:, k, :], core.x_lo[:, k, :]), k == 0, k == KD - 1)
                last.then_inc(done, 1)
                b = c.next()
                pe.wait_ge(core.w_split, b.number + 1)
                hi, lo = core.weights(b, KD, P)
                for k in range(KD):
                    last = core.product(psum[:, 3 * u + 2, :], (hi[:, k, :], lo[:, k, :]),
                                        (core.x_hi[:, k, :], core.x_lo[:, k, :]), k == 0, k == KD - 1)
                last.then_inc(done, 1)

        @block.scalar
        def _(act):
            norm.act(act)
            for j, u, c in turns_of(act, st):
                act.wait_ge(done, c.number + 1)
                nc.scalar.activation(gate_c[:, u, :], psum[:, 3 * u, :], ACT.Copy).then_inc(c_kept, 1)
                act.wait_ge(evac, j + (evac0 + 1))
                nc.scalar.activation(y_hi[:, one(j), :], y[:, one(j), :], ACT.Copy).then_inc(y_hi_made, 1)

        @block.vector
        def _(dve):
            norm.dve(dve)
            for j, u, c in turns_of(dve, st):
                core.split_chunk(dve, c.next())
                dve.wait_ge(done, c.number + 1)
                dve.wait_ge(c_kept, j + 1)
                nc.vector.tensor_tensor(product[:, u, :], gate_c[:, u, :], psum[:, 3 * u + 1, :], ALU.mult)\
                    .then_inc(cx_made, 1)
                dve.wait_ge(cx_made, j + 1)
                nc.vector.tensor_scalar(mixed[:, u, :], product[:, u, :], core.param("conv_w", j + 2 * KW), None,
                                        ALU.mult).then_inc(taps, 1)
                for lag in (1, 2):
                    dve.wait_ge(taps, 3 * j + lag)
                    nc.vector.scalar_tensor_tensor(mixed[:, u, lag:], product[:, u, :S - lag],
                                                   core.param("conv_w", j + (2 - lag) * KW), mixed[:, u, lag:],
                                                   ALU.mult, ALU.add).then_inc(taps, 1)
                core.split_chunk(dve, c.next(2))
                dve.wait_ge(done, c.number + 2)
                dve.wait_ge(taps, 3 * j + 3)
                nc.vector.tensor_tensor(y[:, one(j), :], mixed[:, one(u), :], psum[:, one(3 * u + 2), :], ALU.mult)\
                    .then_inc(evac, 1)
                dve.wait_ge(y_hi_made, j + 1)
                nc.vector.tensor_tensor(y_lo[:, one(j), :], y[:, one(j), :], y_hi[:, one(j), :].bitcast(F32),
                                        ALU.subtract).then_inc(y_split, 1)



Z_WIDTH = [S - b * P for b in range(SB)]
Z_AT = [0, 512, 1024, 896]


def stick_breaking(core):
    core.next_phase()
    nc, psum = core.nc, core.psum
    st_v, st = core.st["sb_v"], core.st["sb_qk"]
    flat = psum[:, :, :].rearrange("p b c -> p (b c)")
    mm = nc.tensor.matmul
    with ExitStack() as scope, nc.Block() as block:
        sb = lambda name, shape, dt=F32: scope.enter_context(nc.sbuf_tensor(name, shape, dt))
        v_pair = sb("sb_v_pair", [P, 2, SB, P])
        v_rows, y, q, k_ = (core.rw_all[:, at:at + n, :] for at, n in ((0, SB), (4, KW), (8, 2), (10, 2)))
        y_hi, y_lo = core.y_sb
        t = sb("sb_softplus", [P, 2, 1280])
        done = core.chunk_done
        names = ("v_kept", "v_staged", "q_kept", "k_kept", "z_made", "abs_made", "exp_made", "log_made", "sp_raw",
                 "sp_masked", "cum_made", "att_raw", "att_masked", "o_made", "o_kept", "y_hi_made", "y_split")
        s_ = {n: core.sem("sb_" + n) for n in names}

        @block.sync
        def _(sp):
            load_stage(core, sp, st_v)
            load_stage(core, sp, st)

        @block.tensor
        def _(pe):
            for c in range(2):
                pe.wait_ge(core.w_split, st_v.base + c + 1)
                w = core.weights(Chunk(st_v.base + c), KD, 256)
                for b in range(SB):
                    for k in range(KD):
                        x = [v[:, k, b * P:(b + 1) * P] for v in (core.x_hi, core.x_lo)]
                        last = core.product(psum[:, 2 * c + b // 2, b % 2 * 256:b % 2 * 256 + 256], x,
                                            (w[0][:, k, :], w[1][:, k, :]), k == 0, k == KD - 1)
                last.then_inc(done, 1)

            def project(j):
                c = Chunk(st.base + j)
                pe.wait_ge(core.w_split, c.number + 1)
                if j == 0:
                    pe.wait_ge(s_["v_kept"], 2)
                else:
                    pe.wait_ge(s_["q_kept"], j)
                    pe.wait_ge(s_["k_kept"], j)
                hi, lo = core.weights(c, 2, KD, P)
                for g in range(2):
                    for k in range(KD):
                        last = core.product(psum[:, g, :], (hi[:, g, k, :], lo[:, g, k, :]),
                                            (core.x_hi[:, k, :], core.x_lo[:, k, :]), k == 0, k == KD - 1)
                last.then_inc(done, 1)

            project(0)
            for j in range(KW):
                u = j % 2
                pe.wait_ge(s_["q_kept"], j + 1)
                pe.wait_ge(s_["k_kept"], j + 1)
                for r in range(2):
                    if j:
                        pe.wait_ge(s_["o_kept"], 2 * j + r - 1)
                    z0, rows = (2 + 3 * r) * 512, slice(64 * r, 64 * r + 64)
                    for b in range(SB):
                        last = mm(flat[:, z0 + Z_AT[b]:z0 + Z_AT[b] + Z_WIDTH[b]], k_[rows, u, b * P:(b + 1) * P],
                                  q[rows, u, b * P:], start=b != 3, stop=False, skip_group_check=True)
                    last.then_inc(s_["z_made"], 1)
                if j + 1 < KW:
                    project(j + 1)
                for r in range(2):
                    z0 = (2 + 3 * r) * 512
                    pe.wait_ge(s_["sp_masked"], 2 * (2 * j + r) + 2)
                    for b in range(SB):
                        for c in range(b, SB):
                            at = z0 + Z_AT[b] + (c - b) * P
                            last = mm(flat[:, at:at + Z_WIDTH[c]], (core.neg_lower if c == b else core.neg_ones)[:, :],
                                      t[:, r, Z_AT[c]:Z_AT[c] + Z_WIDTH[c]], start=False, stop=False,
                                      skip_group_check=True)
                    last.then_inc(s_["cum_made"], 1)
                pe.wait_ge(s_["v_staged"], j + 1)
                for r in range(2):
                    pe.wait_ge(s_["att_masked"], 4 * (2 * j + r) + 4)
                    for b in range(SB):
                        last = mm(psum[64 * r:64 * r + 64, 2 + 3 * r, b * P:], v_pair[:, u, b, 64 * r:64 * r + 64],
                                  t[:, r, Z_AT[b]:Z_AT[b] + Z_WIDTH[b]], start=b == 0, stop=b == SB - 1,
                                  skip_group_check=True)
                    last.then_inc(s_["o_made"], 1)

        @block.scalar
        def _(act):
            for c in range(2):
                act.wait_ge(done, st_v.base + c + 1)
                nc.scalar.activation(v_rows[:, :, 256 * c:256 * c + 256],
                                     psum[:, 2 * c:2 * c + 2, :].rearrange("p a (b c) -> p (a b) c", b=2),
                                     ACT.Copy).then_inc(s_["v_kept"], 1)
            act.wait_ge(s_["v_kept"], 2)

            def keep_q(j):
                act.wait_ge(done, st.base + j + 1)
                nc.scalar.activation(q[:, j % 2, :], psum[:, 0, :], ACT.Copy, scale=0.125).then_inc(s_["q_kept"], 1)
                nc.scalar.activation(v_pair[:, j % 2, :, :], v_rows[:, :, j * P:(j + 1) * P], ACT.Copy)\
                    .then_inc(s_["v_staged"], 1)

            keep_q(0)
            for j in range(KW):
                for r in range(2):
                    n = 2 * j + r
                    z = flat[:, (2 + 3 * r) * 512:(2 + 3 * r) * 512 + 1280]
                    act.wait_ge(s_["z_made"], n + 1)
                    nc.scalar.activation(t[:, r, :], z, ACT.Abs).then_inc(s_["abs_made"], 1)
                    act.wait_ge(s_["abs_made"], n + 1)
                    nc.scalar.activation(t[:, r, :], t[:, r, :], ACT.Exp, scale=-1.0).then_inc(s_["exp_made"], 1)
                    act.wait_ge(s_["exp_made"], n + 1)
                    nc.scalar.activation(t[:, r, :], t[:, r, :], ACT.Ln, bias=1.0).then_inc(s_["log_made"], 1)
                if j + 1 < KW:
                    keep_q(j + 1)
                for r in range(2):
                    n = 2 * j + r
                    act.wait_ge(s_["cum_made"], n + 1)
                    nc.scalar.activation(t[:, r, :], flat[:, (2 + 3 * r) * 512:(2 + 3 * r) * 512 + 1280], ACT.Exp)\
                        .then_inc(s_["att_raw"], 1)
                for r in range(2):
                    act.wait_ge(s_["o_made"], 2 * j + r + 1)
                    nc.scalar.activation(y[64 * r:64 * r + 64, j, :], psum[64 * r:64 * r + 64, 2 + 3 * r, :], ACT.Copy)\
                        .then_inc(s_["o_kept"], 1)
            act.wait_ge(s_["o_kept"], 2 * KW)
            nc.scalar.activation(y_hi[:, :, :], y[:, :, :], ACT.Copy).then_inc(s_["y_hi_made"], 1)

        @block.gpsimd
        def _(pool):
            for n in range(2 * KW):
                pool.wait_ge(s_["att_raw"], n + 1)
                for b in range(SB):
                    diagonal = t[:, n % 2, Z_AT[b]:Z_AT[b] + P]
                    nc.gpsimd.affine_select(out=diagonal, in_=diagonal, compare_op=ALU.is_gt, fill=0.0, base=0,
                                            pattern=[[1, P]], channel_multiplier=-1).then_inc(s_["att_masked"], 1)

        @block.vector
        def _(dve):
            core.split_chunk(dve, Chunk(st_v.base + 1))
            core.split_chunk(dve, Chunk(st.base))

            def keep_and_split(j):
                core.split_chunk(dve, Chunk(st.base + j + 1))
                dve.wait_ge(done, st.base + j + 1)
                nc.vector.tensor_copy(k_[:, j % 2, :], psum[:, 1, :]).then_inc(s_["k_kept"], 1)

            keep_and_split(0)
            for j in range(KW):
                for r in range(2):
                    n = 2 * j + r
                    z = flat[:, (2 + 3 * r) * 512:(2 + 3 * r) * 512 + 1280]
                    dve.wait_ge(s_["log_made"], n + 1)
                    nc.vector.scalar_tensor_tensor(t[:, r, :], z, 0.0, t[:, r, :], ALU.max, ALU.add)\
                        .then_inc(s_["sp_raw"], 1)
                    dve.wait_ge(s_["sp_raw"], n + 1)
                    mask = core.strict[:, :].unsqueeze(1).broadcast_to([P, 2, P])
                    for at, gap in ((0, 512), (896, 128)):
                        pair = t[:, r, at:at + 2 * gap].rearrange("p (a c) -> p a c", a=2)[:, :, 0:P]
                        nc.vector.tensor_tensor(pair, pair, mask, ALU.mult).then_inc(s_["sp_masked"], 1)
                if j + 1 < KW:
                    keep_and_split(j + 1)
            dve.wait_ge(s_["y_hi_made"], 1)
            nc.vector.tensor_tensor(y_lo[:, :, :], y[:, :, :], y_hi[:, :, :].bitcast(F32), ALU.subtract)\
                .then_inc(s_["y_split"], 1)



LEVELS = 7
ALL = (slice(None), slice(None), slice(None))


def rwkv_projections(core):
    core.next_phase()
    nc, psum, a = core.nc, core.psum, core.a
    st, st_l = core.st["rkv"], core.st["lora"]
    evac, evac0 = core.signals["dve_evac"].sem, core.signals["dve_evac"].take(KW)
    rw = core.rw
    with ExitStack() as scope, nc.Block() as block:
        sb = lambda name, shape, dt=F32: scope.enter_context(nc.sbuf_tensor(name, shape, dt))
        scaled = sb("rw_scaled", [P, 6, S])
        one_minus = sb("rw_one_minus_mu", [P, 14])
        low = sb("rw_low", [P, 2, S])
        up = sb("rw_up", [P, 2, W])
        names = ("one_minus_made", "scaled_made", "up_loaded", "low_shifted", "low_mapped", "low_products",
                 "decay_sigmoid", "a_made", "decay_made", "g_kept", "mask_zeroed", "mask_from", "mask_made")
        s_ = {n: core.sem("rw_" + n) for n in names}
        done = core.chunk_done

        @block.sync
        def _(sp):
            sp.dma_start(up[0:64, 0, :], a["w_lora"][0]).then_inc(s_["up_loaded"], 16)
            sp.dma_start(up[64:128, 0, :], a["a_lora"][0]).then_inc(s_["up_loaded"], 16)
            sp.dma_start(up[:, 1, :], a["g_lora"][0]).then_inc(s_["up_loaded"], 16)
            load_stage(core, sp, st)
            load_stage(core, sp, st_l)

        @block.gpsimd
        def _(pool):
            g = nc.gpsimd
            g.memset(core.level_masks[:, :, :, :], 0.0).then_inc(s_["mask_zeroed"], 1)
            pool.wait_ge(s_["mask_zeroed"], 1)
            n = 0
            for level in range(LEVELS):
                w = 1 << level
                q = P // (2 * w)
                source = core.ones[:, 0:q * w].rearrange("p (q w) -> p q w", w=w)
                for flip in range(2):
                    view = core.level_masks[:, flip, level, :].rearrange("p (q h w) -> p q h w", h=2, w=w)[:, :, flip, :]
                    lo_edge = 0 if flip else w
                    g.affine_select(out=view, in_=source, compare_op=ALU.is_ge, fill=0.0, base=-lo_edge,
                                    pattern=[[-2 * w, q], [0, w]], channel_multiplier=1).then_inc(s_["mask_from"], 1)
                    n += 1
                    pool.wait_ge(s_["mask_from"], n)
                    g.affine_select(out=view, in_=view, compare_op=ALU.is_ge, fill=0.0, base=lo_edge + w - 1,
                                    pattern=[[2 * w, q], [0, w]], channel_multiplier=-1).then_inc(s_["mask_made"], 1)

        @block.tensor
        def _(pe):
            for j, u, c in turns_of(pe, st):
                pe.wait_ge(core.w_split, c.number + 1)
                pe.wait_ge(evac, j + (evac0 - 1))
                hi, lo = core.weights(c, 2, KD, P)
                for g in range(2):
                    for k in range(KD):
                        last = core.product(psum[:, 3 * u + g, :], (hi[:, g, k, :], lo[:, g, k, :]),
                                            (core.x_hi[:, k, :], core.x_lo[:, k, :]), k == 0, k == KD - 1)
                last.then_inc(done, 1)
                v = c.next()
                pe.wait_ge(core.w_split, v.number + 1)
                hi, lo = core.weights(v, KD, P)
                for k in range(KD):
                    last = core.product(psum[:, 3 * u + 2, :], (hi[:, k, :], lo[:, k, :]),
                                        (core.x_hi[:, k, :], core.x_lo[:, k, :]), k == 0, k == KD - 1)
                last.then_inc(done, 1)
            pe.wait_ge(core.w_split, st_l.base + 1)
            hi, lo = core.weights(Chunk(st_l.base), KD, 2, P)
            for g in range(2):
                for k in range(KD):
                    last = core.product(psum[:, 6 + g, :], (hi[:, k, g, :], lo[:, k, g, :]),
                                        (core.x_hi[:, k, :], core.x_lo[:, k, :]), k == 0, k == KD - 1)
            last.then_inc(done, 1)
            pe.wait_ge(s_["up_loaded"], 48)
            pe.wait_ge(s_["low_mapped"], 2)
            pe.wait_ge(evac, evac0 + KW)
            for j in range(KW):
                for part, rows in ((0, slice(0, 64)), (1, slice(64, 128))):
                    last = nc.tensor.matmul(psum[:, 4 * part + j, :], up[rows, 0, j * P:(j + 1) * P], low[rows, 0, :],
                                            start=True, stop=True)
                last.then_inc(s_["low_products"], 1)
            for j in range(KW):
                pe.wait_ge(s_["decay_sigmoid"], j + 1)
                nc.tensor.matmul(psum[:, j, :], up[:, 1, j * P:(j + 1) * P], low[:, 1, :], start=True, stop=True)\
                    .then_inc(s_["low_products"], 1)

        @block.scalar
        def _(act):
            for j, u, c in turns_of(act, st):
                for g in range(3):
                    if g != 1:
                        act.wait_ge(done, c.number + (1 if g == 0 else 2))
                    nc.scalar.activation(scaled[:, 3 * u + g, :], psum[:, 3 * u + g, :], ACT.Copy,
                                         scale=core.param("mu_rwkv", j + g * KW)).then_inc(s_["scaled_made"], 1)
            act.wait_ge(done, st_l.base + 1)
            act.wait_ge(evac, evac0 + KW)
            for g in range(2):
                nc.scalar.activation(scaled[:, g, :], psum[:, 6 + g, :], ACT.Copy,
                                     scale=core.param("mu_rwkv", 12 + g)).then_inc(s_["scaled_made"], 1)
            act.wait_ge(s_["low_shifted"], 1)
            nc.scalar.activation(low[0:64, 0, :], low[0:64, 0, :], ACT.Tanh).then_inc(s_["low_mapped"], 1)
            act.wait_ge(s_["low_shifted"], 2)
            nc.scalar.activation(low[:, 1, :], low[:, 1, :], ACT.Sigmoid).then_inc(s_["low_mapped"], 1)
            for j in range(KW):
                act.wait_ge(s_["low_products"], j + 1)
                nc.scalar.activation(rw["rw_decay"][:, j, :], psum[:, j, :], ACT.Sigmoid, bias=core.param("w0", j))\
                    .then_inc(s_["decay_sigmoid"], 1)
            for j in range(KW):
                nc.scalar.activation(rw["rw_a"][:, j, :], psum[:, 4 + j, :], ACT.Sigmoid, bias=core.param("a0", j))\
                    .then_inc(s_["a_made"], 1)

        @block.vector
        def _(dve):
            nc.vector.tensor_scalar(one_minus[:, :], core.params[:, ds(PARAM_AT["mu_rwkv"], 14)], -1.0, 1.0,
                                    ALU.mult, ALU.add).then_inc(s_["one_minus_made"], 1)
            dve.wait_ge(s_["one_minus_made"], 1)

            def shift(out, p, before, weight, sem):
                nc.vector.tensor_scalar(out[:, :, 0:1], p[:, :, 0:1], weight, None, ALU.mult)
                nc.vector.scalar_tensor_tensor(out[:, :, 1:], p[:, :, 1:], weight, before[:, :, 0:S - 1],
                                               ALU.mult, ALU.add).then_inc(sem, 1)

            shifted = core.sem("rw_rk_shifted")
            for j, u, c in turns_of(dve, st):
                core.split_chunk(dve, c.next())
                for g, name in enumerate(("rw_r", "rw_k", "rw_v")):
                    if g == 2:
                        core.split_chunk(dve, c.next(2))
                    dve.wait_ge(s_["scaled_made"], 3 * j + g + 1)
                    shift(rw[name][:, one(j), :], psum[:, one(3 * u + g), :], scaled[:, one(3 * u + g), :],
                          one_minus[:, ds(j + g * KW, 1)], evac if g == 2 else shifted)
            core.split_chunk(dve, Chunk(st_l.base + 1))
            for g in range(2):
                dve.wait_ge(s_["scaled_made"], 3 * KW + g + 1)
                shift(low[:, g:g + 1, :], psum[:, 6 + g:7 + g, :], scaled[:, g:g + 1, :], one_minus[:, 12 + g:13 + g],
                      s_["low_shifted"])
            dve.wait_ge(s_["decay_sigmoid"], KW)
            nc.vector.tensor_scalar(rw["rw_decay"][ALL], rw["rw_decay"][ALL], -DECAY_SCALE, None, ALU.mult)\
                .then_inc(s_["decay_made"], 1)
            for j in range(KW):
                dve.wait_ge(s_["low_products"], KW + j + 1)
                nc.vector.tensor_copy(rw["rw_g"][:, j, :], psum[:, j, :]).then_inc(s_["g_kept"], 1)



class Chain:

    def __init__(self, core, engine, name):
        self.engine, self.counted = engine, core.signals[name]

    def __call__(self, instruction):
        instruction.then_inc(self.counted.sem, 1)
        self.engine.wait_ge(self.counted.sem, self.counted.take(1) + 1)


def rwkv_prepare(core):
    core.next_phase()
    nc, psum, rw = core.nc, core.psum, core.rw
    r, k_, v, lw, a = (rw[n] for n in ("rw_r", "rw_k", "rw_v", "rw_decay", "rw_a"))
    kk, e_plus, e_minus, bonus = core.kk, core.e_plus, core.e_minus, core.bonus
    with nc.Block() as block:
        names = ("kk_raw", "kk_squares", "kk_sums", "kk_inverse", "kk_rstd", "bonus_terms", "bonus_sums",
                 "centred", "before_centred", "exps_made", "middle_made", "growth_made")
        s_ = {n: core.sem("rp_" + n) for n in names}
        by_chunk = lambda t: t[:, :, :].rearrange("p j (c t) -> p j c t", c=SB)

        @block.tensor
        def _(pe):
            pe.wait_ge(s_["kk_squares"], 1)
            for j in range(KW):
                last = nc.tensor.matmul(psum[:, j, :], core.pair_ones[:, :], e_plus[:, j, :], start=True, stop=True)
            last.then_inc(s_["kk_sums"], 1)
            pe.wait_ge(s_["bonus_terms"], KW)
            for j in range(KW):
                last = nc.tensor.matmul(psum[:, 4 + j, :], core.pair_ones[:, :], e_plus[:, j, :], start=True, stop=True)
            last.then_inc(s_["bonus_sums"], 1)

        @block.scalar
        def _(act):
            act.wait_ge(s_["kk_raw"], KW)
            nc.scalar.activation(e_plus[ALL], kk[ALL], ACT.Square).then_inc(s_["kk_squares"], 1)
            act.wait_ge(s_["kk_inverse"], 1)
            nc.scalar.activation(e_plus[ALL], e_plus[ALL], ACT.Sqrt).then_inc(s_["kk_rstd"], 1)
            act.wait_ge(s_["before_centred"], 1)
            nc.scalar.activation(e_plus[ALL], e_minus[ALL], ACT.Exp).then_inc(s_["exps_made"], 1)
            act.wait_ge(s_["exps_made"], 1)
            nc.scalar.activation(e_minus[ALL], e_minus[ALL], ACT.Exp, scale=-1.0).then_inc(s_["exps_made"], 1)
            nc.scalar.activation(lw[ALL], lw[ALL], ACT.Exp).then_inc(s_["exps_made"], 1)
            act.wait_ge(s_["middle_made"], 1)
            nc.scalar.activation(core.growth[ALL], core.growth[ALL], ACT.Exp).then_inc(s_["growth_made"], 1)

        @block.vector
        def _(dve):
            V = nc.vector
            chain = Chain(core, dve, "dve_chain")
            for j in range(KW):
                V.tensor_scalar(kk[:, j, :], k_[:, j, :], core.param("k_k", j), None, ALU.mult)\
                    .then_inc(s_["kk_raw"], 1)
            dve.wait_ge(s_["kk_sums"], 1)
            chain(V.tensor_scalar(e_plus[ALL], psum[:, 0:KW, :], 1e-24, None, ALU.max))
            V.reciprocal(e_plus[ALL], e_plus[ALL]).then_inc(s_["kk_inverse"], 1)
            dve.wait_ge(s_["kk_rstd"], 1)
            chain(V.tensor_tensor(kk[ALL], kk[ALL], e_plus[ALL], ALU.mult))
            chain(V.tensor_scalar(core.k_a_less_1[:, :], core.params[:, ds(PARAM_AT["k_a"], KW)], -1.0, None, ALU.add))
            for j in range(KW):
                chain(V.tensor_scalar(e_minus[:, j, :], a[:, j, :], core.param("k_a", j), core.k_a_less_1[:, j:j + 1],
                                      ALU.mult, ALU.subtract))
            chain(V.tensor_tensor(k_[ALL], k_[ALL], e_minus[ALL], ALU.mult))
            chain(V.tensor_tensor(a[ALL], a[ALL], kk[ALL], ALU.mult))
            for j in range(KW):
                V.scalar_tensor_tensor(e_plus[:, j, :], r[:, j, :], core.param("r_k", j), k_[:, j, :],
                                       ALU.mult, ALU.mult).then_inc(s_["bonus_terms"], 1)
            for j in range(KW):
                for c in range(SB):
                    part = slice(c * P, (c + 1) * P)
                    chain(V.tensor_tensor_scan(e_minus[:, j, part], core.ones[:, :], lw[:, j, part], 0.0,
                                               ALU.mult, ALU.add))
            dve.wait_ge(s_["bonus_sums"], 1)
            chain(V.tensor_tensor(bonus[ALL], v[ALL], psum[:, KW:2 * KW, :], ALU.mult))
            ends = by_chunk(e_minus)[:, :, :, P - 1:P].rearrange("p j c o -> p j (c o)")
            chain(V.tensor_scalar(core.middle[ALL], ends, 0.5, None, ALU.mult))
            middle = core.middle[:, :, :].unsqueeze(3).broadcast_to([P, KW, SB, P])
            V.tensor_tensor(by_chunk(e_minus), by_chunk(e_minus), middle, ALU.subtract).then_inc(s_["centred"], 1)
            dve.wait_ge(s_["centred"], 1)
            V.tensor_tensor(lw[ALL], e_minus[ALL], lw[ALL], ALU.subtract).then_inc(s_["before_centred"], 1)
            chain(V.tensor_copy(core.growth[ALL], core.middle[ALL]))
            V.tensor_tensor(core.growth[:, :, 0:SB - 1], core.middle[:, :, 0:SB - 1], core.middle[:, :, 1:SB], ALU.add)\
                .then_inc(s_["middle_made"], 1)


def rwkv_recurrence(core):
    core.next_phase()
    nc, psum, rw = core.nc, core.psum, core.rw
    r, k_, v, e_before, b_ = (rw[n] for n in ("rw_r", "rw_k", "rw_v", "rw_decay", "rw_a"))
    kk, e_plus, e_minus = core.kk, core.e_plus, core.e_minus
    mm = nc.tensor.matmul
    masks = core.level_masks
    with ExitStack() as scope, nc.Block() as block:
        sb = lambda name, shape, dt=F32: scope.enter_context(nc.sbuf_tensor(name, shape, dt))
        kr = sb("rc_kr", [P, KW, 2, P])
        bh, kh, vc = sb("rc_bh", [P, KW, P]), sb("rc_kh", [P, KW, P]), sb("rc_v", [P, KW, P])
        rows_ = sb("rc_rows", [P, 3, W])
        scores = sb("rc_scores", [P, 2, KW, 4, P])
        x, xt, nx = sb("rc_x", [P, 2, KW, P]), sb("rc_xt", [P, 2, KW, P]), sb("rc_nx", [P, 2, KW, P])
        rhs, u_, state = sb("rc_rhs", [P, 2, KW, 64]), sb("rc_u", [P, 2, KW, 64]), sb("rc_state", [P, KW, 64])
        names = ("staged", "v_staged", "turned", "rows_kept", "scored", "score_kept", "x_set", "x_made", "nx_made",
                 "nx_kept", "q_made", "rhs_made", "rhs_kept", "u_made", "u_kept", "o_made", "s_made", "o_kept",
                 "s_sum", "s_kept")
        s_ = {n: core.sem("rc_" + n) for n in names}
        half = (slice(0, 64), slice(64, 128))
        L1 = LEVELS - 1

        @block.tensor
        def _(pe):
            with pe.Fori(0, SB) as i:
                pe.wait_ge(s_["staged"], i + 1)
                pe.wait_ge(s_["v_staged"], i + 1)
                for n, t in enumerate((bh, kh, vc)):
                    for j in range(KW):
                        last = nc.tensor.transpose(psum[:, n, j * P:(j + 1) * P], t[:, j, :], core.ident[:, :])
                last.then_inc(s_["turned"], 1)
                for e in range(2):
                    if e:
                        pe.wait_ge(s_["rows_kept"], i + 1)
                    for j in range(KW):
                        if e:
                            pe.wait_ge(s_["score_kept"], 8 * i + (j + 1))
                        both = kr[half[e], j, :, :].rearrange("p a t -> p (a t)")
                        mm(psum[:, 3 + j, 0:256], bh[half[e], j, :], both, start=True, stop=True)
                        mm(psum[:, 3 + j, 256:512], kh[half[e], j, :], both, start=True, stop=True)
                        mm(psum[:, (7, 2)[e], j * P:(j + 1) * P], kr[half[e], j, 0, :], bh[half[e], j, :],
                           start=True, stop=True).then_inc(s_["scored"], 1)
                for level in range(1, LEVELS):
                    n = 2 * (level - 1)
                    for e in range(2):
                        pe.wait_ge(s_["x_made"], i * 2 * LEVELS + (n + e + 1))
                        for j in range(KW):
                            last = mm(psum[:, 3 * e, j * P:(j + 1) * P], scores[:, e, j, 0, :], x[:, e, j, :],
                                      start=True, stop=True)
                        last.then_inc(s_["nx_made"], 1)
                    for e in range(2):
                        pe.wait_ge(s_["nx_kept"], i * 2 * L1 + (n + e + 1))
                        for j in range(KW):
                            part = slice(j * P, (j + 1) * P)
                            if level < L1:
                                mm(psum[:, 3 * e + 1, part], xt[:, e, j, :], nx[:, e, j, :], start=True, stop=True)
                            last = mm(psum[:, 3 * e + 2, part], nx[:, e, j, :], xt[:, e, j, :], start=True, stop=True)
                        last.then_inc(s_["q_made"], 1)
                pe.wait_ge(s_["s_kept"], i + 1)
                pe.wait_ge(s_["score_kept"], 8 * i + 8)
                for e in range(2):
                    for j in range(KW):
                        out = psum[:, 6 + e, j * 64:(j + 1) * 64]
                        vj = rows_[:, 2, j * P + 64 * e:j * P + 64 * e + 64]
                        mm(out, kr[half[e], j, 0, :], state[half[e], j, :], start=True, stop=False)
                        last = mm(out, scores[:, e, j, 2, :], vj, start=False, stop=True)
                last.then_inc(s_["rhs_made"], 1)
                pe.wait_ge(s_["x_made"], i * 2 * LEVELS + 2 * LEVELS)
                pe.wait_ge(s_["rhs_kept"], i + 1)
                for e in range(2):
                    for j in range(KW):
                        last = mm(psum[:, e, j * 64:(j + 1) * 64], xt[:, e, j, :], rhs[:, e, j, :], start=True, stop=True)
                last.then_inc(s_["u_made"], 1)
                wait_alone(pe, s_["u_kept"], i + 1)
                for e in range(2):
                    for j in range(KW):
                        out = psum[half[e], 2 + e, j * P:(j + 1) * P]
                        vj = rows_[:, 2, j * P + 64 * e:j * P + 64 * e + 64]
                        mm(out, state[half[e], j, :], kr[half[e], j, 1, :], start=True, stop=False)
                        mm(out, u_[:, e, j, :], scores[:, e, j, 1, :], start=False, stop=False)
                        last = mm(out, vj, scores[:, e, j, 3, :], start=False, stop=True)
                last.then_inc(s_["o_made"], 1)
                for e in range(2):
                    for j in range(KW):
                        out = psum[half[e], 4 + e, j * 64:(j + 1) * 64]
                        at = slice(j * P + 64 * e, j * P + 64 * e + 64)
                        mm(out, rows_[:, 0, at], u_[:, e, j, :], start=True, stop=False)
                        last = mm(out, rows_[:, 1, at], rows_[:, 2, at], start=False, stop=True)
                last.then_inc(s_["s_made"], 1)

        @block.scalar
        def _(act):
            A = nc.scalar.activation
            ident8 = core.ident[:, :].unsqueeze(1).broadcast_to([P, 2 * KW, P])
            with act.Fori(0, SB) as i:
                A(vc[ALL], v[:, :, ds(i * P, P)], ACT.Copy).then_inc(s_["v_staged"], 1)
                A(x[:, :, :, :].rearrange("p e j t -> p (e j) t"), ident8, ACT.Copy)
                A(xt[:, :, :, :].rearrange("p e j t -> p (e j) t"), ident8, ACT.Copy).then_inc(s_["x_set"], 1)
                act.wait_ge(s_["turned"], i + 1)
                A(rows_[ALL], psum[:, 0:3, :], ACT.Copy).then_inc(s_["rows_kept"], 1)
                for n in range(2 * L1):
                    act.wait_ge(s_["nx_made"], i * 2 * L1 + (n + 1))
                    A(nx[:, n % 2, :, :].rearrange("p j t -> p (j t)"), psum[:, 3 * (n % 2), :], ACT.Copy)\
                        .then_inc(s_["nx_kept"], 1)
                act.wait_ge(s_["rhs_made"], i + 1)
                A(rhs[:, :, :, :].rearrange("p e j d -> p e (j d)"), psum[:, 6:8, 0:256], ACT.Copy)\
                    .then_inc(s_["rhs_kept"], 1)
                act.wait_ge(s_["u_made"], i + 1)
                A(u_[:, :, :, :].rearrange("p e j d -> p e (j d)"), psum[:, 0:2, 0:256], ACT.Copy)\
                    .then_inc(s_["u_kept"], 1)
                act.wait_ge(s_["o_made"], i + 1)
                for e in range(2):
                    A(core.o_t[half[e], :, ds(i * P, P)],
                      psum[half[e], 2 + e, :].rearrange("p (j t) -> p j t", j=KW), ACT.Copy).then_inc(s_["o_kept"], 1)

        @block.vector
        def _(dve):
            V = nc.vector
            V.memset(state[ALL], 0.0).then_inc(s_["s_kept"], 1)
            spread = lambda m, n: m.unsqueeze(1).broadcast_to([P, n, P])
            with dve.Fori(0, SB) as i:
                now = (slice(None), slice(None), ds(i * P, P))
                V.scalar_tensor_tensor(kr[:, :, 0, :], kk[now], -1.0, e_before[now], ALU.mult, ALU.mult)
                V.tensor_tensor(kr[:, :, 1, :], r[now], e_plus[now], ALU.mult)
                V.tensor_tensor(bh[ALL], b_[now], e_minus[now], ALU.mult)
                V.tensor_tensor(kh[ALL], k_[now], e_minus[now], ALU.mult).then_inc(s_["staged"], 1)
                for e in range(2):
                    for j in range(KW):
                        dve.wait_ge(s_["scored"], 8 * i + (4 * e + j + 1))
                        for kind, mask in enumerate((core.strict, core.upper)):
                            last = V.tensor_tensor(
                                scores[:, e, j, :, :].rearrange("p (a b) t -> p a b t", b=2)[:, :, kind, :],
                                psum[:, 3 + j, :].rearrange("p (a b t) -> p a b t", a=2, b=2)[:, :, kind, :],
                                spread(mask[:, :], 2), ALU.mult)
                        last.then_inc(s_["score_kept"], 1)
                    wait_alone(dve, s_["x_set"], i + 1)
                    dve.wait_ge(s_["score_kept"], 8 * i + (4 * e + 4))
                    V.copy_predicated(x[:, e, :, :], spread(masks[:, 0, 0, :], KW).bitcast(I32),
                                      psum[:, (7, 2)[e], :].rearrange("p (j t) -> p j t", j=KW))
                    V.copy_predicated(xt[:, e, :, :], spread(masks[:, 1, 0, :], KW).bitcast(I32),
                                      scores[:, e, :, 0, :]).then_inc(s_["x_made"], 1)
                for level in range(1, LEVELS):
                    for e in range(2):
                        wait_alone(dve, s_["q_made"], i * 2 * L1 + (2 * (level - 1) + e + 1))
                        if level < L1:
                            V.copy_predicated(x[:, e, :, :], spread(masks[:, 0, level, :], KW).bitcast(I32),
                                              psum[:, 3 * e + 1, :].rearrange("p (j t) -> p j t", j=KW))
                        V.copy_predicated(xt[:, e, :, :], spread(masks[:, 1, level, :], KW).bitcast(I32),
                                          psum[:, 3 * e + 2, :].rearrange("p (j t) -> p j t", j=KW))\
                            .then_inc(s_["x_made"], 1)
                dve.wait_ge(s_["s_made"], i + 1)
                for e in range(2):
                    V.tensor_tensor(state[half[e], :, :], state[half[e], :, :],
                                    psum[half[e], 4 + e, 0:256].rearrange("p (j d) -> p j d", j=KW), ALU.add)\
                        .then_inc(s_["s_sum"], 1)
                dve.wait_ge(s_["s_sum"], 2 * i + 2)
                V.tensor_tensor(state[ALL], state[ALL], core.growth[:, :, ds(i, 1)].broadcast_to([P, KW, 64]),
                                ALU.mult).then_inc(s_["s_kept"], 1)


def rwkv_finish(core):
    core.next_phase()
    nc, psum, o = core.nc, core.psum, core.o_t
    squares, rstd = core.e_plus, core.e_minus
    with ExitStack() as scope, nc.Block() as block:
        names = ("sums", "centred", "squares", "square_sums", "inverse", "rstd", "y_made", "merged_loaded")
        s_ = {n: core.sem("rf_" + n) for n in names}

        @block.sync
        def _(sp):
            sp.dma_start(core.rw_all[:, 0:2 * KD, :], core.merged_dram).then_inc(s_["merged_loaded"], 16)
            sp.wait_ge(s_["merged_loaded"], 16)

        @block.tensor
        def _(pe):
            for j in range(KW):
                last = nc.tensor.matmul(psum[:, j, :], core.pair_ones[:, :], o[:, j, :], start=True, stop=True)
            last.then_inc(s_["sums"], 1)
            pe.wait_ge(s_["squares"], 1)
            for j in range(KW):
                last = nc.tensor.matmul(psum[:, 4 + j, :], core.pair_ones[:, :], squares[:, j, :], start=True, stop=True)
            last.then_inc(s_["square_sums"], 1)

        @block.scalar
        def _(act):
            act.wait_ge(s_["centred"], 1)
            nc.scalar.activation(squares[ALL], o[ALL], ACT.Square).then_inc(s_["squares"], 1)
            act.wait_ge(s_["inverse"], 1)
            nc.scalar.activation(rstd[ALL], rstd[ALL], ACT.Sqrt).then_inc(s_["rstd"], 1)

        @block.vector
        def _(dve):
            V = nc.vector
            chain = Chain(core, dve, "dve_chain")
            dve.wait_ge(s_["sums"], 1)
            V.scalar_tensor_tensor(o[ALL], psum[:, 0:KW, :], -1.0 / 64, o[ALL], ALU.mult, ALU.add)\
                .then_inc(s_["centred"], 1)
            dve.wait_ge(s_["square_sums"], 1)
            chain(V.tensor_scalar(rstd[ALL], psum[:, KW:2 * KW, :], 1.0 / 64, GN_EPS, ALU.mult, ALU.add))
            V.reciprocal(rstd[ALL], rstd[ALL]).then_inc(s_["inverse"], 1)
            dve.wait_ge(s_["rstd"], 1)
            chain(V.tensor_tensor(o[ALL], o[ALL], rstd[ALL], ALU.mult))
            for j in range(KW):
                chain(V.tensor_scalar(o[:, j, :], o[:, j, :], core.param("lnx_w", j), core.param("lnx_b", j),
                                      ALU.mult, ALU.add))
            chain(V.tensor_tensor(o[ALL], o[ALL], core.bonus[ALL], ALU.add))
            V.tensor_tensor(core.rw["rw_g"][ALL], o[ALL], core.rw["rw_g"][ALL], ALU.mult).then_inc(s_["y_made"], 1)



def gate_two_branches(core):
    core.next_phase()
    nc, psum, st = core.nc, core.psum, core.st["gates"]
    x, y = (core.x_hi, core.x_lo), (core.y_conv, core.y_sb)
    total, third = core.rw_all[:, 0:KD, :], core.rw_all[:, KD:2 * KD, :]
    with ExitStack() as scope, nc.Block() as block:
        gate = scope.enter_context(nc.sbuf_tensor("g_gate", [P, 2, 2, S], F32))
        names = ("gates_mapped", "weighted", "stored")
        s_ = {n: core.sem("g_" + n) for n in names}
        done = core.chunk_done
        evac, evac0 = core.signals["dve_evac"].sem, core.signals["dve_evac"].take(KD)

        @block.sync
        def _(sp):
            load_stage(core, sp, st)
            sp.wait_ge(s_["stored"], 2 * KD * 16)

        @block.tensor
        def _(pe):
            for d, u, c in turns_of(pe, st):
                pe.wait_ge(core.w_split, c.number + 1)
                hi, lo = core.weights(c, 2, KD, P)
                for g in range(2):
                    for k in range(KD):
                        last = core.product(psum[:, g, :], (hi[:, g, k, :], lo[:, g, k, :]),
                                            (x[0][:, k, :], x[1][:, k, :]), k == 0, k == KD - 1)
                last.then_inc(done, 1)
                c = c.next()
                pe.wait_ge(core.w_split, c.number + 1)
                hi, lo = core.weights(c, KD, P)
                for k in range(KD):
                    last = core.product(psum[:, 2, :], (hi[:, k, :], lo[:, k, :]), (x[0][:, k, :], x[1][:, k, :]),
                                        k == 0, k == KD - 1)
                last.then_inc(done, 1)
                c = c.next()
                pe.wait_ge(core.w_split, c.number + 1)
                pe.wait_ge(evac, d + (evac0 - 1))
                hi, lo = core.weights(c, 2, KW, P)
                for g in range(2):
                    for k in range(KW):
                        last = core.product(psum[:, 3 + 2 * u + g, :], (hi[:, g, k, :], lo[:, g, k, :]),
                                            (y[g][0][:, k, :], y[g][1][:, k, :]), k == 0, k == KW - 1)
                pe.wait_ge(s_["gates_mapped"], 3 * d + 3)
                last.then_inc(done, 1)

        @block.scalar
        def _(act):
            nc.scalar.preload_act_table(ACT.Sigmoid)
            for d, u, c in turns_of(act, st):
                for g in range(3):
                    if g != 1:
                        act.wait_ge(done, c.number + (1 if g == 0 else 2))
                    if g == 0:
                        act.wait_ge(evac, d + (evac0 - 1))
                    out = third[:, one(d), :] if g == 2 else gate[:, u, g:g + 1, :]
                    nc.scalar.activation(out, psum[:, g:g + 1, :], ACT.Sigmoid,
                                         bias=core.param("gate_b", d + g * KD)).then_inc(s_["gates_mapped"], 1)
                act.wait_ge(s_["gates_mapped"], 3 * d + 3)
                nc.scalar.dma_start(core.merged_dram[:, ds(d + KD, 1), :], third[:, one(d), :]).then_inc(s_["stored"], 16)
                act.wait_ge(evac, d + (evac0 + 1))
                nc.scalar.dma_start(core.merged_dram[:, one(d), :], total[:, one(d), :]).then_inc(s_["stored"], 16)

        @block.vector
        def _(dve):
            V = nc.vector
            for d, u, c in turns_of(dve, st):
                core.split_chunk(dve, c.next())
                core.split_chunk(dve, c.next(2))
                core.split_chunk(dve, c.next(3))
                dve.wait_ge(s_["gates_mapped"], 3 * d + 2)
                dve.wait_ge(done, c.number + 3)
                for g in range(2):
                    V.tensor_tensor(gate[:, u, g, :], gate[:, u, g, :], psum[:, 3 + 2 * u + g, :], ALU.mult)\
                        .then_inc(s_["weighted"], 1)
                dve.wait_ge(s_["weighted"], 2 * d + 2)
                V.tensor_tensor(total[:, one(d), :], gate[:, u, 0:1, :], gate[:, u, 1:2, :], ALU.add).then_inc(evac, 1)



def pe_tiles(core, pe, st, x, tiles=2, shape=None, k_tiles=KD, evac="dve_evac", norm=None,
             order=None, late=None):
    signal = core.signals[evac]
    base = signal.taken
    if late is not None:
        sem, total, per = late
        pe.wait_ge(sem, total - 2)
    for s, u, c in turns_of(pe, st):
        pe.wait_ge(core.w_split, c.number + 1)
        pe.wait_ge(signal.sem, s + (base - 1))
        if shape == "gk":
            hi, lo = [w.rearrange("p g k m -> p k g m") for w in core.weights(c, tiles, k_tiles, P)]
        else:
            hi, lo = core.weights(c, k_tiles, tiles, P)
        ks = order or list(range(k_tiles))
        for k in ks:
            if norm is not None and k < KD and k % 2 == 0:
                norm.ready(pe, k)
            if late is not None and k in (k_tiles - 2 * per, k_tiles - per):
                pe.wait_ge(sem, total - 1 if k == k_tiles - 2 * per else total)
            for g in range(tiles):
                last = core.product(core.psum[:, 2 * u + g, 0:x[0].shape[2]], (hi[:, k, g, :], lo[:, k, g, :]),
                                    (x[0][:, k, :], x[1][:, k, :]), k == ks[0], k == ks[-1])
        last.then_inc(core.chunk_done, 1)


def add_to(core, dve, st, acc, tiles):
    signal = core.signals["dve_evac"]
    signal.take(st.steps)
    for s, u, c in turns_of(dve, st):
        core.split_chunk(dve, c.next())
        dve.wait_ge(core.chunk_done, c.number + 1)
        part = acc[:, ds(s * tiles, tiles), :]
        core.nc.vector.tensor_tensor(part, part, core.psum[:, 2 * u:2 * u + tiles, :], ALU.add).then_inc(signal.sem, 1)


def split_stage(core, dve, st):
    for s, u, c in turns_of(dve, st):
        core.split_chunk(dve, c.next())


def third_branch_and_mix(core):
    core.next_phase()
    nc, psum = core.nc, core.psum
    st, st_m = core.st["branch"], core.st["mix"]
    evac = core.signals["dve_evac"]
    total, third, y = core.rw_all[:, 0:KD, :], core.rw_all[:, KD:2 * KD, :], core.rw["rw_g"]
    with ExitStack() as scope, nc.Block() as block:
        sb = lambda name, shape, dt=F32: scope.enter_context(nc.sbuf_tensor(name, shape, dt))
        y_split = [sb("tb_y_hi", [P, KW, S], F32R), sb("tb_y_lo", [P, KW, S], F32R)]
        merged = [sb("tb_hi", [P, KD, S], F32R), sb("tb_lo", [P, KD, S], F32R)]
        names = ("y_hi_made", "y_split", "weighted", "summed", "hi_made", "split")
        s_ = {n: core.sem("tb_" + n) for n in names}

        @block.sync
        def _(sp):
            load_stage(core, sp, st)
            load_stage(core, sp, st_m)

        @block.tensor
        def _(pe):
            pe.wait_ge(s_["y_split"], KW)
            pe_tiles(core, pe, st, y_split, k_tiles=KW)
            evac.taken += st.steps
            pe_tiles(core, pe, st_m, merged, late=(s_["split"], st.steps, 2))
            evac.taken -= st.steps

        @block.scalar
        def _(act):
            for j in range(KW):
                nc.scalar.activation(y_split[0][:, j, :], y[:, j, :], ACT.Copy).then_inc(s_["y_hi_made"], 1)
            for s, u, c in turns_of(act, st):
                act.wait_ge(s_["summed"], s + 1)
                nc.scalar.activation(merged[0][:, ds(2 * s, 2), :], total[:, ds(2 * s, 2), :], ACT.Copy)\
                    .then_inc(s_["hi_made"], 1)

        @block.vector
        def _(dve):
            V = nc.vector
            for j in range(KW):
                dve.wait_ge(s_["y_hi_made"], j + 1)
                V.tensor_tensor(y_split[1][:, j, :], y[:, j, :], y_split[0][:, j, :].bitcast(F32), ALU.subtract)\
                    .then_inc(s_["y_split"], 1)
            evac.take(st.steps)
            for s, u, c in turns_of(dve, st):
                core.split_chunk(dve, c.next())
                dve.wait_ge(core.chunk_done, c.number + 1)
                tiles = ds(2 * s, 2)
                V.tensor_tensor(third[:, tiles, :], third[:, tiles, :], psum[:, 2 * u:2 * u + 2, :], ALU.mult)\
                    .then_inc(evac.sem, 1)
                dve.wait_ge(evac.sem, s + (evac.taken - st.steps + 1))
                V.tensor_tensor(total[:, tiles, :], total[:, tiles, :], third[:, tiles, :], ALU.add)\
                    .then_inc(s_["summed"], 1)
                dve.wait_ge(s_["hi_made"], s + 1)
                V.tensor_tensor(merged[1][:, tiles, :], total[:, tiles, :], merged[0][:, tiles, :].bitcast(F32),
                                ALU.subtract).then_inc(s_["split"], 1)
            add_to(core, dve, st_m, core.h, 2)



def memory_projections(core):
    core.next_phase()
    nc, psum = core.nc, core.psum
    st_q, st_k, st_v = (core.st[n] for n in ("ca_q", "ca_k", "ca_v"))
    with ExitStack() as scope, nc.Block() as block:
        sb = lambda name, shape, dt=F32: scope.enter_context(nc.sbuf_tensor(name, shape, dt))
        work, rstd = sb("cn_work", [P, KD, S]), sb("cn_rstd", [P, S])
        x = [sb("cn_x_hi", [P, KD, S], F32R), sb("cn_x_lo", [P, KD, S], F32R)]
        mx = [sb("cn_m_hi", [P, KD, MEM], F32R), sb("cn_m_lo", [P, KD, MEM], F32R)]
        rows, mem_t = sb("cn_mem_rows", [P, 2, D]), sb("cn_mem_t", [P, KD, MEM])
        mwork, mrstd = sb("cn_m_work", [P, KD, MEM]), sb("cn_m_rstd", [P, MEM])
        loaded, turned, kept, v_kept = (core.sem("cn_" + n) for n in ("loaded", "turned", "kept", "v_kept"))
        norm = Norm(core, core.h, work, rstd, "norm_ca", *x)
        norm_m = Norm(core, mem_t, mwork, mrstd, "norm_mem", *mx, width=MEM, bank=6)

        @block.sync
        def _(sp):
            sp.dma_start(rows[ALL], core.a["mem"][0].rearrange("(b p) d -> p b d", p=P)).then_inc(loaded, 16)
            for st in (st_q, st_k, st_v):
                load_stage(core, sp, st)

        @block.tensor
        def _(pe):
            norm.pe(pe)
            pe.wait_ge(loaded, 16)
            for k in range(KD):
                for b in range(2):
                    last = nc.tensor.transpose(psum[:, k // 2, k % 2 * MEM + b * P:k % 2 * MEM + (b + 1) * P],
                                               rows[:, b, k * P:(k + 1) * P], core.ident[:, :])
            last.then_inc(turned, 1)
            norm_m.pe(pe)
            pe.wait_ge(kept, 1)
            pe_tiles(core, pe, st_q, x, norm=norm)
            core.signals["dve_evac"].taken += st_q.steps
            pe_tiles(core, pe, st_k, mx, norm=norm_m)
            core.signals["dve_evac"].taken -= st_q.steps
            for s, u, c in turns_of(pe, st_v):
                pe.wait_ge(core.w_split, c.number + 1)
                pe.wait_ge(core.signals["act_evac"].sem, s + (core.signals["act_evac"].taken - 1))
                w = core.weights(c, KD, 256)
                for b in range(2):
                    for k in range(KD):
                        mb = [t[:, k, b * P:(b + 1) * P] for t in mx]
                        last = core.product(psum[:, 4 + u, b * 256:(b + 1) * 256], mb, (w[0][:, k, :], w[1][:, k, :]),
                                            k == 0, k == KD - 1)
                last.then_inc(core.chunk_done, 1)

        @block.scalar
        def _(act):
            norm.act(act)
            act.wait_ge(kept, 1)
            norm_m.act(act)
            signal = core.signals["act_evac"]
            signal.take(st_v.steps)
            for s, u, c in turns_of(act, st_v):
                act.wait_ge(core.chunk_done, c.number + 1)
                nc.scalar.activation(core.ca_v[:, :, ds(s * 256, 256)],
                                     psum[:, 4 + u, :].rearrange("p (b c) -> p b c", b=2), ACT.Copy)\
                    .then_inc(signal.sem, 1)

        @block.vector
        def _(dve):
            norm.dve(dve)
            dve.wait_ge(turned, 1)
            nc.vector.tensor_copy(mem_t[ALL], psum[:, 0:4, :].rearrange("p a (b c) -> p (a b) c", b=2)).then_inc(kept, 1)
            norm_m.dve(dve)
            signal = core.signals["dve_evac"]
            for st, out, scale in ((st_q, core.ca_q, 0.0625), (st_k, core.ca_k, 1.0)):
                signal.take(st.steps)
                for s, u, c in turns_of(dve, st):
                    core.split_chunk(dve, c.next())
                    dve.wait_ge(core.chunk_done, c.number + 1)
                    nc.vector.tensor_scalar(out[:, ds(2 * s, 2), :], psum[:, 2 * u:2 * u + 2, 0:out.shape[2]], scale,
                                            None, ALU.mult).then_inc(signal.sem, 1)
            split_stage(core, dve, st_v)


def memory_attention(core):
    core.next_phase()
    nc, psum = core.nc, core.psum
    heads = 4
    with ExitStack() as scope, nc.Block() as block:
        sb = lambda name, shape, dt=F32: scope.enter_context(nc.sbuf_tensor(name, shape, dt))
        prob = sb("ca_prob", [P, 2, SB, MEM])
        prob_t = sb("ca_prob_t", [P, 2, 2, S])
        out = sb("ca_out", [P, KD, S])
        top, total = sb("ca_top", [P, 2, SB]), sb("ca_total", [P, 2, SB])
        names = ("scored", "top_made", "exps", "inverse", "scaled", "turned", "turned_kept", "out_made", "out_kept",
                 "hi_made", "split")
        s_ = {n: core.sem("ca_" + n) for n in names}

        @block.tensor
        def _(pe):
            def scores(h):
                if h >= 2:
                    pe.wait_ge(s_["exps"], SB * (h - 1))
                for b in range(SB):
                    for k in range(2):
                        last = nc.tensor.matmul(psum[:, 2 * (h % 2) + b // 2, b % 2 * MEM:(b % 2 + 1) * MEM],
                                                core.ca_q[:, 2 * h + k, b * P:(b + 1) * P], core.ca_k[:, 2 * h + k, :],
                                                start=k == 0, stop=k == 1)
                last.then_inc(s_["scored"], 1)

            scores(0)
            for h in range(heads):
                if h + 1 < heads:
                    scores(h + 1)
                pe.wait_ge(s_["scaled"], SB * (h + 1))
                if h:
                    pe.wait_ge(s_["turned_kept"], 2 * h)
                for m in range(2):
                    for b in range(SB):
                        last = nc.tensor.transpose(psum[:, 4 + m, b * P:(b + 1) * P],
                                                   prob[:, h % 2, b, m * P:(m + 1) * P], core.ident[:, :])
                    last.then_inc(s_["turned"], 1)
                pe.wait_ge(s_["turned_kept"], 2 * h + 2)
                if h:
                    pe.wait_ge(s_["out_kept"], h)
                for d in range(2):
                    for m in range(2):
                        last = nc.tensor.matmul(psum[:, 6 + d, :], core.ca_v[:, m, (2 * h + d) * P:(2 * h + d + 1) * P],
                                                prob_t[:, h % 2, m, :], start=m == 0, stop=m == 1)
                last.then_inc(s_["out_made"], 1)

        @block.scalar
        def _(act):
            nc.scalar.preload_act_table(ACT.Exp)
            for h in range(heads):
                act.wait_ge(s_["top_made"], h + 1)
                if h >= 2:
                    act.wait_ge(s_["turned"], 2 * (h - 1))
                for b in range(SB):
                    nc.scalar.activation(prob[:, h % 2, b, :],
                                         psum[:, 2 * (h % 2) + b // 2, b % 2 * MEM:(b % 2 + 1) * MEM], ACT.Exp,
                                         bias=top[:, h % 2, b:b + 1], accum_out=total[:, h % 2, b:b + 1])\
                        .then_inc(s_["exps"], 1)
                if h:
                    act.wait_ge(s_["out_made"], h)
                    nc.scalar.activation(out[:, 2 * h - 2:2 * h, :], psum[:, 6:8, :], ACT.Copy).then_inc(s_["out_kept"], 1)
            act.wait_ge(s_["out_made"], heads)
            nc.scalar.activation(out[:, 2 * heads - 2:2 * heads, :], psum[:, 6:8, :], ACT.Copy).then_inc(s_["out_kept"], 1)
            act.wait_ge(s_["out_kept"], heads)
            nc.scalar.activation(core.m_hi[ALL], out[ALL], ACT.Copy).then_inc(s_["hi_made"], 1)

        @block.vector
        def _(dve):
            V = nc.vector
            chain = Chain(core, dve, "dve_chain")

            def maxima(h):
                dve.wait_ge(s_["scored"], h + 1)
                if h >= 2:
                    dve.wait_ge(s_["exps"], SB * (h - 1))
                u = h % 2
                chain(V.tensor_reduce(top[:, u, :], psum[:, 2 * u:2 * u + 2, :].rearrange("p a (b c) -> p (a b) c", b=2),
                                      AX.X, ALU.max))
                V.tensor_scalar(top[:, u, :], top[:, u, :], -1.0, None, ALU.mult).then_inc(s_["top_made"], 1)

            maxima(0)
            for h in range(heads):
                if h + 1 < heads:
                    maxima(h + 1)
                u = h % 2
                dve.wait_ge(s_["exps"], SB * (h + 1))
                chain(V.reciprocal(total[:, u, :], total[:, u, :]))
                for b in range(SB):
                    V.tensor_scalar(prob[:, u, b, :], prob[:, u, b, :], total[:, u, b:b + 1], None, ALU.mult)\
                        .then_inc(s_["scaled"], 1)
                for m in range(2):
                    dve.wait_ge(s_["turned"], 2 * h + m + 1)
                    V.tensor_copy(prob_t[:, u, m, :], psum[:, 4 + m, :]).then_inc(s_["turned_kept"], 1)
            dve.wait_ge(s_["hi_made"], 1)
            V.tensor_tensor(core.m_lo[ALL], out[ALL], core.m_hi[ALL].bitcast(F32), ALU.subtract).then_inc(s_["split"], 1)


def memory_out(core):
    core.next_phase()
    with core.nc.Block() as block:
        st = core.st["ca_o"]

        @block.sync
        def _(sp):
            load_stage(core, sp, st)

        @block.tensor
        def _(pe):
            pe_tiles(core, pe, st, (core.m_hi, core.m_lo))

        @block.vector
        def _(dve):
            add_to(core, dve, st, core.h, 2)



def ffn(core):
    core.next_phase()
    nc, psum = core.nc, core.psum
    with ExitStack() as scope, nc.Block() as block:
        sb = lambda name, shape, dt=F32: scope.enter_context(nc.sbuf_tensor(name, shape, dt))
        work, rstd = sb("fn_work", [P, KD, S]), sb("fn_rstd", [P, S])
        x = [sb("fn_x_hi", [P, KD, S], F32R), sb("fn_x_lo", [P, KD, S], F32R)]
        hid = [sb("fn_hid_hi", [P, HF, S], F32R), sb("fn_hid_lo", [P, HF, S], F32R)]
        taps, hidden = sb("fn_taps", [P, 2, 2, S]), sb("fn_hidden", [P, 2, S])
        names = ("first_taps", "second_taps", "third_taps", "silu", "hidden_made", "hi_made", "split")
        s_ = {n: core.sem("fn_" + n) for n in names}
        norm = Norm(core, core.h, work, rstd, "norm_ffn", *x)
        evac = core.signals["dve_evac"]
        done = core.chunk_done

        @block.sync
        def _(sp):
            for h in range(2):
                load_stage(core, sp, core.st[f"ffn_up{h}"])
                load_stage(core, sp, core.st[f"ffn_down{h}"])

        @block.tensor
        def _(pe):
            norm.pe(pe)
            before = evac.taken
            for h in range(2):
                pe_tiles(core, pe, core.st[f"ffn_up{h}"], x, shape="gk", norm=norm)
                evac.taken += HF
                pe.wait_ge(s_["split"], HF * (h + 1))
                pe_tiles(core, pe, core.st[f"ffn_down{h}"], hid, tiles=1, k_tiles=HF)
                evac.taken += KD
            evac.taken = before

        @block.scalar
        def _(act):
            norm.act(act)
            for h in range(2):
                st = core.st[f"ffn_up{h}"]
                for j, u, c in turns_of(act, st):
                    act.wait_ge(done, c.number + 1)
                    for g in range(2):
                        at = j + (g * 2 * HF + h * HF)
                        nc.scalar.activation(taps[:, u, g, :], psum[:, 2 * u + g, :], ACT.Identity,
                                             scale=core.param("ffn_conv_w", at + 4 * 2 * HF),
                                             bias=core.param("ffn_conv_b", at)).then_inc(s_["first_taps"], 1)
                    act.wait_ge(s_["third_taps"], 2 * j + (2 * HF * h + 1))
                    nc.scalar.activation(taps[:, u, 0, :], taps[:, u, 0, :], ACT.Silu).then_inc(s_["silu"], 1)
                    act.wait_ge(s_["hidden_made"], j + (HF * h + 1))
                    nc.scalar.activation(hid[0][:, one(j), :], hidden[:, one(u), :], ACT.Copy).then_inc(s_["hi_made"], 1)

        @block.vector
        def _(dve):
            V = nc.vector
            norm.dve(dve)
            for h in range(2):
                st = core.st[f"ffn_up{h}"]
                base = evac.take(HF)
                for j, u, c in turns_of(dve, st):
                    core.split_chunk(dve, c.next())
                    for g in range(2):
                        at = j + (g * 2 * HF + h * HF)
                        n = 2 * j + (2 * HF * h + g + 1)
                        dve.wait_ge(s_["first_taps"], n)
                        V.scalar_tensor_tensor(taps[:, u, g, 1:], psum[:, 2 * u + g, 0:S - 1],
                                               core.param("ffn_conv_w", at + 2 * 2 * HF), taps[:, u, g, 1:],
                                               ALU.mult, ALU.add).then_inc(s_["second_taps"], 1)
                        dve.wait_ge(s_["second_taps"], n)
                        V.scalar_tensor_tensor(taps[:, u, g, 2:], psum[:, 2 * u + g, 0:S - 2],
                                               core.param("ffn_conv_w", at), taps[:, u, g, 2:],
                                               ALU.mult, ALU.add).then_inc(s_["third_taps"], 1)
                    dve.wait_ge(s_["third_taps"], 2 * j + (2 * HF * h + 2))
                    dve.wait_ge(s_["silu"], j + (HF * h + 1))
                    V.tensor_tensor(hidden[:, u, :], taps[:, u, 0, :], taps[:, u, 1, :], ALU.mult)\
                        .then_inc(s_["hidden_made"], 1)
                    dve.wait_ge(s_["hi_made"], j + (HF * h + 1))
                    V.tensor_tensor(hid[1][:, one(j), :], hidden[:, one(u), :], hid[0][:, one(j), :].bitcast(F32),
                                    ALU.subtract).then_inc(s_["split"], 1)
                    dve.wait_ge(s_["split"], j + (HF * h + 1))
                    V.memset(core.scrap[:, 0:1], 0.0).then_inc(evac.sem, 1)
                add_to(core, dve, core.st[f"ffn_down{h}"], core.h, 1)



HEADS2, WIDE = 16, 3 * P


def input_projections(core):
    core.next_phase()
    nc, psum = core.nc, core.psum
    st_x, st_z, st_q, st_r = (core.st[n] for n in ("xbc", "z", "q2", "kvdt"))
    with ExitStack() as scope, nc.Block() as block:
        sb = lambda name, shape, dt=F32: scope.enter_context(nc.sbuf_tensor(name, shape, dt))
        work, rstd = sb("in_work", [P, KD, S]), sb("in_rstd", [P, S])
        x = [sb("in_x_hi", [P, KD, S], F32R), sb("in_x_lo", [P, KD, S], F32R)]
        k_t, skip_all = sb("in_k", [P, 2, S]), sb("in_skip_all", [P, HEADS2])
        final = Norm(core, core.h, work, rstd, "norm_final", dest=core.h)
        norm = Norm(core, core.h, work, rstd, "norm_mix_pre_2", *x)
        conv = work
        offsets = core.offsets
        names = ("tap_2", "taps", "xbc_made", "rest_kept", "k_placed", "offsets_made", "bias_made", "bias_masked",
                 "slopes_made", "broadcast")
        s_ = {n: core.sem("in_" + n) for n in names}
        done = core.chunk_done
        dsig, asig = core.signals["dve_evac"], core.signals["act_evac"]

        @block.sync
        def _(sp):
            sp.dma_start(core.dt_bias[:, :], core.a["dt_bias_2"].rearrange("a b c -> a (b c)")[0].partition_broadcast(P))\
                .then_inc(s_["broadcast"], 16)
            sp.dma_start(core.a_log[:, :], core.a["a_log_2"].rearrange("a b c -> a (b c)")[0].partition_broadcast(P))\
                .then_inc(s_["broadcast"], 16)
            sp.dma_start(core.sink[:, :], core.a["attn_sink_2"][0].partition_broadcast(P)).then_inc(s_["broadcast"], 16)
            sp.dma_start(skip_all[:, :], core.a["d_skip_2"][0].partition_broadcast(P)).then_inc(s_["broadcast"], 16)
            for st in (st_x, st_z, st_q, st_r):
                load_stage(core, sp, st)
            sp.wait_ge(s_["rest_kept"], 1)
            for g in range(4):
                for e in range(2):
                    sp.dma_start(core.k2[64 * e:64 * e + 64, g, :], k_t[64 * (g % 2):64 * (g % 2) + 64, g // 2, :])\
                        .then_inc(s_["k_placed"], 16)
            sp.wait_ge(s_["k_placed"], 128)

        @block.gpsimd
        def _(pool):
            nc.gpsimd.iota(offsets[:, :], pattern=[[1, WIDE]], base=-P, channel_multiplier=-1)\
                .then_inc(s_["offsets_made"], 1)
            for h in range(HEADS2):
                nc.gpsimd.memset(core.slopes[:, h:h + 1], float(2.0 ** (-8.0 * (h + 1) / HEADS2)))\
                    .then_inc(s_["slopes_made"], 1)
            pool.wait_ge(s_["bias_made"], 1)
            nc.gpsimd.affine_select(out=core.distance[:, :], in_=core.distance[:, :], compare_op=ALU.is_ge, fill=-1e30,
                                    base=0, pattern=[[1, WIDE]], channel_multiplier=-1).then_inc(s_["bias_masked"], 1)
            pool.wait_ge(s_["bias_masked"], 1)
            nc.gpsimd.affine_select(out=core.distance[:, :], in_=core.distance[:, :], compare_op=ALU.is_ge, fill=-1e30,
                                    base=2 * P, pattern=[[-1, WIDE]], channel_multiplier=1)\
                .then_inc(s_["bias_masked"], 1)

        @block.tensor
        def _(pe):
            final.pe(pe)
            norm.pe(pe)
            at = dsig.taken
            pe_tiles(core, pe, st_x, x, norm=norm)
            pe.wait_ge(dsig.sem, at + st_x.steps)
            pe_tiles(core, pe, st_z, x, evac="act_evac")
            pe.wait_ge(asig.sem, asig.taken + st_z.steps)
            dsig.taken += st_x.steps
            pe_tiles(core, pe, st_q, x)
            dsig.taken -= st_x.steps
            pe.wait_ge(dsig.sem, at + st_x.steps + st_q.steps)
            for s, u, c in turns_of(pe, st_r):
                pe.wait_ge(core.w_split, c.number + 1)
                w = core.weights(c, KD, *((2, P), (256,), (P,))[s])
                for g in range((2, SB, 1)[s]):
                    for k in range(KD):
                        xk = [t[:, k, :] for t in x]
                        if s == 0:
                            args = psum[:, g, :], [t[:, k, g, :] for t in w], xk
                        elif s == 1:
                            args = (psum[:, 2 + g // 2, g % 2 * 256:g % 2 * 256 + 256],
                                    [t[:, k, g * P:(g + 1) * P] for t in x], [t[:, k, :] for t in w])
                        else:
                            args = psum[:, 4, :], [t[:, k, :] for t in w], xk
                        last = core.product(*args, k == 0, k == KD - 1)
                last.then_inc(done, 1)

        @block.scalar
        def _(act):
            A = nc.scalar.activation
            final.act(act)
            act.wait_ge(core.signals["normed"].sem, final.normed + KD)
            norm.act(act)
            for s, u, c in turns_of(act, st_x):
                act.wait_ge(done, c.number + 1)
                for g in range(2):
                    at = 2 * s + g
                    A(conv[:, 2 * u + g, :], psum[:, 2 * u + g, :], ACT.Identity,
                      scale=core.param("conv_w_2", at + 2 * 12), bias=core.param("conv_b_2", at))\
                        .then_inc(s_["tap_2"], 1)
                for g in range(2):
                    act.wait_ge(s_["taps"], 8 * s + 4 * g + 4)
                    A(core.xbc[:, ds(2 * s + g, 1), :], conv[:, one(2 * u + g), :], ACT.Silu).then_inc(s_["xbc_made"], 1)
            asig.take(st_z.steps)
            for s, u, c in turns_of(act, st_z):
                act.wait_ge(done, c.number + 1)
                A(core.z[:, ds(2 * s, 2), :], psum[:, 2 * u:2 * u + 2, :], ACT.Silu).then_inc(asig.sem, 1)
            act.wait_ge(done, st_r.base + 1)
            A(k_t[ALL], psum[:, 0:2, :], ACT.Copy).then_inc(s_["rest_kept"], 1)
            act.wait_ge(done, st_r.base + 2)
            A(core.v2[ALL], psum[:, 2:4, :].rearrange("p a (b c) -> p (a b) c", b=2), ACT.Copy)\
                .then_inc(s_["rest_kept"], 1)
            act.wait_ge(done, st_r.base + 3)
            A(core.dt_t[:, :], psum[0:32, 4, :], ACT.Copy).then_inc(s_["rest_kept"], 1)

        @block.vector
        def _(dve):
            V = nc.vector
            chain = Chain(core, dve, "dve_chain")
            final.dve(dve)
            norm.dve(dve)
            dve.wait_ge(s_["offsets_made"], 1)
            chain(V.tensor_copy(core.distance[:, :], offsets[:, :]))
            V.scalar_tensor_tensor(core.distance[:, :], core.distance[:, :], -1.0, core.distance[:, :], ALU.mult, ALU.min)\
                .then_inc(s_["bias_made"], 1)
            dsig.take(st_x.steps)
            for s, u, c in turns_of(dve, st_x):
                core.split_chunk(dve, c.next())
                for g in range(2):
                    dve.wait_ge(s_["tap_2"], 2 * s + g + 1)
                    p, out = psum[:, 2 * u + g, :], conv[:, 2 * u + g, :]
                    for n, tap in enumerate((0, 1, 3, 4)):
                        lag = 2 - tap
                        dst, src = (out[:, lag:], p[:, 0:S - lag]) if lag > 0 else (out[:, 0:S + lag], p[:, -lag:])
                        V.scalar_tensor_tensor(dst, src, core.param("conv_w_2", 2 * s + (g + 12 * tap)), dst,
                                               ALU.mult, ALU.add).then_inc(s_["taps"], 1)
                        dve.wait_ge(s_["taps"], 8 * s + 4 * g + n + 1)
                V.memset(core.scrap[:, 0:1], 0.0).then_inc(dsig.sem, 1)
            split_stage(core, dve, st_z)
            dsig.take(st_q.steps)
            for s, u, c in turns_of(dve, st_q):
                core.split_chunk(dve, c.next())
                dve.wait_ge(done, c.number + 1)
                V.tensor_scalar(core.q2[:, ds(2 * s, 2), :], psum[:, 2 * u:2 * u + 2, :], 0.125, None, ALU.mult)\
                    .then_inc(dsig.sem, 1)
            split_stage(core, dve, st_r)
            dve.wait_ge(s_["broadcast"], 64)
            by_head = skip_all[:, :].rearrange("p (j e) -> p e j", e=2)
            for e in range(2):
                half = slice(64 * e, 64 * e + 64)
                V.tensor_copy(core.d_skip[half, :], by_head[half, e, :])



R2 = 2 * HEADS2


def ssd_prepare(core):
    core.next_phase()
    nc, psum = core.nc, core.psum
    with ExitStack() as scope, nc.Block() as block:
        sb = lambda name, shape, dt=F32: scope.enter_context(nc.sbuf_tensor(name, shape, dt))
        raw, soft, a_ = sb("sp_raw", [P, SB, R2]), sb("sp_soft", [P, SB, R2]), sb("sp_a", [P, SB, R2])
        names = ("turned", "biased", "abs", "exp", "log", "a_exp", "a_made", "sums", "sums_kept", "sums_turned",
                 "decay_arg", "decay_exp", "chunk_exp", "sums_hi_made")
        s_ = {n: core.sem("sp_" + n) for n in names}

        @block.tensor
        def _(pe):
            for c in range(SB):
                last = nc.tensor.transpose(psum[:, 0, c * R2:(c + 1) * R2], core.dt_t[:, c * P:(c + 1) * P],
                                           core.ident[0:R2, 0:R2])
            last.then_inc(s_["turned"], 1)
            pe.wait_ge(s_["a_made"], 1)
            mm = nc.tensor.matmul
            mm(psum[:, 1, 0:64], core.upper[:, :], a_[:, :, 0:HEADS2], start=True, stop=True)
            mm(psum[:, 1, 64:128], core.lower[:, :], a_[:, :, HEADS2:R2], start=True, stop=True)
            mm(psum[:, 1, 128:256], core.ones[:, :], a_[ALL], start=True, stop=True).then_inc(s_["sums"], 1)
            pe.wait_ge(s_["sums_kept"], 1)
            for c in range(SB):
                last = nc.tensor.transpose(psum[0:R2, 2, c * P:(c + 1) * P], core.sums[:, c, :], core.ident[:, :])
            last.then_inc(s_["sums_turned"], 1)

        @block.scalar
        def _(act):
            A = nc.scalar.activation
            A(core.a_log[:, :], core.a_log[:, :], ACT.Exp).then_inc(s_["a_exp"], 1)
            act.wait_ge(s_["biased"], 1)
            A(soft[ALL], raw[ALL], ACT.Abs).then_inc(s_["abs"], 1)
            act.wait_ge(s_["abs"], 1)
            A(soft[ALL], soft[ALL], ACT.Exp, scale=-1.0).then_inc(s_["exp"], 1)
            act.wait_ge(s_["exp"], 1)
            A(soft[ALL], soft[ALL], ACT.Ln, bias=1.0).then_inc(s_["log"], 1)
            act.wait_ge(s_["decay_arg"], 1)
            A(core.state_weight[ALL], core.state_weight[ALL], ACT.Exp).then_inc(s_["decay_exp"], 1)
            A(core.chunk_decay[ALL], core.chunk_decay[ALL], ACT.Exp).then_inc(s_["chunk_exp"], 1)
            act.wait_ge(s_["sums_turned"], 1)
            A(core.sums_t[0][:, :], psum[0:R2, 2, :], ACT.Copy).then_inc(s_["sums_hi_made"], 1)

        @block.vector
        def _(dve):
            V = nc.vector
            chain = Chain(core, dve, "dve_chain")
            dve.wait_ge(s_["turned"], 1)
            V.tensor_tensor(raw[ALL], psum[:, 0, 0:SB * R2].rearrange("p (c r) -> p c r", c=SB),
                            core.dt_bias[:, :].unsqueeze(1).broadcast_to([P, SB, R2]), ALU.add).then_inc(s_["biased"], 1)
            dve.wait_ge(s_["log"], 1)
            dve.wait_ge(s_["biased"], 1)
            chain(V.scalar_tensor_tensor(core.dt[ALL], raw[ALL], 0.0, soft[ALL], ALU.max, ALU.add))
            dve.wait_ge(s_["a_exp"], 1)
            V.scalar_tensor_tensor(a_[ALL], core.dt[ALL], -1.0, core.a_log[:, :].unsqueeze(1).broadcast_to([P, SB, R2]),
                                   ALU.mult, ALU.mult).then_inc(s_["a_made"], 1)
            dve.wait_ge(s_["sums"], 1)
            for part in range(2):
                last = V.tensor_copy(core.sums[:, :, part * HEADS2:(part + 1) * HEADS2],
                                     psum[:, 1, part * 64:part * 64 + 64].rearrange("p (c r) -> p c r", c=SB))
            last.then_inc(s_["sums_kept"], 1)
            chain(V.tensor_copy(core.chunk_decay[ALL], psum[:, 1, 128:256].rearrange("p (c r) -> p c r", c=SB)))
            dve.wait_ge(s_["sums_kept"], 1)
            V.tensor_tensor(core.state_weight[ALL], core.chunk_decay[ALL], core.sums[ALL], ALU.subtract)\
                .then_inc(s_["decay_arg"], 1)
            dve.wait_ge(s_["decay_exp"], 1)
            chain(V.tensor_tensor(core.state_weight[ALL], core.state_weight[ALL], core.dt[ALL], ALU.mult))
            dve.wait_ge(s_["sums_hi_made"], 1)
            chain(V.tensor_tensor(core.sums_t[1][:, :], psum[0:R2, 2, :], core.sums_t[0][:, :].bitcast(F32), ALU.subtract))


def ssd(core):
    core.next_phase()
    nc, psum, mm = core.nc, core.psum, core.nc.tensor.matmul
    with ExitStack() as scope, nc.Block() as block:
        sb = lambda name, shape, dt=F32: scope.enter_context(nc.sbuf_tensor(name, shape, dt))
        select = sb("ss_select", [R2, 2, 2, 2, P], F32R)
        x_t, x_rows = sb("ss_x_t", [P, 2, S]), sb("ss_x_rows", [P, 2, SB, P])
        spare = core.w_raw[Chunk(core.st["out2"].base).slot]
        grown = [spare[:, :].rearrange("p (q s) -> p q s", q=4), sb("ss_grown", [P, 4, S])]
        inner = sb("ss_inner", [P, 2, 4, S])
        cb = sb("ss_cb", [P, 2, 2, SB, P])
        b_rows = sb("ss_b_rows", [P, 2, SB, P])
        x_weighed = sb("ss_x_weighed", [P, 2, SB, P])
        prev = sb("ss_prev", [P, 2, SB, P])
        y = sb("ss_y", [P, S])
        names = ("cb_made", "cb_kept", "b_kept", "staged", "spread", "x_turned", "x_kept", "grown_exp", "diffs",
                 "inner_exp", "grown_made", "weighed", "x_weighed", "states", "prev_steps", "prev_made",
                 "inner_made", "y_made", "states_read", "y_read", "y_kept")
        s_ = {n: core.sem("ss_" + n) for n in names}
        per_g = KD // 2

        def tiles_of(engine):
            with engine.Fori(0, per_g // 2) as i:
                for u in range(2):
                    yield 2 * i + u, u, 0, True
            for t in range(per_g, KD):
                yield t, t % 2, 1, t + 1 < KD

        @block.tensor
        def _(pe):
            for g in range(2):
                b_t, c_t = core.xbc[:, KD + g, :], core.xbc[:, KD + 2 + g, :]
                for c in range(SB):
                    part = slice(c * P, (c + 1) * P)
                    mm(psum[:, 1 + 2 * g, part], b_t[:, part], c_t[:, part], start=True, stop=True)
                    last = nc.tensor.transpose(psum[:, 2 + 2 * g, part], b_t[:, part], core.ident[:, :])
                last.then_inc(s_["cb_made"], 1)
            pe.wait_ge(s_["cb_kept"], 2)
            pe.wait_ge(s_["b_kept"], 2)

            def spread(t, u):
                pe.wait_ge(s_["staged"], t + 1)
                for c in range(SB):
                    last = nc.tensor.transpose(psum[:, 0, c * P:(c + 1) * P], x_t[:, u, c * P:(c + 1) * P],
                                               core.ident[:, :])
                last.then_inc(s_["x_turned"], 1)
                for q in range(4):
                    rows = select[:, u, q // 2, q % 2, :]
                    mm(psum[:, 1 + q, :], rows, core.sums_t[0][:, :], start=True, stop=False)
                    mm(psum[:, 1 + q, :], rows, core.sums_t[1][:, :], start=False, stop=True).then_inc(s_["spread"], 1)

            spread(0, 0)
            for t, u, g, more in tiles_of(pe):
                pe.wait_ge(s_["x_weighed"], 2 * t + 2)
                for way in range(2):
                    for c in (range(0, SB - 1) if way == 0 else range(1, SB)):
                        last = mm(psum[:, 5 + way, c * P:(c + 1) * P], b_rows[:, g, c, :], x_weighed[:, way, c, :],
                                  start=True, stop=True)
                last.then_inc(s_["states"], 1)
                if more:
                    pe.wait_ge(s_["grown_exp"], 4 * t + 4)
                    spread(t + 1, 1 - u)
                pe.wait_ge(s_["inner_made"], 2 * t + 2)
                pe.wait_ge(s_["grown_made"], 4 * t + 4)
                pe.wait_ge(s_["prev_made"], t + 1)
                pe.wait_ge(s_["y_read"], t + 1)
                for e in range(2):
                    rows = slice(64 * e, 64 * e + 64)
                    for c in range(SB):
                        out, part = psum[rows, 7, c * P:(c + 1) * P], slice(c * P, (c + 1) * P)
                        mm(out, x_rows[:, u, c, rows], inner[:, u, e, part], start=True, stop=False)
                        if c > 0:
                            last = mm(out, prev[:, 0, c, rows], grown[u][:, e, part], start=False, stop=c == SB - 1)
                        if c < SB - 1:
                            last = mm(out, prev[:, 1, c, rows], grown[u][:, 2 + e, part], start=False, stop=True)
                last.then_inc(s_["y_made"], 1)

        @block.scalar
        def _(act):
            A = nc.scalar.activation
            nc.scalar.preload_act_table(ACT.Exp)

            def stage(t, u):
                for way in range(2):
                    A(select[:, u, way, :, :],
                      core.ident[0:R2, ds(2 * t + HEADS2 * way, 2)].unsqueeze(2).broadcast_to([R2, 2, P]), ACT.Copy)
                A(x_t[:, u:u + 1, :], core.xbc[:, one(t), :], ACT.Copy).then_inc(s_["staged"], 1)

            def exps(t, u):
                act.wait_ge(s_["x_turned"], t + 1)
                A(x_rows[:, u, :, :], psum[:, 0, :].rearrange("p (c n) -> p c n", c=SB), ACT.Copy)\
                    .then_inc(s_["x_kept"], 1)
                for q in range(4):
                    act.wait_ge(s_["diffs"], 4 * t + (q + 1))
                    A(inner[:, u, q, :], inner[:, u, q, :], ACT.Exp).then_inc(s_["inner_exp"], 1)
                    A(grown[u][:, q, :], psum[:, 1 + q, :], ACT.Exp).then_inc(s_["grown_exp"], 1)

            stage(0, 0)
            for g in range(2):
                act.wait_ge(s_["cb_made"], g + 1)
                A(b_rows[:, g, :, :], psum[:, 2 + 2 * g, :].rearrange("p (c n) -> p c n", c=SB), ACT.Copy)\
                    .then_inc(s_["b_kept"], 1)
            exps(0, 0)
            for t, u, g, more in tiles_of(act):
                if more:
                    act.wait_ge(s_["y_read"], t + 1)
                    stage(t + 1, 1 - u)
                    exps(t + 1, 1 - u)

        @block.gpsimd
        def _(pool):
            for t, u, g, more in tiles_of(pool):
                pool.wait_ge(s_["x_kept"], t + 1)
                pool.wait_ge(s_["states_read"], t + 1)
                for way in range(2):
                    weight = core.state_weight[:, :, ds(2 * t + HEADS2 * way, 2)].unsqueeze(3)
                    nc.gpsimd.tensor_tensor(x_weighed[:, way, :, :].rearrange("p c (e d) -> p c e d", e=2),
                                            x_rows[:, u, :, :].rearrange("p c (e d) -> p c e d", e=2),
                                            weight.broadcast_to([P, SB, 2, 64]), ALU.mult).then_inc(s_["x_weighed"], 1)
                for q in range(4):
                    pool.wait_ge(s_["grown_exp"], 4 * t + (q + 1))
                    nc.gpsimd.tensor_tensor(grown[u][:, q, :], grown[u][:, q, :], core.xbc[:, KD + 2 + g, :], ALU.mult)\
                        .then_inc(s_["grown_made"], 1)

        @block.vector
        def _(dve):
            V = nc.vector
            V.memset(core.scrap[:, 0:1], 0.0).then_inc(s_["y_read"], 1)
            V.memset(core.scrap[:, 1:2], 0.0).then_inc(s_["states_read"], 1)
            row = lambda v, t, c, way, e: v[:, c, ds(2 * t + (HEADS2 * way + e), 1)]
            for g in range(2):
                dve.wait_ge(s_["cb_made"], g + 1)
                for way, mask in enumerate((core.upper, core.lower)):
                    last = V.tensor_tensor(cb[:, g, way, :, :], psum[:, 1 + 2 * g, :].rearrange("p (c l) -> p c l", c=SB),
                                           mask[:, :].unsqueeze(1).broadcast_to([P, SB, P]), ALU.mult)
                last.then_inc(s_["cb_kept"], 1)

            def diffs(t, u):
                for q in range(4):
                    dve.wait_ge(s_["spread"], 4 * t + (q + 1))
                    for c in range(SB):
                        part = slice(c * P, (c + 1) * P)
                        last = V.tensor_scalar(inner[:, u, q, part], psum[:, 1 + q, part],
                                               row(core.sums, t, c, q // 2, q % 2), 0.0, ALU.subtract, ALU.min)
                    last.then_inc(s_["diffs"], 1)

            diffs(0, 0)
            for t, u, g, more in tiles_of(dve):
                for q in range(4):
                    dve.wait_ge(s_["inner_exp"], 4 * t + (q + 1))
                    for c in range(SB):
                        part = slice(c * P, (c + 1) * P)
                        last = V.scalar_tensor_tensor(inner[:, u, q, part], inner[:, u, q, part],
                                                      row(core.dt, t, c, q // 2, q % 2), cb[:, g, q // 2, c, :],
                                                      ALU.mult, ALU.mult)
                    last.then_inc(s_["weighed"], 1)
                dve.wait_ge(s_["states"], t + 1)
                V.tensor_copy(prev[:, 0, 1, :], psum[:, 5, 0:P])
                V.tensor_copy(prev[:, 1, 2, :], psum[:, 6, 3 * P:4 * P]).then_inc(s_["prev_steps"], 1)
                dve.wait_ge(s_["weighed"], 4 * t + 4)
                for e in range(2):
                    V.tensor_tensor(inner[:, u, e, :], inner[:, u, e, :], inner[:, u, 2 + e, :], ALU.add)\
                        .then_inc(s_["inner_made"], 1)
                for step in range(2):
                    dve.wait_ge(s_["prev_steps"], 2 * t + (step + 1))
                    for way, at, to in ((0, 1 + step, 2 + step), (1, 2 - step, 1 - step)):
                        for e in range(2):
                            rows = slice(64 * e, 64 * e + 64)
                            last = V.scalar_tensor_tensor(
                                prev[:, way, to, rows], prev[:, way, at, rows], row(core.chunk_decay, t, at, way, e),
                                psum[:, 5 + way, at * P + 64 * e:at * P + 64 * e + 64], ALU.mult, ALU.add)
                    last.then_inc(s_["prev_steps"] if step == 0 else s_["prev_made"], 1)
                dve.wait_ge(s_["prev_made"], t + 1)
                V.memset(core.scrap[:, 1:2], 0.0).then_inc(s_["states_read"], 1)
                if more:
                    diffs(t + 1, 1 - u)
                dve.wait_ge(s_["y_made"], t + 1)
                V.scalar_tensor_tensor(y[:, :], x_t[:, u, :], core.d_skip[:, one(t)], psum[:, 7, :],
                                       ALU.mult, ALU.add).then_inc(s_["y_read"], 1)
                dve.wait_ge(s_["y_read"], t + 2)
                z = core.z[:, one(t), :]
                V.tensor_tensor(z, y[:, :].unsqueeze(1), z, ALU.mult).then_inc(s_["y_kept"], 1)



SEEN = [(0, 1), (0, 1, 2), (1, 2, 3), (2, 3)]


def window_attention(core):
    core.next_phase()
    nc, psum, mm = core.nc, core.psum, core.nc.tensor.matmul
    with ExitStack() as scope, nc.Block() as block:
        sb = lambda name, shape, dt=F32: scope.enter_context(nc.sbuf_tensor(name, shape, dt))
        q, k_, v = sb("wa_q", [P, 2, S]), sb("wa_k", [P, S]), sb("wa_v", [P, SB, 64])
        prob, prob_t = sb("wa_prob", [P, 2, SB, WIDE]), sb("wa_prob_t", [P, 2, 10, P])
        top, total, rest = sb("wa_top", [P, 2, SB]), sb("wa_total", [P, 2, SB]), sb("wa_rest", [P, 2, SB])
        names = ("q_staged", "v_staged", "scored", "scores_kept", "maxima", "floored", "top_made", "exps", "rest_made", "sums",
                 "inverse", "scaled", "turned", "turned_kept", "out_made", "out_kept", "cleared")
        s_ = {n: core.sem("wa_" + n) for n in names}
        half = (slice(0, 64), slice(64, 128))

        def columns(n):
            lo = (SEEN[n][0] - n + 1) * P
            return lo, lo + len(SEEN[n]) * P

        kv_heads = 4

        def turns(engine):
            with engine.Fori(0, kv_heads - 1) as i:
                yield i, True
            yield kv_heads - 1, False

        @block.tensor
        def _(pe):
            def scores(i, r):
                e = r % 2
                if r >= 2:
                    pe.wait_ge(s_["out_kept"], 4 * i + (r - 1))
                for n in range(SB):
                    lo, hi = columns(n)
                    last = mm(psum[:, 4 * e + n, 0:hi - lo], q[half[e], r % 4 // 2, n * P:(n + 1) * P],
                              k_[half[e], SEEN[n][0] * P:(SEEN[n][-1] + 1) * P], start=True, stop=True)
                last.then_inc(s_["scored"], 1)

            pe.wait_ge(s_["q_staged"], 1)
            scores(0, 0)
            scores(0, 1)
            for i, more in turns(pe):
                for r in range(4):
                    e = r % 2
                    pe.wait_ge(s_["scaled"], 4 * i + (r + 1))
                    for n in range(SB):
                        for m in range(len(SEEN[n])):
                            at = columns(n)[0] + m * P
                            last = nc.tensor.transpose(psum[:, 4 * e + n, m * P:(m + 1) * P],
                                                       prob[:, e, n, at:at + P], core.ident[:, :])
                    last.then_inc(s_["turned"], 1)
                    pe.wait_ge(s_["turned_kept"], 4 * i + (r + 1))
                    if r == 0:
                        pe.wait_ge(s_["v_staged"], i + 1)
                    at = 0
                    for n in range(SB):
                        for m, kb in enumerate(SEEN[n]):
                            last = mm(psum[half[e], 4 * e, n * P:(n + 1) * P], v[:, kb, :], prob_t[:, e, at, :],
                                      start=m == 0, stop=m == len(SEEN[n]) - 1)
                            at += 1
                    last.then_inc(s_["out_made"], 1)
                    if r + 2 < 4 or more:
                        if r == 2:
                            pe.wait_ge(s_["q_staged"], i + 2)
                        scores(i, r + 2)

        @block.scalar
        def _(act):
            A = nc.scalar.activation
            nc.scalar.preload_act_table(ACT.Exp)

            def stage_q(i):
                A(q[ALL], core.q2[:, ds(2 * i, 2), :], ACT.Copy)
                A(k_[:, :].unsqueeze(1), core.k2[:, one(i), :], ACT.Copy).then_inc(s_["q_staged"], 1)

            def stage_v(i):
                A(v[ALL], core.v2[:, :, ds(64 * i, 64)], ACT.Copy).then_inc(s_["v_staged"], 1)

            def exps(i, r):
                e = r % 2
                act.wait_ge(s_["top_made"], 4 * i + (r + 1))
                for n in range(SB):
                    lo, hi = columns(n)
                    A(prob[:, e, n, lo:hi], prob[:, e, n, lo:hi], ACT.Exp, bias=top[:, e, n:n + 1],
                      accum_out=total[:, e, n:n + 1])
                A(rest[:, e, :], rest[:, e, :], ACT.Exp).then_inc(s_["exps"], 1)

            def keep_turned(i, r):
                e = r % 2
                act.wait_ge(s_["turned"], 4 * i + (r + 1))
                A(prob_t[:, e, 0:2, :].rearrange("p a c -> p (a c)"), psum[:, 4 * e, 0:2 * P], ACT.Copy)
                A(prob_t[:, e, 2:8, :].rearrange("p (n a) c -> p n (a c)", n=2), psum[:, 4 * e + 1:4 * e + 3, 0:3 * P],
                  ACT.Copy)
                A(prob_t[:, e, 8:10, :].rearrange("p a c -> p (a c)"), psum[:, 4 * e + 3, 0:2 * P], ACT.Copy)\
                    .then_inc(s_["turned_kept"], 1)

            def keep_out(i, r):
                e = r % 2
                wait_alone(act, s_["out_made"], 4 * i + (r + 1))
                A(core.q2[half[e], ds(2 * i + r // 2, 1), :], psum[half[e], one(4 * e), :], ACT.Copy)\
                    .then_inc(s_["out_kept"], 1)

            stage_q(0)
            stage_v(0)
            exps(0, 0)
            for i, more in turns(act):
                for r in range(4):
                    keep_turned(i, r)
                    if r + 1 < 4 or more:
                        exps(i, r + 1)
                    keep_out(i, r)
                    if r == 2 and more:
                        stage_q(i + 1)
                if more:
                    stage_v(i + 1)

        @block.vector
        def _(dve):
            V = nc.vector
            for e in range(2):
                V.memset(prob[:, e, 0, 0:P], -1e30)
                last = V.memset(prob[:, e, 3, 2 * P:WIDE], -1e30)
            last.then_inc(s_["cleared"], 1)
            dve.wait_ge(s_["cleared"], 1)

            def maxima(i, r):
                e = r % 2
                dve.wait_ge(s_["scored"], 4 * i + (r + 1))
                for n in range(SB):
                    lo, hi = columns(n)
                    last = V.scalar_tensor_tensor(prob[:, e, n, lo:hi], core.distance[:, lo:hi],
                                                  core.slopes[:, ds(4 * i + r, 1)], psum[:, 4 * e + n, 0:hi - lo],
                                                  ALU.mult, ALU.add)
                last.then_inc(s_["scores_kept"], 1)
                dve.wait_ge(s_["scores_kept"], 4 * i + (r + 1))
                V.tensor_reduce(top[:, e, :], prob[:, e, :, :], AX.X, ALU.max).then_inc(s_["maxima"], 1)
                dve.wait_ge(s_["maxima"], 4 * i + (r + 1))
                sink = core.sink[:, ds(4 * i + r, 1)]
                V.tensor_scalar(top[:, e, :], top[:, e, :], sink, -1.0, ALU.max, ALU.mult).then_inc(s_["floored"], 1)
                dve.wait_ge(s_["floored"], 4 * i + (r + 1))
                V.tensor_scalar(rest[:, e, :], top[:, e, :], sink, None, ALU.add).then_inc(s_["top_made"], 1)

            def scale(i, r):
                e = r % 2
                dve.wait_ge(s_["exps"], 4 * i + (r + 1))
                V.tensor_tensor(total[:, e, :], total[:, e, :], rest[:, e, :], ALU.add).then_inc(s_["sums"], 1)
                dve.wait_ge(s_["sums"], 4 * i + (r + 1))
                V.reciprocal(total[:, e, :], total[:, e, :]).then_inc(s_["inverse"], 1)
                dve.wait_ge(s_["inverse"], 4 * i + (r + 1))
                for n in range(SB):
                    lo, hi = columns(n)
                    last = V.tensor_scalar(prob[:, e, n, lo:hi], prob[:, e, n, lo:hi], total[:, e, n:n + 1], None,
                                           ALU.mult)
                last.then_inc(s_["scaled"], 1)

            maxima(0, 0)
            for i, more in turns(dve):
                for r in range(4):
                    scale(i, r)
                    if r + 1 < 4 or more:
                        maxima(i, r + 1)



def project_out(core):
    core.next_phase()
    nc = core.nc
    with ExitStack() as scope, nc.Block() as block:
        sb = lambda name, shape, dt=F32: scope.enter_context(nc.sbuf_tensor(name, shape, dt))
        work, rstd = sb("po_work", [P, KD, S]), sb("po_rstd", [P, S])
        y = [sb("po_y_hi", [P, 2 * KD, S], F32R), sb("po_y_lo", [P, 2 * KD, S], F32R)]
        mix = core.q2
        st = core.st["out2"]
        hi_made, split, added = core.sem("po_hi_made"), core.sem("po_split"), core.sem("po_added")
        ssm = Norm(core, core.z, work, rstd, "ssm_norm_2", y[0][:, 0:KD, :], y[1][:, 0:KD, :])
        post = Norm(core, mix, work, rstd, "norm_mix_post_2")

        @block.sync
        def _(sp):
            load_stage(core, sp, st)

        @block.tensor
        def _(pe):
            ssm.pe(pe)
            pe.wait_ge(split, 1)
            pe_tiles(core, pe, st, y, tiles=1, k_tiles=2 * KD, norm=ssm, order=[*range(KD, 2 * KD), *range(KD)])
            post.pe(pe)

        @block.scalar
        def _(act):
            ssm.act_squares(act)
            nc.scalar.activation(y[0][:, KD:, :], core.q2[ALL], ACT.Copy).then_inc(hi_made, 1)
            ssm.act_rest(act)
            act.wait_ge(core.signals["dve_evac"].sem, core.signals["dve_evac"].taken + KD)
            post.act(act)

        @block.vector
        def _(dve):
            dve.wait_ge(hi_made, 1)
            nc.vector.tensor_tensor(y[1][:, KD:, :], core.q2[ALL], y[0][:, KD:, :].bitcast(F32), ALU.subtract)\
                .then_inc(split, 1)
            ssm.dve(dve)
            keep_split(core, dve, st, mix)
            post.dve(dve)
            dve.wait_ge(core.signals["normed"].sem, post.normed + KD)
            nc.vector.tensor_tensor(core.h[ALL], core.h[ALL], work[ALL], ALU.add).then_inc(added, 1)


def keep_split(core, dve, st, out):
    signal = core.signals["dve_evac"]
    signal.take(st.steps)
    for s, u, c in turns_of(dve, st):
        core.split_chunk(dve, c.next())
        dve.wait_ge(core.chunk_done, c.number + 1)
        core.nc.vector.tensor_copy(out[:, one(s), :], core.psum[:, one(2 * u), :]).then_inc(signal.sem, 1)


def mlp(core):
    core.next_phase()
    nc, psum = core.nc, core.psum
    with ExitStack() as scope, nc.Block() as block:
        sb = lambda name, shape, dt=F32: scope.enter_context(nc.sbuf_tensor(name, shape, dt))
        work, rstd, acc = sb("ml_work", [P, KD, S]), sb("ml_rstd", [P, S]), sb("ml_acc", [P, KD, S])
        x = [sb("ml_x_hi", [P, KD, S], F32R), sb("ml_x_lo", [P, KD, S], F32R)]
        hid = [sb("ml_hid_hi", [P, HM, S], F32R), sb("ml_hid_lo", [P, HM, S], F32R)]
        names = ("relu", "hi_made", "split", "added", "out_turned", "out_kept", "out_stored")
        s_ = {n: core.sem("ml_" + n) for n in names}
        norm = Norm(core, core.h, work, rstd, "norm_mlp_pre_2", *x)
        post = Norm(core, acc, work, rstd, "norm_mlp_post_2")
        relu = work
        evac, asig, done = core.signals["dve_evac"], core.signals["act_evac"], core.chunk_done
        steps = HM // 2
        rows_out = acc[:, :, :].rearrange("p (b k) s -> p b (k s)", b=SB)

        @block.sync
        def _(sp):
            for h in range(2):
                load_stage(core, sp, core.st[f"mlp_up{h}"])
                load_stage(core, sp, core.st[f"mlp_down{h}"])
            for b in range(SB):
                sp.wait_ge(s_["out_kept"], 2 * b + 2)
                sp.dma_start(core.out[0, b * P:(b + 1) * P, :], rows_out[:, b, :]).then_inc(s_["out_stored"], 16)
            sp.wait_ge(s_["out_stored"], 16 * SB)

        @block.tensor
        def _(pe):
            norm.pe(pe)
            before = evac.taken
            for h in range(2):
                pe_tiles(core, pe, core.st[f"mlp_up{h}"], x, norm=norm)
                evac.taken += steps
                pe_tiles(core, pe, core.st[f"mlp_down{h}"], hid, tiles=1, k_tiles=HM,
                         late=(s_["split"], steps * (h + 1), 2))
                evac.taken += KD
            evac.taken = before
            post.pe(pe)
            pe.wait_ge(s_["added"], 1)
            for b in range(SB):
                for a in range(2):
                    for k in range(4):
                        last = nc.tensor.transpose(psum[:, 2 * b + a, k * P:(k + 1) * P],
                                                   core.h[:, 4 * a + k, b * P:(b + 1) * P], core.ident[:, :])
                    last.then_inc(s_["out_turned"], 1)

        @block.scalar
        def _(act):
            norm.act(act)
            at = evac.taken
            for h in range(2):
                st = core.st[f"mlp_up{h}"]
                for s, u, c in turns_of(act, st):
                    act.wait_ge(done, c.number + 1)
                    nc.scalar.activation(relu[:, 2 * u:2 * u + 2, :], psum[:, 2 * u:2 * u + 2, :], ACT.Relu)\
                        .then_inc(s_["relu"], 1)
                    act.wait_ge(evac.sem, s + (at + 1))
                    nc.scalar.activation(hid[0][:, ds(2 * s, 2), :], relu[:, 2 * u:2 * u + 2, :], ACT.Copy)\
                        .then_inc(s_["hi_made"], 1)
                at += steps + KD
            act.wait_ge(evac.sem, at)
            post.act(act)

        @block.vector
        def _(dve):
            V = nc.vector
            norm.dve(dve)
            for h in range(2):
                st = core.st[f"mlp_up{h}"]
                evac.take(steps)
                for s, u, c in turns_of(dve, st):
                    core.split_chunk(dve, c.next())
                    dve.wait_ge(s_["relu"], s + (1 + steps * h))
                    part = relu[:, 2 * u:2 * u + 2, :]
                    V.scalar_tensor_tensor(part, psum[:, 2 * u:2 * u + 2, :], 0.0, part, ALU.max, ALU.mult)\
                        .then_inc(evac.sem, 1)
                    dve.wait_ge(s_["hi_made"], s + (1 + steps * h))
                    V.tensor_tensor(hid[1][:, ds(2 * s, 2), :], part, hid[0][:, ds(2 * s, 2), :].bitcast(F32),
                                    ALU.subtract).then_inc(s_["split"], 1)
                down = core.st[f"mlp_down{h}"]
                if h == 0:
                    keep_split(core, dve, down, acc)
                else:
                    evac.take(KD)
                    for s, u, c in turns_of(dve, down, peeled=1):
                        if c.per or c.number + 1 < core.chunks:
                            core.split_chunk(dve, c.next())
                        dve.wait_ge(done, c.number + 1)
                        V.tensor_tensor(acc[:, one(s), :], acc[:, one(s), :], psum[:, one(2 * u), :], ALU.add)\
                            .then_inc(evac.sem, 1)
            post.dve(dve)
            dve.wait_ge(core.signals["normed"].sem, post.normed + KD)
            V.tensor_tensor(core.h[ALL], core.h[ALL], work[ALL], ALU.add).then_inc(s_["added"], 1)
            for b in range(SB):
                for a in range(2):
                    dve.wait_ge(s_["out_turned"], 2 * b + a + 1)
                    V.tensor_copy(rows_out[:, b, a * S:(a + 1) * S], psum[:, 2 * b + a, :])\
                        .then_inc(s_["out_kept"], 1)


def second_block(core):
    nc = core.nc
    with ExitStack() as outer:
        keep = lambda name, shape, dt=F32: outer.enter_context(nc.sbuf_tensor(name, shape, dt))
        core.q2, core.z = keep("q2", [P, KD, S]), keep("z2", [P, KD, S])
        with ExitStack() as inner:
            keep = lambda name, shape, dt=F32: inner.enter_context(nc.sbuf_tensor(name, shape, dt))
            core.k2, core.v2 = keep("k2", [P, 4, S]), keep("v2", [P, SB, 256])
            core.xbc, core.dt_t = keep("xbc", [P, 12, S]), keep("dt_t", [R2, S])
            core.distance, core.offsets = keep("distance", [P, WIDE]), keep("offsets", [P, WIDE], I32)
            core.dt_bias, core.a_log = keep("dt_bias", [P, R2]), keep("a_log", [P, R2])
            core.sink, core.slopes, core.d_skip = keep("sink", [P, HEADS2]), keep("slopes", [P, HEADS2]), keep("d_skip", [P, KD])
            input_projections(core)
            core.dt, core.sums = keep("dt", [P, SB, R2]), keep("sums", [P, SB, R2])
            core.state_weight, core.chunk_decay = keep("state_weight", [P, SB, R2]), keep("chunk_decay", [P, SB, R2])
            core.sums_t = keep("sums_t_hi", [R2, S], F32R), keep("sums_t_lo", [R2, S], F32R)
            ssd_prepare(core)
            ssd(core)
            window_attention(core)
        project_out(core)
    mlp(core)


def program(nc, inputs, out):
    with ExitStack() as stack:
        core = Core(nc, inputs, out, stack)
        core.st = weight_stages(core)
        core.h = stack.enter_context(nc.sbuf_tensor("h", [P, KD, S], F32))
        mixer(core)
        first_block_rest(core, stack)
        second_block(core)


def mixer(core):
    nc = core.nc
    with ExitStack() as scope:
        r_names = ("rw_r", "rw_k", "rw_v", "rw_decay", "rw_a", "rw_g")
        core.rw_all = scope.enter_context(nc.sbuf_tensor("rw_all", [P, len(r_names) * KW, S], F32))
        core.rw = {name: core.rw_all[:, n * KW:(n + 1) * KW, :] for n, name in enumerate(r_names)}
        core.level_masks = scope.enter_context(nc.sbuf_tensor("level_masks", [P, 2, LEVELS, P], F32))
        with ExitStack() as inner:
            core.x_hi = inner.enter_context(nc.sbuf_tensor("x_hi", [P, KD, S], F32R))
            core.x_lo = inner.enter_context(nc.sbuf_tensor("x_lo", [P, KD, S], F32R))
            with ExitStack() as branches:
                start(core)
                split_pair = lambda name: [branches.enter_context(nc.sbuf_tensor(f"{name}_{part}", [P, KW, S], F32R))
                                           for part in ("hi", "lo")]
                core.y_conv = split_pair("y_conv")
                conv_branch(core)
                core.y_sb = split_pair("y_sb")
                stick_breaking(core)
                gate_two_branches(core)
            rwkv_projections(core)
        with ExitStack() as inner:
            keep = lambda name, shape: inner.enter_context(nc.sbuf_tensor(name, shape, F32))
            core.kk, core.e_plus, core.e_minus, core.bonus = (keep("rw_" + name, [P, KW, S])
                                                              for name in ("kk", "e_plus", "e_minus", "bonus"))
            core.middle, core.growth = keep("rw_middle", [P, KW, SB]), keep("rw_growth", [P, KW, SB])
            core.k_a_less_1 = keep("rw_k_a_less_1", [P, KW])
            core.o_t = core.kk
            rwkv_prepare(core)
            rwkv_recurrence(core)
            rwkv_finish(core)
        third_branch_and_mix(core)


def first_block_rest(core, scope):
    nc = core.nc
    def split_tiles(inner, name):
        core.m_hi = inner.enter_context(nc.sbuf_tensor(name + "_hi", [P, KD, S], F32R))
        core.m_lo = inner.enter_context(nc.sbuf_tensor(name + "_lo", [P, KD, S], F32R))

    with ExitStack() as attention:
        keep = lambda name, shape: attention.enter_context(nc.sbuf_tensor(name, shape, F32))
        core.ca_q, core.ca_k, core.ca_v = keep("ca_q", [P, KD, S]), keep("ca_k", [P, KD, MEM]), keep("ca_v", [P, 2, D])
        memory_projections(core)
        split_tiles(attention, "attended")
        memory_attention(core)
        memory_out(core)
    ffn(core)


_INS = ["x", "mem", "w_comb", "w_lora", "a_lora", "g_lora", "branch_proj", "w_mix_out", "ca_wq", "ca_wkv", "ca_wo",
        "ffn_up", "ffn_down", "w_in_2", "dt_bias_2", "a_log_2", "d_skip_2", "attn_sink_2", "w_out_2", "w_up_2",
        "w_down_2"] + [name for name, _ in PARAM_ROWS]


def kernel(**inputs):
    import numpy as np
    from concourse import bacc
    from concourse.bass_utils import run_bass_kernel_spmd

    nc = bacc.Bacc("TRN2", target_bir_lowering=False, num_devices=1)
    arrays, aps = {}, {}
    for name in _INS:
        arrays[f"in_{name}"] = np.ascontiguousarray(inputs[name])
        aps[name] = nc.dram_tensor(f"in_{name}", arrays[f"in_{name}"].shape, F32, kind="ExternalInput").ap()
    out = nc.dram_tensor("out", (1, S, D), F32, kind="ExternalOutput").ap()
    program(nc, aps, out)
    result = run_bass_kernel_spmd(nc, [arrays], core_ids=[0])
    return result.results[0]["out"]
```
